# Optimizing a Trainium2 kernel written in Bass

```python
import math
import jax, jax.numpy as jnp
from jax import lax
import numpy as np

D_MODEL = 2048
BATCH = 1
SEQ = 256
DEPTH = 2

CHUNK = 64
PLE_DIM = 256
N_MIXERS = 2
SB_HEADS = 16
SB_HEAD_DIM = D_MODEL // SB_HEADS
SB_WIDTH = SB_HEADS * SB_HEAD_DIM
SB_QBLOCK = 128
SSM_EXPAND = 2
SSM_INNER = SSM_EXPAND * D_MODEL
SSM_HEAD_DIM = 64
SSM_HEADS = SSM_INNER // SSM_HEAD_DIM
SSM_GROUPS = 8
SSM_HEADS_PER_GROUP = SSM_HEADS // SSM_GROUPS
SSM_STATE = 128
SSM_CONV = 4
SSM_CONV_DIM = SSM_INNER + 2 * SSM_GROUPS * SSM_STATE
SSM_IN_PROJ = 2 * SSM_INNER + 2 * SSM_GROUPS * SSM_STATE + SSM_HEADS
D_FF = 4 * D_MODEL
NORM_EPS = 1e-6

kernel_name = 'hybrid_stickbreak_ssd_trunk'

def rms_norm(x, g):
    xf = x.astype(jnp.float32)
    y = xf * lax.rsqrt(jnp.mean(xf * xf, axis=-1, keepdims=True) + NORM_EPS)
    return (y * g.astype(jnp.float32)).astype(x.dtype)

def stick_breaking_attention(q, k, v):
    L = q.shape[2]
    scale = SB_HEAD_DIM ** -0.5
    outs = []
    for blk in range(L // SB_QBLOCK):
        t0 = blk * SB_QBLOCK
        t1 = t0 + SB_QBLOCK
        qb = q[:, :, t0:t1]
        kb = k[:, :, :t1]
        vb = v[:, :, :t1]
        z = jnp.einsum('bhtd,bhsd->bhts', qb, kb).astype(jnp.float32) * scale
        t_idx = t0 + jnp.arange(SB_QBLOCK)[:, None]
        s_idx = jnp.arange(t1)[None, :]
        mask = s_idx < t_idx
        log_beta = jax.nn.log_sigmoid(z)
        log_1m_beta = jnp.where(mask, -jax.nn.softplus(z), 0.0)
        suffix = lax.cumsum(log_1m_beta, axis=3, reverse=True) - log_1m_beta
        a = jnp.where(mask, jnp.exp(log_beta + suffix), 0.0)
        outs.append(jnp.einsum('bhts,bhsd->bhtd', a.astype(vb.dtype), vb))
    return jnp.concatenate(outs, axis=2)

def stick_breaking_mixer(hn, w_qkv, g_q, g_k, w_o):
    b, l, _ = hn.shape
    qkv = (hn @ w_qkv).reshape(b, l, 3, SB_HEADS, SB_HEAD_DIM)
    q = rms_norm(qkv[:, :, 0], g_q).transpose(0, 2, 1, 3)
    k = rms_norm(qkv[:, :, 1], g_k).transpose(0, 2, 1, 3)
    v = qkv[:, :, 2].transpose(0, 2, 1, 3)
    o = stick_breaking_attention(q, k, v)
    o = o.transpose(0, 2, 1, 3).reshape(b, l, SB_WIDTH)
    return o @ w_o

def causal_dwconv(x, w, bias):
    k = w.shape[0]
    y = lax.conv_general_dilated(x, w[:, None, :].astype(x.dtype), window_strides=(1,),
                                 padding=[(k - 1, 0)], dimension_numbers=('NWC', 'WIO', 'NWC'),
                                 feature_group_count=x.shape[-1])
    return y + bias.astype(x.dtype)

def ssd_chunked(x, dt, a, bm, cm):
    b, l, g, hg, pd = x.shape
    n = bm.shape[-1]
    c = l // CHUNK
    x = x.reshape(b, c, CHUNK, g, hg, pd)
    dt = dt.reshape(b, c, CHUNK, g, hg)
    bm = bm.reshape(b, c, CHUNK, g, n)
    cm = cm.reshape(b, c, CHUNK, g, n)
    acum = jnp.cumsum(dt * a, axis=2)
    diff = acum[:, :, :, None] - acum[:, :, None, :]
    causal = jnp.tril(jnp.ones((CHUNK, CHUNK), dtype=bool))[:, :, None, None]
    lmat = jnp.exp(jnp.where(causal, diff, -jnp.inf))
    cb = jnp.einsum('bcign,bcjgn->bcijg', cm, bm)
    y_diag = jnp.einsum('bcijg,bcijgh,bcjgh,bcjghp->bcighp', cb, lmat, dt, x)
    decay_states = jnp.exp(acum[:, :, -1:] - acum)
    states = jnp.einsum('bcjgn,bcjgh,bcjghp->bcghpn', bm, decay_states * dt, x)
    chunk_decay = jnp.exp(acum[:, :, -1])

    def step(carry, inp):
        st, dec = inp
        return carry * dec[..., None, None] + st, carry

    init = jnp.zeros((b, g, hg, pd, n), jnp.float32)
    _, h_in = lax.scan(step, init, (jnp.moveaxis(states, 1, 0).astype(jnp.float32),
                                    jnp.moveaxis(chunk_decay, 1, 0)))
    h_in = jnp.moveaxis(h_in, 0, 1)
    y_off = jnp.einsum('bcign,bcghpn,bcigh->bcighp', cm, h_in, jnp.exp(acum))
    return (y_diag + y_off).reshape(b, l, g, hg, pd)

def ssd_mixer(hn, w_in, conv_w, conv_b, dt_bias, a_log, d_skip, g_out, w_out):
    b, l, _ = hn.shape
    zxbcdt = hn @ w_in
    z = zxbcdt[..., :SSM_INNER]
    xbc = zxbcdt[..., SSM_INNER:SSM_INNER + SSM_CONV_DIM]
    dt_raw = zxbcdt[..., SSM_INNER + SSM_CONV_DIM:]
    xbc = jax.nn.silu(causal_dwconv(xbc, conv_w, conv_b))
    gn = SSM_GROUPS * SSM_STATE
    xs = xbc[..., :SSM_INNER].reshape(b, l, SSM_GROUPS, SSM_HEADS_PER_GROUP, SSM_HEAD_DIM)
    bm = xbc[..., SSM_INNER:SSM_INNER + gn].reshape(b, l, SSM_GROUPS, SSM_STATE)
    cm = xbc[..., SSM_INNER + gn:].reshape(b, l, SSM_GROUPS, SSM_STATE)
    dt = jax.nn.softplus(dt_raw.astype(jnp.float32) + dt_bias.astype(jnp.float32))
    dt = dt.reshape(b, l, SSM_GROUPS, SSM_HEADS_PER_GROUP)
    a = -jnp.exp(a_log.astype(jnp.float32)).reshape(SSM_GROUPS, SSM_HEADS_PER_GROUP)
    y = ssd_chunked(xs, dt, a, bm, cm)
    y = y + d_skip.astype(jnp.float32).reshape(SSM_GROUPS, SSM_HEADS_PER_GROUP, 1) * xs
    y = y.astype(hn.dtype).reshape(b, l, SSM_INNER) * jax.nn.silu(z)
    y = rms_norm(y.reshape(b, l, SSM_GROUPS, SSM_INNER // SSM_GROUPS),
                 g_out.reshape(SSM_GROUPS, SSM_INNER // SSM_GROUPS))
    return y.reshape(b, l, SSM_INNER) @ w_out

def squared_relu_mlp(hn, w_up, w_down):
    u = jax.nn.relu(hn @ w_up)
    return (u * u) @ w_down

def setup_inputs(seed: int = 0) -> dict:
    key = jax.random.key(seed)
    ks = jax.random.split(key, 24)
    na = (DEPTH + 1) // 2
    ns = DEPTH // 2
    res_scale = (2.0 * DEPTH) ** -0.5

    def dense(k, shape, fan_in, scale=1.0):
        return jax.random.normal(k, shape, jnp.float32) * (scale * fan_in ** -0.5)

    def gain(k, shape):
        return 1.0 + 0.05 * jax.random.normal(k, shape, jnp.float32)

    dt = jnp.exp(jax.random.uniform(ks[14], (ns, SSM_HEADS), jnp.float32)
                 * (math.log(0.1) - math.log(0.001)) + math.log(0.001))
    dt = jnp.maximum(dt, 1e-4)
    dt_bias = dt + jnp.log(-jnp.expm1(-dt))
    a_log = jnp.log(jax.random.uniform(ks[15], (ns, SSM_HEADS), jnp.float32, 1.0, 16.0))

    return {
        'x': jax.random.normal(ks[0], (BATCH, SEQ, D_MODEL), jnp.float32),
        'p': jax.random.normal(ks[1], (DEPTH, BATCH, SEQ, PLE_DIM), jnp.float32),
        'attn_norm': gain(ks[2], (na, D_MODEL)),
        'attn_w_qkv': dense(ks[3], (na, D_MODEL, 3 * SB_WIDTH), D_MODEL),
        'attn_q_norm': gain(ks[4], (na, SB_HEAD_DIM)),
        'attn_k_norm': gain(ks[5], (na, SB_HEAD_DIM)),
        'attn_w_o': dense(ks[6], (na, SB_WIDTH, D_MODEL), SB_WIDTH, res_scale),
        'ssm_norm': gain(ks[7], (ns, D_MODEL)),
        'ssm_w_in': dense(ks[8], (ns, D_MODEL, SSM_IN_PROJ), D_MODEL),
        'ssm_conv_w': dense(ks[9], (ns, SSM_CONV, SSM_CONV_DIM), SSM_CONV),
        'ssm_conv_b': 0.02 * jax.random.normal(ks[10], (ns, SSM_CONV_DIM), jnp.float32),
        'ssm_dt_bias': dt_bias,
        'ssm_a_log': a_log,
        'ssm_d': gain(ks[11], (ns, SSM_HEADS)),
        'ssm_out_norm': gain(ks[12], (ns, SSM_INNER)),
        'ssm_w_out': dense(ks[13], (ns, SSM_INNER, D_MODEL), SSM_INNER, res_scale),
        'mlp_norm': gain(ks[16], (DEPTH, D_MODEL)),
        'mlp_w_up': dense(ks[17], (DEPTH, D_MODEL, D_FF), D_MODEL),
        'mlp_w_down': dense(ks[18], (DEPTH, D_FF, D_MODEL), D_FF, res_scale),
        'ple_w_proj': dense(ks[19], (DEPTH, PLE_DIM, D_MODEL), PLE_DIM),
        'ple_norm': gain(ks[20], (DEPTH, D_MODEL)),
        'ple_gate_norm': gain(ks[21], (DEPTH, D_MODEL)),
        'ple_w_gate': dense(ks[22], (DEPTH, D_MODEL, D_MODEL), D_MODEL),
    }

def reference(x, p, attn_norm, attn_w_qkv, attn_q_norm, attn_k_norm, attn_w_o,
              ssm_norm, ssm_w_in, ssm_conv_w, ssm_conv_b, ssm_dt_bias, ssm_a_log, ssm_d,
              ssm_out_norm, ssm_w_out, mlp_norm, mlp_w_up, mlp_w_down,
              ple_w_proj, ple_norm, ple_gate_norm, ple_w_gate):
    h = x
    for i in range(DEPTH):
        j = i // N_MIXERS
        if i % N_MIXERS == 0:
            h = h + stick_breaking_mixer(rms_norm(h, attn_norm[j]), attn_w_qkv[j],
                                         attn_q_norm[j], attn_k_norm[j], attn_w_o[j])
        else:
            h = h + ssd_mixer(rms_norm(h, ssm_norm[j]), ssm_w_in[j], ssm_conv_w[j], ssm_conv_b[j],
                              ssm_dt_bias[j], ssm_a_log[j], ssm_d[j], ssm_out_norm[j], ssm_w_out[j])
        h = h + squared_relu_mlp(rms_norm(h, mlp_norm[i]), mlp_w_up[i], mlp_w_down[i])
        e = rms_norm(p[i] @ ple_w_proj[i], ple_norm[i])
        gate = jax.nn.sigmoid(rms_norm(h, ple_gate_norm[i]) @ ple_w_gate[i])
        h = h + gate * e
    return h


_drawn_inputs = setup_inputs


def setup_inputs(seed=0):
    import zlib

    import numpy as np

    out = dict(_drawn_inputs(seed))
    spreads = {}
    factors = {'attn_norm': 2.987,
     'attn_q_norm': 7.678,
     'attn_k_norm': 6.68,
     'ssm_conv_b': 6.135,
     'ssm_d': 4.847,
     'ssm_out_norm': 3.346,
     'ple_gate_norm': 14.128}
    for name, (base, spread) in spreads.items():
        noise = np.random.default_rng([zlib.crc32(name.encode()), seed]).standard_normal(out[name].shape)
        drawn = base * np.exp(spread * noise) if base else spread * noise
        out[name] = __import__('jax').numpy.asarray(drawn.astype(out[name].dtype))
    for name, factor in factors.items():
        out[name] = (out[name] * factor).astype(out[name].dtype)
    return out
```

```python
from contextlib import ExitStack, contextmanager

import concourse.bass as bass
from concourse import mybir

F32 = mybir.dt.float32
F32R = mybir.dt.float32r
ALU = mybir.AluOpType
ACT = mybir.ActivationFunctionType

P = 128
D = 2048
T = 256
KT = D // P
TB = T // P
EPS = 1e-6
HEADS, HD = 16, 128
FF = 4 * D
PLE = 256
GC = 512
TG = GC // P
HS_PER_GROUP = KT // 2
RAW, CUT = 8, 4
AHEAD = CUT
INNER = 4096
SH, SHD, SG, SN = 64, 64, 8, 128
CONV_TILES = (INNER + 2 * SG * SN) // P
KC = 4


class Steps:

    def __init__(self, eng, sem):
        self.eng, self.sem, self.base, self.k = eng, sem, 0, 0

    def inc(self, ins):
        ins.then_inc(self.sem, 1)
        self.k += 1

    def settle(self):
        self.eng.wait_ge(self.sem, self.base + self.k)

    @contextmanager
    def loop(self, start, end, per):
        base, k = self.base, self.k
        with self.eng.Fori(start, end) as i:
            self.base, self.k = base + k + (i - start) * per, 0
            yield i
            assert self.k == per, (self.k, per)
        self.base, self.k = base, k + (end - start) * per


class Stage:

    def __init__(self, slot, group, groups, per_group):
        self.slot, self.group, self.groups, self.per_group = slot, group, groups, per_group


def plan(layers):
    st, at = {}, [0, 0]

    def add(name, groups, per_group=HS_PER_GROUP):
        st[name] = Stage(at[0], at[1], groups, per_group)
        at[0] += groups * per_group
        at[1] += groups

    for l in range(layers):
        if l == 0:
            add("qk", 8)
            add("v", 4)
            add("wo", 4)
        else:
            add("bc0", 1)
            add("dt", 1, 1)
            add("bc", 3)
            for half in range(2):
                add(f"xz{half}", SG)
                add(f"out{half}", 4)
        add(f"mlp{l}", 32)
        add(f"ple{l}", 4, 1)
        add(f"gate{l}", 4)
    return st, at[0]


def build_trunk(nc, layers, x, p, attn_norm, attn_w_qkv, attn_q_norm, attn_k_norm, attn_w_o,
                ssm_norm, ssm_w_in, ssm_conv_w, ssm_conv_b, ssm_dt_bias, ssm_a_log, ssm_d,
                ssm_out_norm, ssm_w_out, mlp_norm, mlp_w_up, mlp_w_down,
                ple_w_proj, ple_norm, ple_gate_norm, ple_w_gate, out, decay_rows):
    st, n_slots = plan(layers)
    with ExitStack() as ctx:
        def sb(name, shape, dt=F32):
            return ctx.enter_context(nc.sbuf_tensor(name, shape, dt))

        sems = {}

        def sem(name):
            if name not in sems:
                sems[name] = ctx.enter_context(nc.semaphore(name))
            return sems[name]

        raw = [sb(f"raw{i}", [P, 2, GC]) for i in range(RAW)]
        w_hi = [sb(f"w_hi{i}", [P, 2, GC], F32R) for i in range(CUT)]
        w_lo = [sb(f"w_lo{i}", [P, 2, GC], F32R) for i in range(CUT)]
        h = sb("h", [P, KT, T])
        xa = sb("xa", [P, KT, 2, T], F32R)
        ident = sb("ident", [P, P])
        ones = sb("ones", [P, P])
        later = sb("later", [P, P])
        earlier = sb("earlier", [P, P])
        upto = sb("upto", [P, P])
        eps = sb("eps", [P, 1])
        never = sb("never", [P, P])
        N_GAIN, N_CONV, N_CB = 8 * KT, KC * CONV_TILES, CONV_TILES
        gains = sb("gains", [P, N_GAIN])
        conv_w = sb("conv_w", [P, N_CONV])
        misc = sb("misc", [P, N_CB + 2 + INNER // P])
        G_ATTN, G_SSM, G_MLP, G_PLE, G_GATE = 0, KT, 2 * KT, 4 * KT, 6 * KT
        Q_COL, K_COL, OUT_COL = N_CB, N_CB + 1, N_CB + 2
        qscale = sb("qscale", [P, 1])
        rstd = sb("rstd", [P, T])
        rstd_tok = sb("rstd_tok", [P, TB])
        rstd_e = sb("rstd_e", [P, T])
        sq4 = sb("sq4", [P, TG, T])
        acc4 = sb("acc4", [P, TG, T])

        with ExitStack() as c:
            c.enter_context(nc.sbuf_tensor("xb_first_half", [P, KT * T], F32))
            v_tok = c.enter_context(nc.sbuf_tensor("v_tok", [P, HEADS, TB, HD], F32))
        xb = sb("xb", [P, KT, 2, T], F32R)

        def phase(tensors):
            with ExitStack() as c:
                return [c.enter_context(nc.sbuf_tensor(n, s, dt)) for n, s, dt in tensors]

        x_tok, rows0, rows1, rows2, rows3 = phase(
            [("x_tok", [P, TB, D], F32)] + [(f"rows{i}", [P, P], F32) for i in range(4)])
        qk, qn, nrm = phase([("qk", [P, HEADS, 2, T], F32), ("qn", [P, TG, T], F32),
                             ("nrm", [P, TG, T], F32)])
        soft, logb, ell = phase([("qk_again", [P, HEADS, 2, T], F32), ("qn_again", [P, TG, T], F32),
                                    ("nrm_again", [P, TG, T], F32), ("soft", [P, 2, 384], F32),
                                    ("logb", [P, 2, 384], F32), ("ell", [P, 2, 384], F32)])[3:]
        e, rbuf, ubuf, p_tok, p_t, sig, acc_e = phase(
            [("e", [P, KT, T], F32), ("rbuf", [P, TG, T], F32), ("ubuf", [P, TG, T], F32),
             ("p_tok", [P, TB, PLE], F32), ("p_t", [P, 2, 2, T], F32R), ("sig", [P, TG, T], F32),
             ("acc_e", [P, TG, T], F32)])

        ssm_shapes = [("cb", [P, SG, 384], F32), ("xr", [P, TG, KC - 1 + T], F32), ("xc", [P, TG * T], F32),
                      ("x_skip", [P, TB * GC], F32), ("zg", [P, TB * GC], F32), ("dt", [P, TB, SH], F32),
                      ("dt_a", [P, TB, SH], F32), ("dt_ell", [P, TB, SH], F32), ("decay_t", [SH, T], F32),
                      ("offset", [P, 3, SH], F32), ("head_p", [P, 3, SH], F32), ("y_rms", [P, TB], F32)]
        cb, xr, xc, x_skip, zg, dt, dt_a, dt_ell, decay_t, offset, head_p, y_rms, rb, mix = phase(
            ssm_shapes + [("rb", [P, 4, T], F32), ("mix", [P, 2, 4, 384], F32)])
        bt, ct = phase([(n + "_again", *z) for n, *z in ssm_shapes] +
                       [("bt", [P, SG, T], F32), ("ct", [P, SG, T], F32)])[-2:]

        gp = [ctx.enter_context(nc.psum_tensor(f"group_pair{i}", [P, 2 * GC], F32)) for i in range(2)]
        aux = [ctx.enter_context(nc.psum_tensor(f"aux_pair{i}", [P, 2 * GC], F32)) for i in range(2)]

        landed = [sem(f"landed{i}") for i in range(RAW)]
        hi_made = sem("hi_made")
        lo_made = sem("lo_made")
        slot_used = sem("slot_used")
        group_read = sem("group_read")

        def gain(col, n=1):
            return gains[:, bass.ds(col, n)]

        norm_col = {"attn": G_ATTN, "ssm": G_SSM}
        for l in range(layers):
            norm_col[f"mlp{l}"] = G_MLP + KT * l
            norm_col[f"gate{l}"] = G_GATE + KT * l

        block = ctx.enter_context(nc.Block())

        @block.sync
        def _(sp):
            def load_x(c):
                sp.dma_start(x_tok[:, :, c * GC:(c + 1) * GC],
                             x[0, :, c * GC:(c + 1) * GC].rearrange("(b q) n -> q b n", q=P)).then_inc(
                                 sem(f"x_in{c}"), 16)
            load_x(0)
            rows = [
                (rows0, 0, attn_norm.rearrange("l (k p) -> (l k) p", p=P)),
                (rows0, G_SSM, ssm_norm.rearrange("l (k p) -> (l k) p", p=P)),
                (rows0, G_MLP, mlp_norm.rearrange("l (k p) -> (l k) p", p=P)),
                (rows0, G_PLE, ple_norm.rearrange("l (k p) -> (l k) p", p=P)),
                (rows0, G_GATE, ple_gate_norm.rearrange("l (k p) -> (l k) p", p=P)),
                (rows1, 0, ssm_conv_w[0].rearrange("c (k p) -> (c k) p", p=P)[0:P]),
                (rows2, 0, ssm_conv_w[0].rearrange("c (k p) -> (c k) p", p=P)[P:N_CONV]),
                (rows3, 0, ssm_conv_b.rearrange("l (k p) -> (l k) p", p=P)),
                (rows3, Q_COL, attn_q_norm),
                (rows3, K_COL, attn_k_norm),
                (rows3, OUT_COL, ssm_out_norm.rearrange("l (k p) -> (l k) p", p=P)),
            ]
            for dst, at, src in rows:
                sp.dma_start(dst[at:at + src.shape[0], :], src).then_inc(sem("rows_in"), 16)
            for c in range(1, 4):
                load_x(c)

            def load(slot, r, src, shape=None):
                dst = raw[slot % RAW][:] if shape is None else \
                    raw[slot % RAW][:].rearrange("p a b -> p (a b)").rearrange("p (k n) -> p k n", k=shape)
                if slot >= RAW or not isinstance(r, int):
                    sp.wait_ge(lo_made, slot - RAW + 1 + RAW * r)
                sp.dma_start(dst, src).then_inc(landed[slot % RAW], 16)

            def load_group(slot, r, w, k0, col):
                for j in range(HS_PER_GROUP):
                    load(slot + j, r, w[:, bass.ds(k0 + 2 * j, 2), bass.ds(col, GC)])

            def tiles(w):
                return w.rearrange("(k p) n -> p k n", p=P)

            def load_mlp(l):
                s = st[f"mlp{l}"].slot
                up, down = tiles(mlp_w_up[l]), tiles(mlp_w_down[l])
                with sp.Fori(0, 4) as f:
                    with sp.Fori(0, 4) as c:
                        load_group(s, f * 8 + c, up, 0, f * D + c * GC)
                    with sp.Fori(0, 4) as c:
                        load_group(s + 32, f * 8 + c, down, f * KT, c * GC)

            def load_ple(l):
                s = st[f"ple{l}"].slot
                for j in range(4):
                    load(s + j, 0, tiles(ple_w_proj[l])[:, :, j * GC:(j + 1) * GC])
                with sp.Fori(0, 4) as c:
                    load_group(st[f"gate{l}"].slot, c, tiles(ple_w_gate[l]), 0, c * GC)

            def load_simple(name, w, groups, col=0):
                with sp.Fori(0, groups) as c:
                    load_group(st[name].slot, c, w, 0, c * GC + col)

            wqkv = tiles(attn_w_qkv[0])
            s = st["qk"].slot
            load_group(s, 0, wqkv, 0, 0)
            load_group(s + 8, 0, wqkv, 0, D)
            with sp.Fori(1, 4) as c:
                load_group(s, c * 2, wqkv, 0, c * GC)
                load_group(s + 8, c * 2, wqkv, 0, c * GC + D)
            load_simple("v", wqkv, 4, 2 * D)
            load_simple("wo", tiles(attn_w_o[0]), 4)
            for l in range(layers):
                if l == 1:
                    w_in, w_out = tiles(ssm_w_in[0]), tiles(ssm_w_out[0])
                    load_group(st["bc0"].slot, 0, w_in, 0, 2 * INNER)
                    load(st["dt"].slot, 0, w_in[:, :, 2 * INNER + 2 * SG * SN:], shape=KT)
                    load_simple("bc", w_in, 3, 2 * INNER + GC)
                    for half in range(2):
                        with sp.Fori(1, 5) as i:
                            first, col = st[f"xz{half}"].slot - 2 * HS_PER_GROUP, half * D - GC
                            load_group(first, 2 * i, w_in, 0, INNER + col + i * GC)
                            load_group(first + HS_PER_GROUP, 2 * i, w_in, 0, col + i * GC)
                        with sp.Fori(0, 4) as c:
                            load_group(st[f"out{half}"].slot, c, w_out, half * KT, c * GC)
                sp.dma_start(p_tok[:], p[l, 0].rearrange("(b q) n -> q b n", q=P)).then_inc(
                    sem(f"p_in{l}"), 16)
                load_mlp(l)
                load_ple(l)
            for c in range(4):
                sp.wait_ge(sem("out_staged"), c + 1)
                sp.dma_start(out[0].rearrange("(b q) n -> q b n", q=P)[:, :, c * GC:(c + 1) * GC],
                             (rbuf if c % 2 == 0 else ubuf)[:].rearrange("p a b -> p (a b)")
                             .rearrange("p (b n) -> p b n", b=TB)).then_inc(sem(f"out_done{c % 2}"), 16)
            for i in range(2):
                sp.wait_ge(sem(f"out_done{i}"), 32)

        @block.gpsimd
        def _(pool):
            own = Steps(pool, sem("pool_step"))
            for m in (ident, later, earlier, never):
                own.inc(pool.memset(m[:], 0.0))
            for m in (ones, upto):
                own.inc(pool.memset(m[:], 1.0))
            own.inc(pool.memset(eps[:], EPS))
            own.settle()
            def mask(m, op, sign, fill):
                pool.affine_select(out=m[:], in_=m[:], compare_op=op, fill=fill, base=0,
                                   pattern=[[-sign, P]], channel_multiplier=sign).then_inc(sem("masks"), 1)
            mask(ident, ALU.not_equal, 1, 1.0)
            mask(later, ALU.is_ge, -1, 1.0)
            mask(earlier, ALU.is_ge, 1, 1.0)
            mask(never, ALU.is_ge, -1, -1e38)
            mask(upto, ALU.is_ge, -1, 0.0)

            def square_group(src, ready, value, acc, first):
                pool.wait_ge(ready, value)
                own.settle()
                if first:
                    own.inc(pool.tensor_tensor(acc[:], src, src, ALU.mult))
                    return
                own.inc(pool.tensor_tensor(sq4[:], src, src, ALU.mult))
                own.settle()
                own.inc(pool.tensor_tensor(acc[:], acc[:], sq4[:], ALU.add))

            def fold(name, acc):
                own.settle()
                own.inc(pool.tensor_tensor(acc[:, 0:2, :], acc[:, 0:2, :], acc[:, 2:4, :], ALU.add))
                own.settle()
                pool.tensor_tensor(acc[:, 0, :], acc[:, 0, :], acc[:, 1, :], ALU.add).then_inc(
                    sem(f"{name}_sum"), 1)

            def square_h(name, before=None, ready=None, at=0):
                if before:
                    pool.wait_ge(sem(f"{before}_mean"), 1)
                for c in range(4):
                    square_group(h[:, 4 * c:4 * c + 4, :], ready or sem(f"{name}_h"), at + c + 1, acc4, c == 0)
                fold(name, acc4)

            def decays():
                for i, a in enumerate((ssm_dt_bias, ssm_a_log, ssm_d)):
                    if i == 0:
                        pool.wait_ge(sem("ssm_h"), 4)
                    pool.dma_start(head_p[:, i, :], a.broadcast_to([P, SH])).then_inc(sem("heads_in"), 16)
                pool.wait_ge(sem("decay_t"), 1)
                pool.dma_start(decay_rows, decay_t[:]).then_inc(sem("rows_out"), 16)
                pool.wait_ge(sem("rows_out"), 16)
                pool.wait_ge(sem("cb"), SG)
                for half in range(2):
                    with own.loop(4 * half, 4 * half + 4, 6) as g:
                        for b in range(2):
                            own.settle()
                            pool.dma_start(rb[:], decay_rows[bass.ds(8 * g + 4 * b, 4), :].unsqueeze(0)
                                           .broadcast_to([P, 4, T])).then_inc(sem("rb_in"), 16)
                            pool.wait_ge(sem("rb_in"), 32 * g + 16 * b + 16)
                            if b == 0:
                                pool.wait_ge(sem("mix_free"), g + 1)
                            for dst, src, o in ((0, 0, 0), (1, 1, 2), (2, 1, 1)):
                                own.inc(pool.tensor_tensor(
                                    mix[:, b, :, dst * P:(dst + 1) * P], rb[:, :, src * P:(src + 1) * P],
                                    offset[:, o, bass.ds(8 * g + 4 * b, 4)].unsqueeze(2).broadcast_to([P, 4, P]),
                                    ALU.add))
                            own.settle()
                            diagonal = mix[:, b].rearrange("p h (c n) -> p h c n", c=3)[:, :, 0:3:2, :]
                            pool.tensor_tensor(diagonal, diagonal,
                                               never[:].unsqueeze(1).unsqueeze(1).broadcast_to([P, 4, 2, P]),
                                               ALU.add).then_inc(sem("exponents"), 1)

            square_h("attn")
            for hd in range(HEADS):
                pool.wait_ge(sem("weights_raw"), hd + 1)
                a = qk[:, hd].rearrange("p a b -> p (a b)")[:, 0:384].rearrange("p (c n) -> p c n", c=3)
                pool.tensor_tensor(a[:, 0:3:2, :], a[:, 0:3:2, :],
                                   earlier[:].unsqueeze(1).broadcast_to([P, 2, P]),
                                   ALU.mult).then_inc(sem("weights_masked"), 1)
            for l in range(layers):
                if l == 1:
                    square_h("ssm", before="gate0")
                    decays()
                m = st[f"mlp{l}"].group
                square_h(f"mlp{l}", "attn" if l == 0 else "ssm", group_read, m - 4)
                square_h(f"gate{l}", f"mlp{l}", group_read, m + 28)
                for c in range(4):
                    square_group(e[:, 4 * c:4 * c + 4, :], group_read, m + 32 + c + 1, acc_e, c == 0)
                fold(f"e{l}", acc_e)

        @block.scalar
        def _(act):
            own = Steps(act, sem("act_step"))

            def cut(slot, r=0):
                if slot >= n_slots:
                    return
                act.wait_ge(landed[slot % RAW], 16 * (slot // RAW + 1) + 16 * r)
                if slot >= CUT:
                    act.wait_ge(slot_used, slot - CUT + 1 + RAW * r)
                act.activation(w_hi[slot % CUT][:], raw[slot % RAW][:], ACT.Copy).then_inc(hi_made, 1)

            def cuts(slot, r=0, js=range(HS_PER_GROUP)):
                for j in js:
                    cut(slot + AHEAD + j, r)

            def x_hi(name, c, dst, ready, value):
                col = norm_col[name]
                act.wait_ge(ready, value)
                for n in range(TG):
                    k = 4 * c + n
                    ins = act.activation(dst[:, bass.ds(k, 1), 0, :], h[:, bass.ds(k, 1), :], ACT.Copy,
                                         scale=gain(col + k))
                ins.then_inc(sem(f"{name}_hi"), 1)

            def norm_root(name, tok=False):
                act.wait_ge(sem(f"{name}_mean"), 1)
                ins = act.activation(rstd[:], aux[1][:, 0:T], ACT.Sqrt, bias=eps[:, 0:1], scale=1.0 / D)
                if tok:
                    ins = act.activation(rstd_tok[:], aux[1][:, GC:GC + TB], ACT.Sqrt, bias=eps[:, 0:1],
                                         scale=1.0 / D)
                ins.then_inc(sem(f"{name}_root"), 1)

            act.wait_ge(sem("masks"), 5)
            act.wait_ge(sem("params"), 1)
            for j in range(AHEAD):
                cut(j)
            for c in range(4):
                x_hi("attn", c, xa, sem("attn_h"), c + 1)

            def square_heads(m):
                act.wait_ge(group_read, m + 1)
                act.activation(nrm[:], qn[:], ACT.Square).then_inc(sem("qk_squared"), 1)

            def root_heads(m, pair=0):
                act.wait_ge(sem("qk_mean"), m + 1)
                act.activation(nrm[:], aux[pair][:], ACT.Sqrt, bias=eps[:, 0:1],
                               scale=1.0 / HD).then_inc(sem("qk_rooted"), 1)

            q = st["qk"]
            for m in range(2):
                if m == 1:
                    cuts(q.slot + 8, js=range(0, 3))
                    root_heads(0)
                    cuts(q.slot + 8, js=range(3, 8))
                else:
                    cuts(q.slot)
                    norm_root("attn", tok=True)
                square_heads(m)
            with act.Fori(1, 4) as c:
                for m in range(2):
                    cuts(q.slot + 8 * m, 2 * c, range(0, 3))
                    root_heads(2 * c + m - 1)
                    cuts(q.slot + 8 * m, 2 * c, range(3, 8))
                    square_heads(2 * c + m)
            def soft_head(hd):
                b = hd % 2
                z = aux[0][:, b * GC:b * GC + 384]
                act.wait_ge(sem("z"), hd + 1)
                own.inc(act.activation(ell[:, b, :], z, ACT.Abs))
                own.settle()
                own.inc(act.activation(ell[:, b, :], ell[:, b, :], ACT.Exp, scale=-1.0))
                own.settle()
                act.activation(ell[:, b, :], ell[:, b, :], ACT.Ln, bias=1.0).then_inc(sem("ell"), 1)

            def weigh_head(hd):
                act.wait_ge(sem("log_weights"), hd + 1)
                act.activation(qk[:, hd].rearrange("p a b -> p (a b)")[:, 0:384], logb[:, hd % 2, :],
                               ACT.Exp).then_inc(sem("weights_raw"), 1)

            for g in range(4):
                for i in range(4):
                    soft_head(4 * g + i)
                    cuts(st["v"].slot + 8 * g, js=range(2 * i, 2 * i + 1))
                    if g == 0 and i == 0:
                        root_heads(7, pair=1)
                    if 4 * g + i:
                        weigh_head(4 * g + i - 1)
                    cuts(st["v"].slot + 8 * g, js=range(2 * i + 1, 2 * i + 2))
            weigh_head(HEADS - 1)
            for hd in range(HEADS):
                act.wait_ge(sem("o"), hd + 1)
                act.activation(xb[:, hd, 0, :], aux[0][:, (hd % 2) * GC:(hd % 2) * GC + T],
                               ACT.Copy).then_inc(sem("o_hi"), 1)

            with act.Fori(0, 4) as c:
                cuts(st["wo"].slot, c)
                x_hi("mlp0", c, xa, group_read, st["wo"].group + c + 1)

            def mlp(l, x_next):
                s = st[f"mlp{l}"].slot
                ub = xb if l == 0 else xa

                def squares(c, f):
                    act.wait_ge(group_read, st[f"mlp{l}"].group + 8 * f + c + 1)
                    own.inc(act.activation(ubuf[:], rbuf[:], ACT.Square))
                    own.settle()
                    act.activation(ub[:, bass.ds(4 * c, 4), 0, :], ubuf[:], ACT.Copy).then_inc(
                        sem(f"u_hi{l}"), 1)

                def up_down(f, first=False, last=False):
                    if first:
                        cuts(s)
                        norm_root(f"mlp{l}")
                        squares(0, 0)
                        act.wait_ge(sem(f"p_turned{l}"), 1)
                        act.activation(p_t[:, :, 0, :], aux[0][:, 0:GC].rearrange("p (a b) -> p a b", a=2),
                                       ACT.Copy).then_inc(sem(f"p_hi{l}"), 1)
                    with own.loop(int(first), 4, 1) as c:
                        cuts(s, 8 * f + c)
                        squares(c, f)
                    with act.Fori(0, 4) as c:
                        cuts(s + 32, 8 * f + c)
                        if last:
                            x_hi(f"gate{l}", c, x_next, group_read, st[f"mlp{l}"].group + 28 + c + 1)

                up_down(0, first=True)
                with own.loop(1, 3, 4) as f:
                    up_down(f)
                up_down(3, last=True)

            def ple_gate(l, x_next, next_name):
                for j in range(4):
                    cuts(st[f"ple{l}"].slot + j, js=range(1))
                s = st[f"gate{l}"].slot
                for c in range(4):
                    cuts(s + 8 * c, js=range(0, 4))
                    if c == 0:
                        norm_root(f"gate{l}")
                        act.wait_ge(sem(f"e{l}_mean"), 1)
                        act.activation(rstd_e[:], aux[1][:, GC:GC + T], ACT.Sqrt, bias=eps[:, 0:1],
                                       scale=1.0 / D).then_inc(sem(f"e{l}_root"), 1)
                    cuts(s + 8 * c, js=range(4, 8))
                    act.wait_ge(group_read, st[f"gate{l}"].group + c + 1)
                    act.activation(sig[:], rbuf[:], ACT.Sigmoid).then_inc(sem(f"gate_open{l}"), 1)
                    if x_next is not None:
                        x_hi(next_name, c, x_next, sem(f"{next_name}_h"), c + 1)

            def silu_conv(q, dst, bias_col):
                act.wait_ge(sem("conv"), q + 1)
                for n in range(TG):
                    ins = act.activation(dst(n), xc[:, n * T:(n + 1) * T], ACT.Silu,
                                         bias=misc[:, bass.ds(bias_col + n, 1)])
                ins.then_inc(sem("conv_silu"), 1)

            def y_square(g):
                act.wait_ge(sem("gated"), g + 1)
                for b in range(TB):
                    own.inc(act.activation(sq4[:].rearrange("p a b -> p (a b)")[:, b * GC:(b + 1) * GC],
                                              zg[:, b * GC:(b + 1) * GC], ACT.Square,
                                              accum_out=y_rms[:, b:b + 1]))
                own.settle()
                act.activation(y_rms[:], y_rms[:], ACT.Sqrt, bias=eps[:, 0:1],
                               scale=1.0 / GC).then_inc(sem("y_root"), 1)

            def y_hi(g, half):
                act.wait_ge(sem("y_turned"), g + 1)
                for n in range(TG):
                    ins = act.activation(xa[:, bass.ds(4 * g - KT * half + n, 1), 0, :],
                                         aux[0][:, n * T:(n + 1) * T], ACT.Copy,
                                         scale=misc[:, bass.ds(OUT_COL + 4 * g + n, 1)])
                ins.then_inc(sem("y_hi"), 1)

            def decay(g, b):
                act.wait_ge(sem("exponents"), 2 * g + b + 1)
                act.activation(mix[:, b], mix[:, b], ACT.Exp).then_inc(sem("decayed"), 1)

            def ssm_pair(half, g, i, first):
                s, r = st[f"xz{half}"].slot, 2 * i
                cuts(s, r, range(0, 2))
                if not first:
                    y_square(g - 1)
                cuts(s, r, range(2, 4))
                if first and half == 0:
                    silu_conv(3, lambda n: ct[:, 4 + n, :], 44)
                cuts(s, r, range(4, 5))
                if not first:
                    y_hi(g - 1, half)
                cuts(s, r, range(5, 8))
                if not first:
                    decay(g, 0)
                cuts(s + 8, r, range(0, 1))
                if not first:
                    decay(g, 1)
                cuts(s + 8, r, range(1, 4))
                silu_conv(4 + g, lambda n: xc[:, n * T:(n + 1) * T], 4 * g)
                cuts(s + 8, r, range(4, 5))
                if first:
                    decay(g, 0)
                cuts(s + 8, r, range(5, 7))
                if first:
                    decay(g, 1)
                cuts(s + 8, r, range(7, 8))
                act.wait_ge(slot_used, s + 16 + RAW * r)
                for b in range(TB):
                    ins = act.activation(zg[:, b * GC:(b + 1) * GC],
                                         gp[(st[f"xz{half}"].group + 1) % 2][:, b * GC:(b + 1) * GC],
                                         ACT.Silu, scale=rstd_tok[:, b:b + 1])
                ins.then_inc(sem("z_silu"), 1)

            def ssm():
                s = st["bc0"].slot
                cuts(s, js=range(0, 6))
                norm_root("ssm", tok=True)
                cuts(s, js=range(6, 8))
                cuts(st["dt"].slot, js=range(1))
                s = st["bc"].slot
                cuts(s, js=range(0, 4))
                silu_conv(0, lambda n: bt[:, n, :], 32)
                act.wait_ge(sem("dt_raw"), 1)
                own.inc(act.activation(dt_ell[:], dt[:], ACT.Abs))
                own.settle()
                own.inc(act.activation(dt_ell[:], dt_ell[:], ACT.Exp, scale=-1.0))
                own.inc(act.activation(head_p[:, 1, :], head_p[:, 1, :], ACT.Exp))
                own.settle()
                act.activation(dt_ell[:], dt_ell[:], ACT.Ln, bias=1.0).then_inc(sem("dt_ell"), 1)
                cuts(s, js=range(4, 8))
                for q in range(1, 3):
                    cuts(s + 8 * q, js=range(0, 4))
                    silu_conv(q, lambda n: (bt if q < 2 else ct)[:, 4 * (q % 2) + n, :], 32 + 4 * q)
                    cuts(s + 8 * q, js=range(4, 8))
                for half in range(2):
                    ssm_pair(half, 4 * half, 0, True)
                    with own.loop(1, 4, 2) as i:
                        ssm_pair(half, 4 * half + i, i, False)
                    s = st[f"out{half}"]
                    for c in range(4):
                        cuts(s.slot + 8 * c, js=range(0, 2))
                        if c == 0:
                            y_square(4 * half + 3)
                        cuts(s.slot + 8 * c, js=range(2, 5))
                        if c == 0:
                            y_hi(4 * half + 3, half)
                        cuts(s.slot + 8 * c, js=range(5, 8))
                        if half == 1:
                            x_hi("mlp1", c, xb, group_read, s.group + c + 1)

            mlp(0, xa)
            ple_gate(0, xb if layers > 1 else None, "ssm")
            if layers > 1:
                ssm()
                mlp(1, xb)
                ple_gate(1, None, "final")

        @block.vector
        def _(dve):
            own = Steps(dve, sem("dve_step"))

            def cut(slot, r=0):
                if slot >= n_slots:
                    return
                dve.wait_ge(hi_made, slot + 1 + RAW * r)
                dve.tensor_tensor(w_lo[slot % CUT][:], raw[slot % RAW][:], w_hi[slot % CUT][:].bitcast(F32),
                                  ALU.subtract).then_inc(lo_made, 1)

            def cuts(slot, r=0, js=range(HS_PER_GROUP)):
                for j in js:
                    cut(slot + AHEAD + j, r)

            def x_lo(name, c, dst):
                col = norm_col[name]
                dve.wait_ge(sem(f"{name}_hi"), c + 1)
                for n in range(TG):
                    k = 4 * c + n
                    ins = dve.scalar_tensor_tensor(
                        dst[:, bass.ds(k, 1), 1, :], h[:, bass.ds(k, 1), :], gain(col + k),
                        dst[:, bass.ds(k, 1), 0, :].bitcast(F32), ALU.mult, ALU.subtract)
                ins.then_inc(sem(f"{name}_lo"), 1)

            def read_group(s, done, r=0):
                dve.wait_ge(slot_used, done + RAW * r)

            def residual(s, done, r, c, par, name=None, dst=None):
                read_group(s, done, r)
                hc = h[:, bass.ds(4 * c, 4), :]
                dve.tensor_tensor(hc, hc, gp[par][:].rearrange("p (a b) -> p a b", a=TG),
                                  ALU.add).then_inc(group_read, 1)
                if name:
                    x_lo(name, c, dst)

            def norm_recip(name, tok=False):
                dve.wait_ge(sem(f"{name}_root"), 1)
                own.inc(dve.reciprocal(rstd[:], rstd[:]))
                if tok:
                    own.inc(dve.reciprocal(rstd_tok[:], rstd_tok[:]))
                own.settle()

            rstd4 = rstd[:].unsqueeze(1).broadcast_to([P, TG, T])

            for i, (dst, n, at) in enumerate(((gains, N_GAIN, 0), (conv_w, P, 0), (conv_w, N_CONV - P, P),
                                              (misc, N_CB + 2 + INNER // P, 0))):
                dve.wait_ge(sem("rows_turned"), 1)
                ins = dve.tensor_copy(dst[:, at:at + n], aux[1][:, 128 * i:128 * i + n])
                if i == 3:
                    own.inc(ins)
                    own.settle()
            dve.tensor_scalar(qscale[:], misc[:, Q_COL:Q_COL + 1], float(HD) ** -0.5, None,
                              ALU.mult).then_inc(sem("params"), 1)
            for c in range(4):
                dve.wait_ge(sem("x_turned"), c + 1)
                dve.tensor_copy(h[:, 4 * c:4 * c + 4, :],
                                (gp + [aux[0]])[c % 3][:].rearrange("p (a b) -> p a b", a=TG)).then_inc(
                                    sem("attn_h"), 1)
            for c in range(4):
                cut(c)
                x_lo("attn", c, xa)

            q = st["qk"]

            def scale_heads(m, par):
                read_group(q, q.slot + 8, m)
                if not isinstance(m, int) or m:
                    dve.wait_ge(sem("qk_normed"), m)
                dve.tensor_tensor(qn[:], gp[par][:].rearrange("p (a b) -> p a b", a=TG), rstd4,
                                  ALU.mult).then_inc(group_read, 1)

            def norm_heads(m, c, which, slot, r):
                g = qscale[:, 0:1] if which == 0 else misc[:, K_COL:K_COL + 1]
                cuts(slot, r, range(0, 3))
                dve.wait_ge(sem("qk_rooted"), m + 1)
                for n in range(TG):
                    own.inc(dve.reciprocal(nrm[:, n, :], nrm[:, n, :]))
                    own.settle()
                    ins = dve.scalar_tensor_tensor(qk[:, bass.ds(4 * c + n, 1), which, :], qn[:, n, :], g,
                                                   nrm[:, n, :], ALU.mult, ALU.mult)
                    cuts(slot, r, range(3 + n, 4 + n))
                ins.then_inc(sem("qk_normed"), 1)
                cuts(slot, r, range(7, 8))

            cuts(q.slot)
            norm_recip("attn", tok=True)
            scale_heads(0, 0)
            norm_heads(0, 0, 0, q.slot + 8, 0)
            scale_heads(1, 1)
            with own.loop(1, 4, 8) as c:
                norm_heads(2 * c - 1, c - 1, 1, q.slot, 2 * c)
                scale_heads(2 * c, 0)
                norm_heads(2 * c, c, 0, q.slot + 8, 2 * c)
                scale_heads(2 * c + 1, 1)

            def soft_head(hd):
                b = hd % 2
                z = aux[0][:, b * GC:b * GC + 384]
                dve.wait_ge(sem("ell"), hd + 1)
                own.inc(dve.scalar_tensor_tensor(soft[:, b, :], z, 0.0, ell[:, b, :], ALU.max, ALU.add))
                own.inc(dve.scalar_tensor_tensor(logb[:, b, :], z, 0.0, ell[:, b, :], ALU.min, ALU.subtract))
                own.settle()
                d = soft[:, b, :].rearrange("p (c n) -> p c n", c=3)[:, 0:3:2, :]
                dve.tensor_tensor(d, d, earlier[:].unsqueeze(1).broadcast_to([P, 2, P]),
                                  ALU.mult).then_inc(sem("soft"), 1)

            def log_head(hd):
                b = hd % 2
                dve.wait_ge(sem("suffix"), hd + 1)
                dve.tensor_tensor(logb[:, b, :], logb[:, b, :], aux[1][:, b * GC:b * GC + 384],
                                  ALU.subtract).then_inc(sem("log_weights"), 1)

            v = st["v"]
            for g in range(4):
                for i in range(4):
                    hd = 4 * g + i
                    if g == 0 and i > 1:
                        for n in range(2 * i - 4, 2 * i - 2):
                            dve.wait_ge(sem("qk_rooted"), 8)
                            own.inc(dve.reciprocal(nrm[:, n, :], nrm[:, n, :]))
                            own.settle()
                            ins = dve.scalar_tensor_tensor(qk[:, 12 + n, 1, :], qn[:, n, :],
                                                           misc[:, K_COL:K_COL + 1], nrm[:, n, :],
                                                           ALU.mult, ALU.mult)
                        if i == 3:
                            ins.then_inc(sem("qk_normed"), 1)
                    soft_head(hd)
                    cuts(v.slot + 8 * g, js=range(2 * i, 2 * i + 1))
                    if hd:
                        log_head(hd - 1)
                    cuts(v.slot + 8 * g, js=range(2 * i + 1, 2 * i + 2))
                read_group(v, v.slot + 8, g)
                for b in range(TB):
                    ins = dve.tensor_scalar(v_tok[:, 4 * g:4 * g + 4, b, :],
                                            gp[(v.group + g) % 2][:, b * GC:(b + 1) * GC].rearrange(
                                                "p (a d) -> p a d", a=4),
                                            rstd_tok[:, b:b + 1], None, ALU.mult)
                ins.then_inc(group_read, 1)
            log_head(HEADS - 1)
            for hd in range(HEADS):
                dve.wait_ge(sem("o_hi"), hd + 1)
                dve.tensor_tensor(xb[:, hd, 1, :], aux[0][:, (hd % 2) * GC:(hd % 2) * GC + T],
                                  xb[:, hd, 0, :].bitcast(F32), ALU.subtract).then_inc(sem("o_lo"), 1)

            s = st["wo"]
            with dve.Fori(0, 2) as c2:
                for b in range(2):
                    cuts(s.slot + 8 * b, 2 * c2)
                    residual(s, s.slot + 8 * b + 8, 2 * c2, 2 * c2 + b, (s.group + b) % 2, "mlp0", xa)

            def mlp(l, x_next):
                s = st[f"mlp{l}"]
                ub = xb if l == 0 else xa
                g0 = s.group % 2

                def relu(c, f, par):
                    read_group(s, s.slot + 8, 8 * f + c)
                    dve.scalar_tensor_tensor(rbuf[:], gp[par][:].rearrange("p (a b) -> p a b", a=TG), 0.0,
                                             rstd4, ALU.max, ALU.mult).then_inc(group_read, 1)
                    dve.wait_ge(sem(f"u_hi{l}"), 4 * f + c + 1)
                    dve.tensor_tensor(ub[:, bass.ds(4 * c, 4), 1, :], ubuf[:],
                                      ub[:, bass.ds(4 * c, 4), 0, :].bitcast(F32),
                                      ALU.subtract).then_inc(sem(f"u_lo{l}"), 1)

                def up_down(f, first=False, last=False):
                    if first:
                        cuts(s.slot)
                        norm_recip(f"mlp{l}")
                        relu(0, 0, g0)
                        cuts(s.slot + 8, js=range(0, 1))
                        dve.wait_ge(sem(f"p_hi{l}"), 1)
                        dve.tensor_tensor(p_t[:, :, 1, :], aux[0][:, 0:GC].rearrange("p (a b) -> p a b", a=2),
                                          p_t[:, :, 0, :].bitcast(F32), ALU.subtract).then_inc(
                                              sem(f"p_lo{l}"), 1)
                        cuts(s.slot + 8, js=range(1, 8))
                        relu(1, 0, (g0 + 1) % 2)
                    with dve.Fori(int(first), 2) as c2:
                        for b in range(2):
                            cuts(s.slot + 8 * b, 8 * f + 2 * c2)
                            relu(2 * c2 + b, f, (g0 + b) % 2)
                    with dve.Fori(0, 2) as c2:
                        for b in range(2):
                            cuts(s.slot + 32 + 8 * b, 8 * f + 2 * c2)
                            residual(s, s.slot + 40 + 8 * b, 8 * f + 2 * c2, 2 * c2 + b, (g0 + b) % 2,
                                     *((f"gate{l}", x_next) if last else ()))

                up_down(0, first=True)
                with dve.Fori(1, 3) as f:
                    up_down(f)
                up_down(3, last=True)

            def ple_gate(l, x_next, next_name):
                s = st[f"ple{l}"]
                for j in range(4):
                    cuts(s.slot + j, js=range(1))
                    read_group(s, s.slot + j + 1)
                    dve.tensor_copy(e[:, 4 * j:4 * j + 4, :],
                                    gp[(s.group + j) % 2][:].rearrange("p (a b) -> p a b", a=TG)).then_inc(
                                        group_read, 1)
                s = st[f"gate{l}"]
                for c in range(4):
                    cuts(s.slot + 8 * c, js=range(0, 4))
                    if c == 0:
                        norm_recip(f"gate{l}")
                        dve.wait_ge(sem(f"e{l}_root"), 1)
                        own.inc(dve.reciprocal(rstd_e[:], rstd_e[:]))
                        own.settle()
                    for n in range(TG):
                        k = 4 * c + n
                        ins = dve.scalar_tensor_tensor(e[:, k, :], e[:, k, :], gain(G_PLE + KT * l + k), rstd_e[:],
                                                       ALU.mult, ALU.mult)
                    own.inc(ins)
                    cuts(s.slot + 8 * c, js=range(4, 8))
                    read_group(s, s.slot + 8, c)
                    dve.tensor_tensor(rbuf[:], gp[(s.group + c) % 2][:].rearrange("p (a b) -> p a b", a=TG),
                                      rstd4, ALU.mult).then_inc(group_read, 1)
                    dve.wait_ge(sem(f"gate_open{l}"), c + 1)
                    own.settle()
                    own.inc(dve.tensor_tensor(sig[:], sig[:], e[:, 4 * c:4 * c + 4, :], ALU.mult))
                    own.settle()
                    hc = h[:, 4 * c:4 * c + 4, :]
                    dve.tensor_tensor(hc, hc, sig[:], ALU.add).then_inc(sem(f"{next_name}_h"), 1)
                    if x_next is not None:
                        x_lo(next_name, c, x_next)

            def conv_open(q, s, done, r, par):
                read_group(s, done, r)
                if not isinstance(q, int) or q >= 1:
                    dve.wait_ge(sem("conv_silu"), q)
                own.inc(dve.tensor_tensor(xr[:, :, KC - 1:], gp[par][:].rearrange("p (a b) -> p a b", a=TG),
                                          rstd4, ALU.mult))
                own.settle()
                dve.sem_inc(group_read, 1)

            def conv_tap(tap, col):
                for n in range(TG):
                    w = conv_w[:, bass.ds(tap * CONV_TILES + col + n, 1)]
                    o = xc[:, n * T:(n + 1) * T]
                    if tap == 0:
                        ins = dve.tensor_scalar(o, xr[:, n, 0:T], w, None, ALU.mult)
                    else:
                        ins = dve.scalar_tensor_tensor(o, xr[:, n, tap:tap + T], w, o, ALU.mult, ALU.add)
                if tap < KC - 1:
                    own.inc(ins)
                    own.settle()
                else:
                    ins.then_inc(sem("conv"), 1)

            def conv_taps(slot, r, col):
                conv_tap(0, col)
                for tap in range(1, KC):
                    conv_tap(tap, col)
                    cuts(slot, r, range(tap - 1, tap))
                cuts(slot, r, range(KC - 1, KC))

            def time_steps():
                s = st["dt"]
                read_group(s, s.slot + 1)
                dve.wait_ge(sem("heads_in"), 48)
                for b in range(TB):
                    ins = dve.scalar_tensor_tensor(dt[:, b, :], gp[s.group % 2][:, b * GC:b * GC + SH],
                                                   rstd_tok[:, b:b + 1], head_p[:, 0, :], ALU.mult, ALU.add)
                own.inc(ins)
                own.settle()
                dve.sem_inc(group_read, 1)
                dve.sem_inc(sem("dt_raw"), 1)
                dve.wait_ge(sem("dt_ell"), 1)
                own.inc(dve.scalar_tensor_tensor(dt[:], dt[:], 0.0, dt_ell[:], ALU.max, ALU.add))
                own.settle()
                dve.scalar_tensor_tensor(dt_a[:], dt[:], -1.0, head_p[:, 1, :].unsqueeze(1).broadcast_to([P, TB, SH]),
                                         ALU.mult, ALU.mult).then_inc(sem("dt_a"), 1)
                dve.wait_ge(sem("cumulated"), 1)
                dve.tensor_copy(decay_t[:], aux[1][0:SH, 0:T]).then_inc(sem("decay_t"), 1)
                dve.tensor_scalar(offset[:, 0:2, :], aux[1][:, GC:GC + 2 * SH].rearrange("p (b h) -> p b h", b=2),
                                  -1.0, None, ALU.mult)
                dve.tensor_copy(offset[:, 2, :], aux[1][:, GC + 2 * SH:GC + 3 * SH]).then_inc(sem("offset"), 1)

            def keep_cb(g):
                dve.wait_ge(sem("cb_raw"), g + 1)
                dve.tensor_copy(cb[:, g, :], aux[0][:, (g % 2) * GC:(g % 2) * GC + 384]).then_inc(sem("cb"), 1)

            def mix_heads(g, b):
                dve.wait_ge(sem("decayed"), 2 * g + b + 1)
                dve.tensor_tensor(mix[:, b], mix[:, b], cb[:, bass.ds(g, 1), :].broadcast_to([P, 4, 384]),
                                  ALU.mult).then_inc(sem("mixed"), 1)

            def y_gate(g):
                dve.wait_ge(sem("y"), g + 1)
                own.inc(dve.tensor_tensor(x_skip[:], x_skip[:], aux[1][:], ALU.add))
                dve.wait_ge(sem("z_silu"), g + 1)
                dve.sem_inc(group_read, 1)
                own.settle()
                dve.tensor_tensor(zg[:], zg[:], x_skip[:], ALU.mult).then_inc(sem("gated"), 1)

            def y_scale(g):
                dve.wait_ge(sem("y_root"), g + 1)
                own.inc(dve.reciprocal(y_rms[:], y_rms[:]))
                own.settle()
                for b in range(TB):
                    ins = dve.tensor_scalar(zg[:, b * GC:(b + 1) * GC], zg[:, b * GC:(b + 1) * GC],
                                            y_rms[:, b:b + 1], None, ALU.mult)
                ins.then_inc(sem("y_scaled"), 1)

            def y_lo(g, half):
                dve.wait_ge(sem("y_hi"), g + 1)
                for n in range(TG):
                    k = bass.ds(4 * g - KT * half + n, 1)
                    ins = dve.scalar_tensor_tensor(xa[:, k, 1, :], aux[0][:, n * T:(n + 1) * T],
                                                   misc[:, bass.ds(OUT_COL + 4 * g + n, 1)],
                                                   xa[:, k, 0, :].bitcast(F32), ALU.mult, ALU.subtract)
                ins.then_inc(sem("y_lo"), 1)

            def spread_x(g):
                dve.wait_ge(sem("x_tok"), g + 1)
                for b in range(TB):
                    src = aux[0][:, b * GC:(b + 1) * GC].rearrange("p (h d) -> p h d", h=8)
                    for dst, w in ((x_skip, head_p[:, 2, bass.ds(8 * g, 8)]), (xc, dt[:, b, bass.ds(8 * g, 8)])):
                        ins = dve.tensor_tensor(dst[:, b * GC:(b + 1) * GC].rearrange("p (h d) -> p h d", h=8), src,
                                                w.unsqueeze(2).broadcast_to([P, 8, SHD]), ALU.mult)
                ins.then_inc(sem("x_dt"), 1)

            def ssm_pair(half, g, i, first):
                sx = st[f"xz{half}"]
                s, r = sx.slot, 2 * i
                if first and half == 0:
                    conv_taps(s, r, 44)
                    cuts(s, r, range(4, 5))
                else:
                    cuts(s, r, range(0, 2))
                    if not first:
                        y_gate(g - 1)
                    cuts(s, r, range(2, 3))
                    if not first:
                        y_scale(g - 1)
                    cuts(s, r, range(3, 5))
                if not first:
                    y_lo(g - 1, half)
                if first and half == 0:
                    for j in range(4):
                        keep_cb(2 * j)
                        keep_cb(2 * j + 1)
                        if j < 3:
                            cuts(s, r, range(5 + j, 6 + j))
                else:
                    cuts(s, r, range(5, 8))
                conv_open(4 + g, sx, s + 8, r, sx.group % 2)
                conv_taps(s + 8, r, 4 * g)
                cuts(s + 8, r, range(4, 5))
                mix_heads(g, 0)
                cuts(s + 8, r, range(5, 7))
                mix_heads(g, 1)
                cuts(s + 8, r, range(7, 8))
                spread_x(g)

            def ssm():
                own.inc(dve.memset(xr[:, :, 0:KC - 1], 0.0))
                s = st["bc0"]
                cuts(s.slot, js=range(0, 6))
                norm_recip("ssm", tok=True)
                cuts(s.slot, js=range(6, 8))
                conv_open(0, s, s.slot + 8, 0, s.group % 2)
                cuts(st["dt"].slot, js=range(1))
                s = st["bc"]
                conv_taps(s.slot, 0, 32)
                time_steps()
                cuts(s.slot, js=range(4, 8))
                for q in range(3):
                    conv_open(q + 1, s, s.slot + 8 * q + 8, 0, (s.group + q) % 2)
                    if q < 2:
                        conv_taps(s.slot + 8 * q + 8, 0, 36 + 4 * q)
                        cuts(s.slot + 8 * q + 8, js=range(4, 8))
                for half in range(2):
                    ssm_pair(half, 4 * half, 0, True)
                    with own.loop(1, 4, 6) as i:
                        ssm_pair(half, 4 * half + i, i, False)
                    s = st[f"out{half}"]
                    for c in range(4):
                        cuts(s.slot + 8 * c, js=range(0, 2))
                        if c == 0:
                            y_gate(4 * half + 3)
                        cuts(s.slot + 8 * c, js=range(2, 3))
                        if c == 0:
                            y_scale(4 * half + 3)
                        cuts(s.slot + 8 * c, js=range(3, 5))
                        if c == 0:
                            y_lo(4 * half + 3, half)
                        cuts(s.slot + 8 * c, js=range(5, 8))
                        residual(s, s.slot + 8, c, c, (s.group + c) % 2, *(("mlp1", xb) if half else ()))

            mlp(0, xa)
            ple_gate(0, xb if layers > 1 else None, "ssm" if layers > 1 else "final")
            if layers > 1:
                ssm()
                mlp(1, xb)
                ple_gate(1, None, "final")
            for c in range(4):
                dve.wait_ge(sem("final_turned"), c + 1)
                if c >= 2:
                    dve.wait_ge(sem(f"out_done{c % 2}"), 16)
                dve.tensor_copy((rbuf if c % 2 == 0 else ubuf)[:].rearrange("p a b -> p (a b)"),
                                aux[c % 2][:]).then_inc(sem("out_staged"), 1)

        @block.tensor
        def _(pe):
            def open_group(group, par):
                if not isinstance(group, int) or group >= 2:
                    pe.wait_ge(group_read, group - 1)
                return gp[par]

            def products(pst, slot, r, xs, k0, first, last):
                pe.wait_ge(lo_made, slot + 1 + RAW * r)
                hi, lo = w_hi[slot % CUT], w_lo[slot % CUT]
                for n in range(TG):
                    for k in range(2):
                        cols = slice(n * P, (n + 1) * P)
                        for i, (w, part) in enumerate(((hi, 0), (hi, 1), (lo, 0))):
                            mm = pe.matmul(pst[:, n * T:(n + 1) * T], w[:, k, cols], xs[:, k0 + k, part, :],
                                           start=first and k == 0 and i == 0 and n % 2 == 0,
                                           stop=last and k == 1 and i == 2, skip_group_check=True)
                            if n == TG - 1 and k == 1 and i == 2:
                                mm.then_inc(slot_used, 1)

            def products_tok(pst, slot, r, xs, k0, first, last):
                pe.wait_ge(lo_made, slot + 1 + RAW * r)
                hi, lo = w_hi[slot % CUT], w_lo[slot % CUT]
                for b in range(TB):
                    for k in range(2):
                        for i, (w, part) in enumerate(((hi, 0), (hi, 1), (lo, 0))):
                            mm = pe.matmul(pst[:, b * GC:(b + 1) * GC], xs[:, k0 + k, part, b * P:(b + 1) * P],
                                           w[:, k, :], start=first and k == 0 and i == 0,
                                           stop=last and k == 1 and i == 2)
                            if b == TB - 1 and k == 1 and i == 2:
                                mm.then_inc(slot_used, 1)

            def half_slots(pst, slot, r, xs, js, x_ready=None, x_from=0, fn=products):
                for j in js:
                    if x_ready is not None and j % 2 == 0:
                        if j % 2 == 0:
                            pe.wait_ge(x_ready, x_from + (2 * j) // 4 + 1)
                    fn(pst, slot + j, r, xs, 2 * j, j == 0, j == HS_PER_GROUP - 1)

            def mean(name, tok=False):
                pe.wait_ge(sem(f"{name}_sum"), 1)
                mm = pe.matmul(aux[1][:, 0:T], ones[:], acc4[:, 0, :], start=True, stop=True)
                if tok:
                    for b in range(TB):
                        mm = pe.matmul(aux[1][:, GC + b:GC + b + 1], acc4[:, 0, b * P:(b + 1) * P], ones[:, 0:1],
                                       start=True, stop=True)
                mm.then_inc(sem(f"{name}_mean"), 1)

            pe.wait_ge(sem("masks"), 5)
            pe.wait_ge(sem("rows_in"), 16 * 11)
            for i, (src, n) in enumerate(((rows0, N_GAIN), (rows1, P), (rows2, N_CONV - P),
                                          (rows3, N_CB + 2 + INNER // P))):
                tr = pe.transpose(aux[1][:, 128 * i:128 * i + n], src[0:n, :], ident[0:n, 0:n])
            tr.then_inc(sem("rows_turned"), 1)
            for c in range(4):
                pe.wait_ge(sem(f"x_in{c}"), 16)
                if c == 3:
                    pe.wait_ge(sem("attn_h"), 1)
                for n in range(TG):
                    for b in range(TB):
                        tr = pe.transpose((gp + [aux[0]])[c % 3][:, n * T + b * P:n * T + (b + 1) * P],
                                          x_tok[:, b, (4 * c + n) * P:(4 * c + n + 1) * P], ident[:])
                tr.then_inc(sem("x_turned"), 1)

            q = st["qk"]

            def head_means(m, pair=0):
                pe.wait_ge(sem("qk_squared"), m + 1)
                for b in range(2):
                    mm = pe.matmul(aux[pair][:, b * GC:(b + 1) * GC], ones[:],
                                   nrm[:, 2 * b:2 * b + 2, :], start=True, stop=True)
                mm.then_inc(sem("qk_mean"), 1)

            pe.wait_ge(sem("attn_h"), 4)
            ps = open_group(0, 0)
            half_slots(ps, q.slot, 0, xa, range(0, 4), sem("attn_lo"))
            pe.wait_ge(sem("params"), 1)
            mean("attn", tok=True)
            half_slots(ps, q.slot, 0, xa, range(4, 8), sem("attn_lo"))
            ps = open_group(1, 1)
            half_slots(ps, q.slot + 8, 0, xa, range(0, 2))
            head_means(0)
            half_slots(ps, q.slot + 8, 0, xa, range(2, 8))
            with pe.Fori(1, 4) as c:
                for m in range(2):
                    ps = open_group(q.group + 2 * c + m, m)
                    half_slots(ps, q.slot + 8 * m, 2 * c, xa, range(0, 2))
                    head_means(2 * c + m - 1)
                    half_slots(ps, q.slot + 8 * m, 2 * c, xa, range(2, 8))

            def scores(hd):
                b = hd % 2
                pe.wait_ge(sem("qk_normed"), 8 if hd >= 12 else 7)
                if hd >= 2:
                    pe.wait_ge(sem("soft"), hd - 1)
                z = aux[0][:, b * GC:b * GC + 384]
                pe.matmul(z[:, 0:T], qk[:, hd, 1, 0:P], qk[:, hd, 0, :], start=True, stop=True)
                pe.matmul(z[:, T:T + P], qk[:, hd, 1, P:T], qk[:, hd, 0, P:T], start=True,
                          stop=True).then_inc(sem("z"), 1)

            def suffix(hd):
                b = hd % 2
                pe.wait_ge(sem("soft"), hd + 1)
                if hd >= 2:
                    pe.wait_ge(sem("log_weights"), hd - 1)
                u = aux[1][:, b * GC:b * GC + 384]
                pe.matmul(u, later[:], soft[:, b, :], start=True, stop=False, skip_group_check=True)
                pe.matmul(u[:, P:T], ones[:], soft[:, b, T:T + P], start=False, stop=True,
                          skip_group_check=True).then_inc(sem("suffix"), 1)

            v = st["v"]
            for g in range(4):
                ps = open_group(v.group + g, (v.group + g) % 2)
                for i in range(4):
                    hd = 4 * g + i
                    scores(hd)
                    if hd == 0:
                        half_slots(ps, v.slot, 0, xa, range(0, 1), fn=products_tok)
                        head_means(7, pair=1)
                        half_slots(ps, v.slot, 0, xa, range(1, 2), fn=products_tok)
                        pe.wait_ge(sem("qk_rooted"), 8)
                    else:
                        half_slots(ps, v.slot + 8 * g, 0, xa, range(2 * i, 2 * i + 2), fn=products_tok)
                    suffix(hd)

            for hd in range(HEADS):
                pe.wait_ge(sem("weights_masked"), hd + 1)
                pe.wait_ge(group_read, v.group + 4)
                if hd >= 2:
                    pe.wait_ge(sem("o_lo"), hd - 1)
                o = aux[0][:, (hd % 2) * GC:(hd % 2) * GC + T]
                a = qk[:, hd].rearrange("p a b -> p (a b)")
                pe.matmul(o, v_tok[:, hd, 0, :], a[:, 0:T], start=True, stop=False, skip_group_check=True)
                pe.matmul(o[:, P:T], v_tok[:, hd, 1, :], a[:, T:T + P], start=False, stop=True,
                          skip_group_check=True).then_inc(sem("o"), 1)

            def pair_loop(s, slot, group, xs, x_ready, x_step, n=2, r0=0, start=0, wait_from=0):
                with pe.Fori(start, n) as c2:
                    for b in range(2):
                        ps = open_group(group + 2 * c2 + b + r0, (s.group + b) % 2)
                        for j in range(HS_PER_GROUP):
                            if x_ready is not None and j % 2 == 0:
                                pe.wait_ge(x_ready, wait_from + x_step * (j // 2 + 1))
                            products(ps, slot + 8 * b + j, 2 * c2 + r0, xs, 2 * j, j == 0, j == 7)

            s = st["wo"]
            pair_loop(s, s.slot, s.group, xb, sem("o_lo"), 4)

            def mlp(l, xs, us):
                s = st[f"mlp{l}"]
                ps = open_group(s.group, s.group % 2)
                half_slots(ps, s.slot, 0, xs, range(0, 4), sem(f"mlp{l}_lo"))
                mean(f"mlp{l}")
                half_slots(ps, s.slot, 0, xs, range(4, 6), sem(f"mlp{l}_lo"))
                pe.wait_ge(sem(f"p_in{l}"), 16)
                for k in range(2):
                    for b in range(TB):
                        tr = pe.transpose(aux[0][:, k * T + b * P:k * T + (b + 1) * P],
                                          p_tok[:, b, k * P:(k + 1) * P], ident[:])
                tr.then_inc(sem(f"p_turned{l}"), 1)
                half_slots(ps, s.slot, 0, xs, range(6, 8), sem(f"mlp{l}_lo"))
                ps = open_group(s.group + 1, (s.group + 1) % 2)
                half_slots(ps, s.slot + 8, 0, xs, range(8))
                pair_loop(s, s.slot, s.group, xs, None, 0, start=1)
                pair_loop(s, s.slot + 32, s.group + 4, us, sem(f"u_lo{l}"), 1)
                with pe.Fori(1, 4) as f:
                    pair_loop(s, s.slot, s.group, xs, None, 0, r0=8 * f)
                    pair_loop(s, s.slot + 32, s.group + 4, us, sem(f"u_lo{l}"), 1, r0=8 * f, wait_from=4 * f)

            def ple_gate(l, xs):
                s = st[f"ple{l}"]
                pe.wait_ge(sem(f"p_lo{l}"), 1)
                for j in range(4):
                    ps = open_group(s.group + j, (s.group + j) % 2)
                    products(ps, s.slot + j, 0, p_t, 0, True, True)
                s = st[f"gate{l}"]
                for c in range(4):
                    ps = open_group(s.group + c, (s.group + c) % 2)
                    half_slots(ps, s.slot + 8 * c, 0, xs, range(0, 4), sem(f"gate{l}_lo"))
                    if c == 0:
                        pe.wait_ge(sem(f"e{l}_sum"), 1)
                        pe.matmul(aux[1][:, GC:GC + T], ones[:], acc_e[:, 0, :], start=True,
                                  stop=True).then_inc(sem(f"e{l}_mean"), 1)
                        mean(f"gate{l}")
                    half_slots(ps, s.slot + 8 * c, 0, xs, range(4, 8), sem(f"gate{l}_lo"))

            def cumulate():
                pe.wait_ge(sem("dt_a"), 1)
                for b in range(TB):
                    pe.matmul(aux[1][0:SH, b * P:(b + 1) * P], dt_a[:, b, :], upto[:], start=True, stop=True)
                for b in range(TB):
                    pe.matmul(aux[1][:, GC + b * SH:GC + (b + 1) * SH], upto[:], dt_a[:, b, :], start=True,
                              stop=True)
                pe.matmul(aux[1][:, GC + 2 * SH:GC + 3 * SH], later[:], dt_a[:, 0, :], start=True,
                          stop=True).then_inc(sem("cumulated"), 1)

            def cb_products(g):
                pe.wait_ge(sem("conv_silu"), 4)
                if g >= 2:
                    pe.wait_ge(sem("cb"), g - 1)
                o = aux[0][:, (g % 2) * GC:(g % 2) * GC + 384]
                pe.matmul(o[:, 0:T], bt[:, g, 0:P], ct[:, g, :], start=True, stop=True)
                pe.matmul(o[:, T:T + P], bt[:, g, P:T], ct[:, g, P:T], start=True,
                          stop=True).then_inc(sem("cb_raw"), 1)

            def turn_y(g):
                pe.wait_ge(sem("y_scaled"), g + 1)
                for n in range(TG):
                    for b in range(TB):
                        tr = pe.transpose(aux[0][:, n * T + b * P:n * T + (b + 1) * P],
                                          zg[:, b * GC + n * P:b * GC + (n + 1) * P], ident[:])
                tr.then_inc(sem("y_turned"), 1)

            def turn_x(g):
                pe.wait_ge(sem("conv_silu"), g + 5)
                if not isinstance(g, int) or g:
                    pe.wait_ge(sem("y_lo"), g)
                else:
                    pe.wait_ge(sem("cb"), SG)
                for n in range(TG):
                    for b in range(TB):
                        tr = pe.transpose(aux[0][:, b * GC + n * P:b * GC + (n + 1) * P],
                                          xc[:, n * T + b * P:n * T + (b + 1) * P], ident[:])
                tr.then_inc(sem("x_tok"), 1)

            def y_products(g):
                pe.wait_ge(sem("mixed"), 2 * g + 2)
                pe.wait_ge(sem("x_dt"), g + 1)
                for hd in range(8):
                    m = mix[:, hd // 4, hd % 4, :]
                    c = slice(hd * SHD, (hd + 1) * SHD)
                    x0, x1 = xc[:, 0:GC][:, c], xc[:, GC:2 * GC][:, c]
                    y0, y1 = aux[1][:, 0:GC][:, c], aux[1][:, GC:2 * GC][:, c]
                    pe.matmul(y0, m[:, 0:P], x0, start=True, stop=True)
                    pe.matmul(y1, m[:, P:T], x0, start=True, stop=False)
                    mm = pe.matmul(y1, m[:, T:T + P], x1, start=False, stop=True)
                mm.then_inc(sem("y"), 1)
                pe.wait_ge(sem("y"), g + 1)
                pe.sem_inc(sem("mix_free"), 1)

            def ssm_pair(half, g, i, first):
                sx = st[f"xz{half}"]
                s, r = sx.slot, 2 * i
                ps = open_group(sx.group + 2 * i, sx.group % 2)
                half_slots(ps, s, r, xb, range(0, 2))
                if not first:
                    y_products(g - 1)
                half_slots(ps, s, r, xb, range(2, 5))
                if first:
                    if half == 0:
                        for j in range(3):
                            cb_products(2 * j)
                            cb_products(2 * j + 1)
                            half_slots(ps, s, r, xb, range(5 + j, 6 + j))
                        cb_products(6)
                        cb_products(7)
                    else:
                        half_slots(ps, s, r, xb, range(5, 8))
                else:
                    turn_y(g - 1)
                    half_slots(ps, s, r, xb, range(5, 8))
                ps = open_group(sx.group + 2 * i + 1, (sx.group + 1) % 2)
                half_slots(ps, s + 8, r, xb, range(0, 6), fn=products_tok)
                turn_x(g)
                half_slots(ps, s + 8, r, xb, range(6, 8), fn=products_tok)

            def ssm():
                pe.sem_inc(sem("mix_free"), 1)
                s = st["bc0"]
                ps = open_group(s.group, s.group % 2)
                half_slots(ps, s.slot, 0, xb, range(0, 6), sem("ssm_lo"))
                mean("ssm", tok=True)
                half_slots(ps, s.slot, 0, xb, range(6, 8), sem("ssm_lo"))
                s = st["dt"]
                pe.wait_ge(lo_made, s.slot + 1)
                ps = open_group(s.group, s.group % 2)
                hi, lo = (w[s.slot % CUT][:].rearrange("p a b -> p (a b)").rearrange("p (k n) -> p k n", k=KT)
                          for w in (w_hi, w_lo))
                for b in range(TB):
                    for k in range(KT):
                        for i, (w, part) in enumerate(((hi, 0), (hi, 1), (lo, 0))):
                            mm = pe.matmul(ps[:, b * GC:b * GC + SH], xb[:, k, part, b * P:(b + 1) * P], w[:, k, :],
                                           start=k == 0 and i == 0, stop=k == KT - 1 and i == 2)
                mm.then_inc(slot_used, 1)
                s = st["bc"]
                for q in range(3):
                    ps = open_group(s.group + q, (s.group + q) % 2)
                    half_slots(ps, s.slot + 8 * q, 0, xb, range(0, 6))
                    if q == 0:
                        cumulate()
                    half_slots(ps, s.slot + 8 * q, 0, xb, range(6, 8))
                for half in range(2):
                    ssm_pair(half, 4 * half, 0, True)
                    with pe.Fori(1, 4) as i:
                        ssm_pair(half, 4 * half + i, i, False)
                    s = st[f"out{half}"]
                    for c in range(4):
                        ps = open_group(s.group + c, (s.group + c) % 2)
                        half_slots(ps, s.slot + 8 * c, 0, xa, range(0, 2), sem("y_lo"), 4 * half)
                        if c == 0:
                            y_products(4 * half + 3)
                        half_slots(ps, s.slot + 8 * c, 0, xa, range(2, 5), sem("y_lo"), 4 * half)
                        if c == 0:
                            turn_y(4 * half + 3)
                        half_slots(ps, s.slot + 8 * c, 0, xa, range(5, 8), sem("y_lo"), 4 * half)

            mlp(0, xa, xb)
            ple_gate(0, xa)
            if layers > 1:
                ssm()
                mlp(1, xb, xa)
                ple_gate(1, xb)
            for c in range(4):
                pe.wait_ge(sem("final_h"), c + 1)
                if c >= 2:
                    pe.wait_ge(sem("out_staged"), c - 1)
                for b in range(TB):
                    for n in range(TG):
                        tr = pe.transpose(aux[c % 2][:, b * GC + n * P:b * GC + (n + 1) * P],
                                          h[:, 4 * c + n, b * P:(b + 1) * P], ident[:])
                tr.then_inc(sem("final_turned"), 1)


_INS = ['x', 'p', 'attn_norm', 'attn_w_qkv', 'attn_q_norm', 'attn_k_norm', 'attn_w_o', 'ssm_norm',
        'ssm_w_in', 'ssm_conv_w', 'ssm_conv_b', 'ssm_dt_bias', 'ssm_a_log', 'ssm_d', 'ssm_out_norm',
        'ssm_w_out', 'mlp_norm', 'mlp_w_up', 'mlp_w_down', 'ple_w_proj', 'ple_norm', 'ple_gate_norm',
        'ple_w_gate']


def kernel(**inputs):
    import numpy as _np
    import concourse.bacc as _bacc
    from concourse import mybir as _mybir
    from concourse.bass_utils import run_bass_kernel_spmd as _run

    nc = _bacc.Bacc("TRN2", target_bir_lowering=False, num_devices=1)
    arrays, args = {}, {}
    for name in _INS:
        a = _np.ascontiguousarray(inputs[name])
        arrays[f"in_{name}"] = a
        args[name] = nc.dram_tensor(f"in_{name}", a.shape, _mybir.dt.from_np(a.dtype), kind="ExternalInput").ap()
    args["out"] = nc.dram_tensor("out_h", (1, T, D), F32, kind="ExternalOutput").ap()
    args["decay_rows"] = nc.dram_tensor("decay_rows", (SH, T), F32).ap()
    build_trunk(nc, 2, **args)
    r = _run(nc, [arrays], core_ids=[0])
    return r.results[0]["out_h"]
```

```python
from contextlib import ExitStack, contextmanager

import concourse.bass as bass
from concourse import mybir

F32 = mybir.dt.float32
F32R = mybir.dt.float32r
ALU = mybir.AluOpType
ACT = mybir.ActivationFunctionType

P = 128
D = 2048
T = 256
KT = D // P
TB = T // P
EPS = 1e-6
HEADS, HD = 16, 128
FF = 4 * D
PLE = 256
GC = 512
TG = GC // P
HS_PER_GROUP = KT // 2
RAW, CUT = 8, 4
AHEAD = CUT
INNER = 4096
SH, SHD, SG, SN = 64, 64, 8, 128
CONV_TILES = (INNER + 2 * SG * SN) // P
KC = 4


class Steps:

    def __init__(self, eng, sem):
        self.eng, self.sem, self.base, self.k = eng, sem, 0, 0

    def inc(self, ins):
        ins.then_inc(self.sem, 1)
        self.k += 1

    def settle(self):
        self.eng.wait_ge(self.sem, self.base + self.k)

    @contextmanager
    def loop(self, start, end, per):
        base, k = self.base, self.k
        with self.eng.Fori(start, end) as i:
            self.base, self.k = base + k + (i - start) * per, 0
            yield i
            assert self.k == per, (self.k, per)
        self.base, self.k = base, k + (end - start) * per


class Stage:

    def __init__(self, slot, group, groups, per_group):
        self.slot, self.group, self.groups, self.per_group = slot, group, groups, per_group


def plan(layers):
    st, at = {}, [0, 0]

    def add(name, groups, per_group=HS_PER_GROUP):
        st[name] = Stage(at[0], at[1], groups, per_group)
        at[0] += groups * per_group
        at[1] += groups

    for l in range(layers):
        if l == 0:
            add("qk", 8)
            add("v", 4)
            add("wo", 4)
        else:
            add("bc0", 1)
            add("dt", 1, 1)
            add("bc", 3)
            for half in range(2):
                add(f"xz{half}", SG)
                add(f"out{half}", 4)
        add(f"ple{l}", 4, 1)
        add(f"mlp{l}", 32)
        add(f"gate{l}", 4)
    return st, at[0]


def build_trunk(nc, layers, x, p, attn_norm, attn_w_qkv, attn_q_norm, attn_k_norm, attn_w_o,
                ssm_norm, ssm_w_in, ssm_conv_w, ssm_conv_b, ssm_dt_bias, ssm_a_log, ssm_d,
                ssm_out_norm, ssm_w_out, mlp_norm, mlp_w_up, mlp_w_down,
                ple_w_proj, ple_norm, ple_gate_norm, ple_w_gate, out, decay_rows):
    st, n_slots = plan(layers)
    with ExitStack() as ctx:
        def sb(name, shape, dt=F32):
            return ctx.enter_context(nc.sbuf_tensor(name, shape, dt))

        sems = {}

        def sem(name):
            if name not in sems:
                sems[name] = ctx.enter_context(nc.semaphore(name))
            return sems[name]

        raw = [sb(f"raw{i}", [P, 2, GC]) for i in range(RAW)]
        w_hi = [sb(f"w_hi{i}", [P, 2, GC], F32R) for i in range(CUT)]
        w_lo = [sb(f"w_lo{i}", [P, 2, GC], F32R) for i in range(CUT)]
        h = sb("h", [P, KT, T])
        xa = sb("xa", [P, KT, 2, T], F32R)
        ident = sb("ident", [P, P])
        ones = sb("ones", [P, P])
        later = sb("later", [P, P])
        earlier = sb("earlier", [P, P])
        upto = sb("upto", [P, P])
        eps = sb("eps", [P, 1])
        never = sb("never", [P, P])
        N_GAIN, N_CONV, N_CB = 8 * KT, KC * CONV_TILES, CONV_TILES
        gains = sb("gains", [P, N_GAIN])
        conv_w = sb("conv_w", [P, N_CONV])
        misc = sb("misc", [P, N_CB + 2 + INNER // P])
        G_SSM, G_MLP, G_PLE, G_GATE, G_ATTN = 0, KT, 3 * KT, 5 * KT, 7 * KT
        Q_COL, K_COL, OUT_COL = N_CB, N_CB + 1, N_CB + 2
        qscale = sb("qscale", [P, 1])
        rstd = sb("rstd", [P, T])
        rstd_tok = sb("rstd_tok", [P, TB])
        rstd_e = sb("rstd_e", [P, T])
        head_eps = rstd_e
        sq4 = sb("sq4", [P, TG, T])
        acc4 = sb("acc4", [P, TG, T])

        with ExitStack() as c:
            c.enter_context(nc.sbuf_tensor("xb_first_half", [P, KT * T], F32))
            v_tok = c.enter_context(nc.sbuf_tensor("v_tok", [P, HEADS, TB, HD], F32))
        xb = sb("xb", [P, KT, 2, T], F32R)

        def phase(tensors):
            with ExitStack() as c:
                return [c.enter_context(nc.sbuf_tensor(n, s, dt)) for n, s, dt in tensors]

        x_tok, rows0, rows1, rows2, rows3, rows4 = phase(
            [("x_tok", [P, TB, D], F32)] + [(f"rows{i}", [P, P], F32) for i in range(5)])
        qk, sq, nrm = phase([("qk", [P, HEADS, 2, T], F32), ("sq", [P, TG, T], F32),
                             ("nrm", [P, TG, T], F32)])
        soft, logb, ell = phase([("qk_again", [P, HEADS, 2, T], F32), ("sq_again", [P, TG, T], F32),
                                    ("nrm_again", [P, TG, T], F32), ("soft", [P, 2, 384], F32),
                                    ("logb", [P, 2, 384], F32), ("ell", [P, 2, 384], F32)])[3:]
        e, rbuf, ubuf, p_tok, p_t, sig, acc_e = phase(
            [("e", [P, KT, T], F32), ("rbuf", [P, TG, T], F32), ("ubuf", [P, TG, T], F32),
             ("p_tok", [P, TB, PLE], F32), ("p_t", [P, 2, 2, T], F32R), ("sig", [P, TG, T], F32),
             ("acc_e", [P, TG, T], F32)])

        ssm_shapes = [("cb", [P, SG, 384], F32), ("xr", [P, TG, KC - 1 + T], F32), ("xc", [P, TG * T], F32),
                      ("x_skip", [P, TB * GC], F32), ("zg", [P, TB * GC], F32), ("dt", [P, TB, SH], F32),
                      ("dt_a", [P, TB, SH], F32), ("dt_ell", [P, TB, SH], F32), ("decay_t", [SH, T], F32),
                      ("offset", [P, 3, SH], F32), ("head_p", [P, 3, SH], F32), ("y_rms", [P, TB], F32)]
        cb, xr, xc, x_skip, zg, dt, dt_a, dt_ell, decay_t, offset, head_p, y_rms, rb, mix = phase(
            ssm_shapes + [("rb", [P, 4, T], F32), ("mix", [P, 2, 4, 384], F32)])
        bt, ct = phase([(n + "_again", *z) for n, *z in ssm_shapes] +
                       [("bt", [P, SG, T], F32), ("ct", [P, SG, T], F32)])[-2:]

        gp = [ctx.enter_context(nc.psum_tensor(f"group_pair{i}", [P, 2 * GC], F32)) for i in range(2)]
        aux = [ctx.enter_context(nc.psum_tensor(f"aux_pair{i}", [P, 2 * GC], F32)) for i in range(2)]

        landed = [sem(f"landed{i}") for i in range(RAW)]
        hi_made = sem("hi_made")
        lo_made = sem("lo_made")
        slot_used = sem("slot_used")
        group_read = sem("group_read")

        def gain(col, n=1):
            return gains[:, bass.ds(col, n)]

        norm_col = {"attn": G_ATTN, "ssm": G_SSM}
        for l in range(layers):
            norm_col[f"mlp{l}"] = G_MLP + KT * l
            norm_col[f"gate{l}"] = G_GATE + KT * l

        block = ctx.enter_context(nc.Block())

        @block.sync
        def _(sp):
            def load_x(c):
                sp.dma_start(x_tok[:, :, c * GC:(c + 1) * GC],
                             x[0, :, c * GC:(c + 1) * GC].rearrange("(b q) n -> q b n", q=P)).then_inc(
                                 sem(f"x_in{c}"), 16)
            sp.dma_start(rows4[0:KT, :], attn_norm.rearrange("l (k p) -> (l k) p", p=P)).then_inc(
                sem("gain_in"), 16)
            load_x(0)
            rows = [
                (rows0, G_SSM, ssm_norm.rearrange("l (k p) -> (l k) p", p=P)),
                (rows0, G_MLP, mlp_norm.rearrange("l (k p) -> (l k) p", p=P)),
                (rows0, G_PLE, ple_norm.rearrange("l (k p) -> (l k) p", p=P)),
                (rows0, G_GATE, ple_gate_norm.rearrange("l (k p) -> (l k) p", p=P)),
                (rows1, 0, ssm_conv_w[0].rearrange("c (k p) -> (c k) p", p=P)[0:P]),
                (rows2, 0, ssm_conv_w[0].rearrange("c (k p) -> (c k) p", p=P)[P:N_CONV]),
                (rows3, 0, ssm_conv_b.rearrange("l (k p) -> (l k) p", p=P)),
                (rows3, Q_COL, attn_q_norm),
                (rows3, K_COL, attn_k_norm),
                (rows3, OUT_COL, ssm_out_norm.rearrange("l (k p) -> (l k) p", p=P)),
            ]

            def load(slot, r, src, shape=None):
                dst = raw[slot % RAW][:] if shape is None else \
                    raw[slot % RAW][:].rearrange("p a b -> p (a b)").rearrange("p (k n) -> p k n", k=shape)
                if slot >= RAW or not isinstance(r, int):
                    sp.wait_ge(lo_made, slot - RAW + 1 + RAW * r)
                sp.dma_start(dst, src).then_inc(landed[slot % RAW], 16)

            def load_group(slot, r, w, k0, col):
                for j in range(HS_PER_GROUP):
                    load(slot + j, r, w[:, bass.ds(k0 + 2 * j, 2), bass.ds(col, GC)])

            def tiles(w):
                return w.rearrange("(k p) n -> p k n", p=P)

            def load_out(name, w, k0, l=None):
                for c in range(4):
                    load_group(st[name].slot, c, w, k0, c * GC)
                    if c == 2 and l is not None:
                        sp.dma_start(p_tok[:], p[l, 0].rearrange("(b q) n -> q b n", q=P)).then_inc(
                            sem(f"p_in{l}"), 16)

            def load_mlp(l):
                s = st[f"mlp{l}"].slot
                up, down = tiles(mlp_w_up[l]), tiles(mlp_w_down[l])
                with sp.Fori(0, 4) as f:
                    with sp.Fori(0, 4) as c:
                        load_group(s, f * 8 + c, up, 0, f * D + c * GC)
                    with sp.Fori(0, 4) as c:
                        load_group(s + 32, f * 8 + c, down, f * KT, c * GC)

            def load_ple(l):
                s = st[f"ple{l}"].slot
                for j in range(4):
                    load(s + j, 0, tiles(ple_w_proj[l])[:, :, j * GC:(j + 1) * GC])

            def load_simple(name, w, groups, col=0):
                with sp.Fori(0, groups) as c:
                    load_group(st[name].slot, c, w, 0, c * GC + col)

            wqkv = tiles(attn_w_qkv[0])
            s = st["qk"].slot
            for j in range(HS_PER_GROUP):
                load(s + j, 0, wqkv[:, 2 * j:2 * j + 2, 0:GC])
                if j < 2:
                    load_x(j + 1)
                if j == 1:
                    load_x(3)
                if j == 3:
                    for dst, at, src in rows:
                        sp.dma_start(dst[at:at + src.shape[0], :], src).then_inc(sem("rows_in"), 16)
            load_group(s + 8, 0, wqkv, 0, D)
            with sp.Fori(1, 4) as c:
                load_group(s, c * 2, wqkv, 0, c * GC)
                load_group(s + 8, c * 2, wqkv, 0, c * GC + D)
            load_simple("v", wqkv, 4, 2 * D)
            load_out("wo", tiles(attn_w_o[0]), 0, 0)
            for l in range(layers):
                if l == 1:
                    w_in, w_out = tiles(ssm_w_in[0]), tiles(ssm_w_out[0])
                    load_group(st["bc0"].slot, 0, w_in, 0, 2 * INNER)
                    load(st["dt"].slot, 0, w_in[:, :, 2 * INNER + 2 * SG * SN:], shape=KT)
                    load_simple("bc", w_in, 3, 2 * INNER + GC)
                    for half in range(2):
                        with sp.Fori(1, 5) as i:
                            first, col = st[f"xz{half}"].slot - 2 * HS_PER_GROUP, half * D - GC
                            load_group(first, 2 * i, w_in, 0, INNER + col + i * GC)
                            load_group(first + HS_PER_GROUP, 2 * i, w_in, 0, col + i * GC)
                        load_out(f"out{half}", w_out, half * KT, 1 if half else None)
                load_ple(l)
                load_mlp(l)
                load_simple(f"gate{l}", tiles(ple_w_gate[l]), 4)
            for c in range(4):
                sp.wait_ge(sem("out_staged"), c + 1)
                sp.dma_start(out[0].rearrange("(b q) n -> q b n", q=P)[:, :, c * GC:(c + 1) * GC],
                             (rbuf if c % 2 == 0 else ubuf)[:].rearrange("p a b -> p (a b)")
                             .rearrange("p (b n) -> p b n", b=TB)).then_inc(sem(f"out_done{c % 2}"), 16)
            for i in range(2):
                sp.wait_ge(sem(f"out_done{i}"), 32)

        @block.gpsimd
        def _(pool):
            own = Steps(pool, sem("pool_step"))
            for m in (ident, later, earlier, never):
                own.inc(pool.memset(m[:], 0.0))
            for m in (ones, upto):
                own.inc(pool.memset(m[:], 1.0))
            own.inc(pool.memset(eps[:], EPS))
            own.settle()
            def mask(m, op, sign, fill):
                pool.affine_select(out=m[:], in_=m[:], compare_op=op, fill=fill, base=0,
                                   pattern=[[-sign, P]], channel_multiplier=sign).then_inc(sem("masks"), 1)
            mask(ident, ALU.not_equal, 1, 1.0)
            mask(later, ALU.is_ge, -1, 1.0)
            mask(earlier, ALU.is_ge, 1, 1.0)
            mask(never, ALU.is_ge, -1, -1e38)
            mask(upto, ALU.is_ge, -1, 0.0)

            def square_group(src, ready, value, acc, first):
                pool.wait_ge(ready, value)
                own.settle()
                if first:
                    own.inc(pool.tensor_tensor(acc[:], src, src, ALU.mult))
                    return
                own.inc(pool.tensor_tensor(sq4[:], src, src, ALU.mult))
                own.settle()
                own.inc(pool.tensor_tensor(acc[:], acc[:], sq4[:], ALU.add))

            def fold(name, acc):
                own.settle()
                own.inc(pool.tensor_tensor(acc[:, 0:2, :], acc[:, 0:2, :], acc[:, 2:4, :], ALU.add))
                own.settle()
                pool.tensor_tensor(acc[:, 0, :], acc[:, 0, :], acc[:, 1, :], ALU.add).then_inc(
                    sem(f"{name}_sum"), 1)

            def square_h(name, before=None, ready=None, at=0):
                if before:
                    pool.wait_ge(sem(f"{before}_mean"), 1)
                for c in range(4):
                    square_group(h[:, 4 * c:4 * c + 4, :], ready or sem(f"{name}_h"), at + c + 1, acc4, c == 0)
                fold(name, acc4)

            def decays():
                for i, a in enumerate((ssm_dt_bias, ssm_a_log, ssm_d)):
                    if i == 0:
                        pool.wait_ge(sem("ssm_h"), 4)
                    pool.dma_start(head_p[:, i, :], a.broadcast_to([P, SH])).then_inc(sem("heads_in"), 16)
                pool.wait_ge(sem("decay_t"), 1)
                pool.dma_start(decay_rows, decay_t[:]).then_inc(sem("rows_out"), 16)
                pool.wait_ge(sem("rows_out"), 16)
                pool.wait_ge(sem("cb"), SG)
                for half in range(2):
                    with own.loop(4 * half, 4 * half + 4, 6) as g:
                        for b in range(2):
                            own.settle()
                            pool.dma_start(rb[:], decay_rows[bass.ds(8 * g + 4 * b, 4), :].unsqueeze(0)
                                           .broadcast_to([P, 4, T])).then_inc(sem("rb_in"), 16)
                            pool.wait_ge(sem("rb_in"), 32 * g + 16 * b + 16)
                            if b == 0:
                                pool.wait_ge(sem("mix_free"), g + 1)
                            for dst, src, o in ((0, 0, 0), (1, 1, 2), (2, 1, 1)):
                                own.inc(pool.tensor_tensor(
                                    mix[:, b, :, dst * P:(dst + 1) * P], rb[:, :, src * P:(src + 1) * P],
                                    offset[:, o, bass.ds(8 * g + 4 * b, 4)].unsqueeze(2).broadcast_to([P, 4, P]),
                                    ALU.add))
                            own.settle()
                            diagonal = mix[:, b].rearrange("p h (c n) -> p h c n", c=3)[:, :, 0:3:2, :]
                            pool.tensor_tensor(diagonal, diagonal,
                                               never[:].unsqueeze(1).unsqueeze(1).broadcast_to([P, 4, 2, P]),
                                               ALU.add).then_inc(sem("exponents"), 1)

            square_h("attn")
            pool.wait_ge(sem("head_eps"), 1)
            with pool.Fori(0, 8) as m:
                pool.wait_ge(sem("qk_squared"), m + 1)
                pool.tensor_tensor(sq[:], sq[:], head_eps[:].unsqueeze(1).broadcast_to([P, TG, T]),
                                   ALU.add).then_inc(sem("qk_squares"), 1)
            for hp in range(HEADS // 2):
                pool.wait_ge(sem("weights_raw"), hp + 1)
                a = qk[:, 2 * hp:2 * hp + 2].rearrange("p h a b -> p h (a b)")[:, :, 0:384].rearrange(
                    "p h (c n) -> p h c n", c=3)[:, :, 0:3:2, :]
                pool.tensor_tensor(a, a, earlier[:].unsqueeze(1).unsqueeze(1).broadcast_to([P, 2, 2, P]),
                                   ALU.mult).then_inc(sem("weights_masked"), 1)
            for l in range(layers):
                if l == 1:
                    square_h("ssm", before="gate0")
                    decays()
                m = st[f"mlp{l}"].group
                square_h(f"mlp{l}", "attn" if l == 0 else "ssm", group_read, m - 8)
                for c in range(4):
                    square_group(e[:, 4 * c:4 * c + 4, :], group_read, m - 4 + c + 1, acc_e, c == 0)
                fold(f"e{l}", acc_e)
                square_h(f"gate{l}", f"mlp{l}", group_read, m + 28)

        @block.scalar
        def _(act):
            own = Steps(act, sem("act_step"))

            def cut(slot, r=0):
                if slot >= n_slots:
                    return
                act.wait_ge(landed[slot % RAW], 16 * (slot // RAW + 1) + 16 * r)
                if slot >= CUT:
                    act.wait_ge(slot_used, slot - CUT + 1 + RAW * r)
                act.activation(w_hi[slot % CUT][:], raw[slot % RAW][:], ACT.Copy).then_inc(hi_made, 1)

            def cuts(slot, r=0, js=range(HS_PER_GROUP)):
                for j in js:
                    cut(slot + AHEAD + j, r)

            def x_hi(name, c, dst, ready, value):
                col = norm_col[name]
                act.wait_ge(ready, value)
                for n in range(TG):
                    k = 4 * c + n
                    ins = act.activation(dst[:, bass.ds(k, 1), 0, :], h[:, bass.ds(k, 1), :], ACT.Copy,
                                         scale=gain(col + k))
                ins.then_inc(sem(f"{name}_hi"), 1)

            def norm_root(name, tok=False):
                act.wait_ge(sem(f"{name}_mean"), 1)
                ins = act.activation(rstd[:], aux[1][:, 0:T], ACT.Sqrt, bias=eps[:, 0:1], scale=1.0 / D)
                if tok:
                    ins = act.activation(rstd_tok[:], aux[1][:, GC:GC + TB], ACT.Sqrt, bias=eps[:, 0:1],
                                         scale=1.0 / D)
                ins.then_inc(sem(f"{name}_root"), 1)

            act.wait_ge(sem("masks"), 5)
            act.wait_ge(sem("gain_kept"), 1)
            for c in range(4):
                if c != 2:
                    first = (0, 2, None, 4)[c]
                    cut(first)
                    cut(first + 1)
                x_hi("attn", c, xa, sem("attn_h"), c + 1)

            def square_heads(m, par, done, r):
                act.wait_ge(slot_used, done + RAW * r)
                act.activation(sq[:], gp[par][:].rearrange("p (a b) -> p a b", a=TG),
                               ACT.Square).then_inc(sem("qk_squared"), 1)

            def root_heads(m, pair=0):
                act.wait_ge(sem("qk_mean"), m + 1)
                if not isinstance(m, int) or m:
                    act.wait_ge(group_read, m)
                act.activation(nrm[:], aux[pair][:], ACT.Sqrt, scale=1.0 / HD).then_inc(sem("qk_rooted"), 1)

            q = st["qk"]
            cuts(q.slot, js=range(2, 7))
            norm_root("attn", tok=True)
            act.wait_ge(sem("attn_root"), 1)
            act.activation(head_eps[:], rstd[:], ACT.Square, scale=EPS ** 0.5).then_inc(sem("head_eps"), 1)
            cuts(q.slot, js=range(7, 8))
            square_heads(0, 0, q.slot + 8, 0)
            cuts(q.slot + 8, js=range(0, 2))
            root_heads(0)
            cuts(q.slot + 8, js=range(2, 8))
            square_heads(1, 1, q.slot + 16, 0)
            with act.Fori(1, 4) as c:
                for m in range(2):
                    cuts(q.slot + 8 * m, 2 * c, range(0, 2))
                    root_heads(2 * c + m - 1)
                    cuts(q.slot + 8 * m, 2 * c, range(2, 8))
                    square_heads(2 * c + m, m, q.slot + 8 * m + 8, 2 * c)
            def pair_of(m):
                return m[:].rearrange("p (b n) -> p b n", b=2)[:, :, 0:384]

            def soft_pair(hp):
                act.wait_ge(sem("z"), hp + 1)
                own.inc(act.activation(ell[:], pair_of(aux[0]), ACT.Abs))
                own.settle()
                own.inc(act.activation(ell[:], ell[:], ACT.Exp, scale=-1.0))
                own.settle()
                act.activation(ell[:], ell[:], ACT.Ln, bias=1.0).then_inc(sem("ell"), 1)

            def weigh_pair(hp):
                act.wait_ge(sem("log_weights"), hp + 1)
                act.activation(qk[:, 2 * hp:2 * hp + 2].rearrange("p h a b -> p h (a b)")[:, :, 0:384], logb[:],
                               ACT.Exp).then_inc(sem("weights_raw"), 1)

            for g in range(4):
                for i in range(2):
                    if 2 * g + i:
                        weigh_pair(2 * g + i - 1)
                    soft_pair(2 * g + i)
                    cuts(st["v"].slot + 8 * g, js=range(4 * i, 4 * i + 2))
                    if g == i == 0:
                        root_heads(7, pair=1)
                    cuts(st["v"].slot + 8 * g, js=range(4 * i + 2, 4 * i + 4))
            weigh_pair(HEADS // 2 - 1)

            def o_hi(q):
                act.wait_ge(sem("o"), q + 1)
                act.activation(xb[:, 4 * q:4 * q + 4, 0, :], aux[q % 2][:].rearrange("p (a b) -> p a b", a=4),
                               ACT.Copy).then_inc(sem("o_hi"), 1)

            o_hi(0)
            o_hi(1)

            def p_hi(l):
                act.wait_ge(sem(f"p_turned{l}"), 1)
                act.activation(p_t[:, :, 0, :], aux[0][:, 0:GC].rearrange("p (a b) -> p a b", a=2),
                               ACT.Copy).then_inc(sem(f"p_hi{l}"), 1)

            def keep_e(l, j):
                act.wait_ge(slot_used, st[f"ple{l}"].slot + j + 1)
                if j == 0:
                    act.wait_ge(group_read, st[f"ple{l}"].group)
                act.activation(e[:, 4 * j:4 * j + 4, :],
                               gp[(st[f"ple{l}"].group + j) % 2][:].rearrange("p (a b) -> p a b", a=TG),
                               ACT.Copy).then_inc(group_read, 1)

            def embed(l, x_next):
                s = st[f"ple{l}"]
                cuts(s.slot, js=range(1))
                keep_e(l, 0)
                x_hi(f"mlp{l}", 3, x_next, group_read, s.group)
                for j in range(1, 4):
                    cuts(s.slot + j, js=range(1))
                    keep_e(l, j)

            for c in range(4):
                for j in range(HS_PER_GROUP):
                    cuts(st["wo"].slot + 8 * c, js=range(j, j + 1))
                    if c == 0 and j in (1, 3):
                        o_hi(2 + j // 2)
                    if c == 3 and j == 4:
                        p_hi(0)
                if c < 3:
                    x_hi("mlp0", c, xa, group_read, st["wo"].group + c + 1)
            embed(0, xa)

            def mlp(l, x_next):
                s = st[f"mlp{l}"].slot
                ub = xb if l == 0 else xa

                def squares(c, f):
                    act.wait_ge(group_read, st[f"mlp{l}"].group + 8 * f + c + 1)
                    own.inc(act.activation(ubuf[:], rbuf[:], ACT.Square))
                    own.settle()
                    act.activation(ub[:, bass.ds(4 * c, 4), 0, :], ubuf[:], ACT.Copy).then_inc(
                        sem(f"u_hi{l}"), 1)

                def up_down(f, first=False, last=False):
                    if first:
                        cuts(s, js=range(0, 7))
                        norm_root(f"mlp{l}")
                        cuts(s, js=range(7, 8))
                        squares(0, 0)
                        cuts(s + 8, js=range(0, 7))
                        act.wait_ge(sem(f"e{l}_mean"), 1)
                        act.activation(rstd_e[:], aux[1][:, GC:GC + T], ACT.Sqrt, bias=eps[:, 0:1],
                                       scale=1.0 / D).then_inc(sem(f"e{l}_root"), 1)
                        cuts(s + 8, js=range(7, 8))
                        squares(1, 0)
                    with own.loop(2 * int(first), 4, 1) as c:
                        cuts(s, 8 * f + c)
                        squares(c, f)
                    with act.Fori(0, 4) as c:
                        cuts(s + 32, 8 * f + c)
                        if last:
                            x_hi(f"gate{l}", c, x_next, group_read, st[f"mlp{l}"].group + 28 + c + 1)

                up_down(0, first=True)
                with own.loop(1, 3, 4) as f:
                    up_down(f)
                up_down(3, last=True)

            def gate(l, x_next, next_name):
                s = st[f"gate{l}"].slot
                for c in range(4):
                    cuts(s + 8 * c, js=range(0 if c == 0 else 2, 6))
                    if c == 0:
                        norm_root(f"gate{l}")
                    cuts(s + 8 * c, js=range(6, 8))
                    act.wait_ge(group_read, st[f"gate{l}"].group + c + 1)
                    act.activation(sig[:], rbuf[:], ACT.Sigmoid).then_inc(sem(f"gate_open{l}"), 1)
                    cuts(s + 8 * c + 8, js=range(0, 1))
                    if x_next is not None:
                        x_hi(next_name, c, x_next, sem(f"{next_name}_h"), c + 1)
                    cuts(s + 8 * c + 8, js=range(1, 2))

            def silu_conv(q, dst, bias_col):
                act.wait_ge(sem("conv"), q + 1)
                for n in range(TG):
                    ins = act.activation(dst(n), xc[:, n * T:(n + 1) * T], ACT.Silu,
                                         bias=misc[:, bass.ds(bias_col + n, 1)])
                ins.then_inc(sem("conv_silu"), 1)

            def y_square(g):
                act.wait_ge(sem("gated"), g + 1)
                for b in range(TB):
                    own.inc(act.activation(sq4[:].rearrange("p a b -> p (a b)")[:, b * GC:(b + 1) * GC],
                                              zg[:, b * GC:(b + 1) * GC], ACT.Square,
                                              accum_out=y_rms[:, b:b + 1]))
                own.settle()
                act.activation(y_rms[:], y_rms[:], ACT.Sqrt, bias=eps[:, 0:1],
                               scale=1.0 / GC).then_inc(sem("y_root"), 1)

            def y_hi(g, half):
                act.wait_ge(sem("y_turned"), g + 1)
                for n in range(TG):
                    ins = act.activation(xa[:, bass.ds(4 * g - KT * half + n, 1), 0, :],
                                         aux[0][:, n * T:(n + 1) * T], ACT.Copy,
                                         scale=misc[:, bass.ds(OUT_COL + 4 * g + n, 1)])
                ins.then_inc(sem("y_hi"), 1)

            def decay(g, b):
                act.wait_ge(sem("exponents"), 2 * g + b + 1)
                act.activation(mix[:, b], mix[:, b], ACT.Exp).then_inc(sem("decayed"), 1)

            def ssm_pair(half, g, i, first):
                s, r = st[f"xz{half}"].slot, 2 * i
                cuts(s, r, range(0, 2))
                if not first:
                    y_square(g - 1)
                cuts(s, r, range(2, 4))
                if first and half == 0:
                    silu_conv(3, lambda n: ct[:, 4 + n, :], 44)
                cuts(s, r, range(4, 5))
                if not first:
                    y_hi(g - 1, half)
                cuts(s, r, range(5, 8))
                if not first:
                    decay(g, 0)
                cuts(s + 8, r, range(0, 1))
                if not first:
                    decay(g, 1)
                cuts(s + 8, r, range(1, 4))
                silu_conv(4 + g, lambda n: xc[:, n * T:(n + 1) * T], 4 * g)
                cuts(s + 8, r, range(4, 5))
                if first:
                    decay(g, 0)
                cuts(s + 8, r, range(5, 7))
                if first:
                    decay(g, 1)
                cuts(s + 8, r, range(7, 8))
                act.wait_ge(slot_used, s + 16 + RAW * r)
                for b in range(TB):
                    ins = act.activation(zg[:, b * GC:(b + 1) * GC],
                                         gp[(st[f"xz{half}"].group + 1) % 2][:, b * GC:(b + 1) * GC],
                                         ACT.Silu, scale=rstd_tok[:, b:b + 1])
                ins.then_inc(sem("z_silu"), 1)

            def ssm():
                s = st["bc0"].slot
                cuts(s, js=range(2, 6))
                norm_root("ssm", tok=True)
                cuts(s, js=range(6, 8))
                silu_conv(0, lambda n: bt[:, n, :], 32)
                cuts(st["dt"].slot, js=range(1))
                s = st["bc"].slot
                act.wait_ge(sem("dt_raw"), 1)
                own.inc(act.activation(dt_ell[:], dt[:], ACT.Abs))
                own.settle()
                own.inc(act.activation(dt_ell[:], dt_ell[:], ACT.Exp, scale=-1.0))
                own.inc(act.activation(head_p[:, 1, :], head_p[:, 1, :], ACT.Exp))
                own.settle()
                act.activation(dt_ell[:], dt_ell[:], ACT.Ln, bias=1.0).then_inc(sem("dt_ell"), 1)
                cuts(s, js=range(0, 8))
                for q in range(1, 3):
                    cuts(s + 8 * q, js=range(0, 4))
                    silu_conv(q, lambda n: (bt if q < 2 else ct)[:, 4 * (q % 2) + n, :], 32 + 4 * q)
                    cuts(s + 8 * q, js=range(4, 8))
                for half in range(2):
                    ssm_pair(half, 4 * half, 0, True)
                    with own.loop(1, 4, 2) as i:
                        ssm_pair(half, 4 * half + i, i, False)
                    s = st[f"out{half}"]
                    for c in range(4):
                        cuts(s.slot + 8 * c, js=range(0, 2))
                        if c == 0:
                            y_square(4 * half + 3)
                        cuts(s.slot + 8 * c, js=range(2, 5))
                        if c == 0:
                            y_hi(4 * half + 3, half)
                        if half == 1 and c == 3:
                            p_hi(1)
                        cuts(s.slot + 8 * c, js=range(5, 8))
                        if half == 1 and c < 3:
                            x_hi("mlp1", c, xb, group_read, s.group + c + 1)
                embed(1, xb)

            mlp(0, xa)
            gate(0, xb if layers > 1 else None, "ssm")
            if layers > 1:
                ssm()
                mlp(1, xb)
                gate(1, None, "final")

        @block.vector
        def _(dve):
            own = Steps(dve, sem("dve_step"))

            def cut(slot, r=0):
                if slot >= n_slots:
                    return
                dve.wait_ge(hi_made, slot + 1 + RAW * r)
                dve.tensor_tensor(w_lo[slot % CUT][:], raw[slot % RAW][:], w_hi[slot % CUT][:].bitcast(F32),
                                  ALU.subtract).then_inc(lo_made, 1)

            def cuts(slot, r=0, js=range(HS_PER_GROUP)):
                for j in js:
                    cut(slot + AHEAD + j, r)

            def x_lo(name, c, dst):
                col = norm_col[name]
                dve.wait_ge(sem(f"{name}_hi"), c + 1)
                for n in range(TG):
                    k = 4 * c + n
                    ins = dve.scalar_tensor_tensor(
                        dst[:, bass.ds(k, 1), 1, :], h[:, bass.ds(k, 1), :], gain(col + k),
                        dst[:, bass.ds(k, 1), 0, :].bitcast(F32), ALU.mult, ALU.subtract)
                ins.then_inc(sem(f"{name}_lo"), 1)

            def read_group(s, done, r=0):
                dve.wait_ge(slot_used, done + RAW * r)

            def residual(s, done, r, c, par, name=None, dst=None):
                read_group(s, done, r)
                hc = h[:, bass.ds(4 * c, 4), :]
                dve.tensor_tensor(hc, hc, gp[par][:].rearrange("p (a b) -> p a b", a=TG),
                                  ALU.add).then_inc(group_read, 1)
                if name:
                    x_lo(name, c, dst)

            def norm_recip(name, tok=False):
                dve.wait_ge(sem(f"{name}_root"), 1)
                own.inc(dve.reciprocal(rstd[:], rstd[:]))
                if tok:
                    own.inc(dve.reciprocal(rstd_tok[:], rstd_tok[:]))
                own.settle()

            rstd4 = rstd[:].unsqueeze(1).broadcast_to([P, TG, T])

            dve.wait_ge(sem("gain_turned"), 1)
            dve.tensor_copy(gains[:, G_ATTN:G_ATTN + KT], aux[1][:, 0:KT]).then_inc(sem("gain_kept"), 1)

            def keep_rows():
                dve.wait_ge(sem("rows_turned"), 1)
                for i, (dst, n, at) in enumerate(((gains, N_GAIN - KT, 0), (conv_w, P, 0),
                                                  (conv_w, N_CONV - P, P),
                                                  (misc, N_CB + 2 + INNER // P, 0))):
                    ins = dve.tensor_copy(dst[:, at:at + n], aux[1][:, 128 * i:128 * i + n])
                own.inc(ins)
                own.settle()
                dve.tensor_scalar(qscale[:], misc[:, Q_COL:Q_COL + 1], float(HD) ** -0.5, None,
                                  ALU.mult).then_inc(sem("params"), 1)

            def keep_x(c):
                dve.wait_ge(sem("x_turned"), c + 1)
                dve.tensor_copy(h[:, 4 * c:4 * c + 4, :],
                                (gp[1], aux[0], aux[1])[c % 3][:].rearrange("p (a b) -> p a b", a=TG)).then_inc(
                                    sem("attn_h"), 1)

            keep_x(0)
            for c in range(4):
                if c < 3:
                    keep_x(c + 1)
                if c != 2:
                    first = (0, 2, None, 4)[c]
                    cut(first)
                    cut(first + 1)
                x_lo("attn", c, xa)
            keep_rows()

            q = st["qk"]

            def norm_head(n, par, k, which):
                g = qscale[:, 0:1] if which == 0 else misc[:, K_COL:K_COL + 1]
                own.inc(dve.reciprocal(nrm[:, n, :], nrm[:, n, :]))
                own.settle()
                return dve.scalar_tensor_tensor(qk[:, bass.ds(k, 1), which, :], gp[par][:, n * T:(n + 1) * T],
                                                g, nrm[:, n, :], ALU.mult, ALU.mult)

            def norm_heads(m, par, c, which, slot, r):
                cuts(slot, r, range(0, 2))
                dve.wait_ge(sem("qk_rooted"), m + 1)
                for n in range(TG):
                    ins = norm_head(n, par, 4 * c + n, which)
                    if n == TG - 1:
                        ins.then_inc(group_read, 1)
                    cuts(slot, r, range(2 + n, 3 + n))
                cuts(slot, r, range(6, 8))

            cuts(q.slot, js=range(2, 8))
            dve.wait_ge(sem("attn_root"), 1)
            own.inc(dve.reciprocal(rstd_tok[:], rstd_tok[:]))
            own.settle()
            norm_heads(0, 0, 0, 0, q.slot + 8, 0)
            with own.loop(1, 4, 8) as c:
                norm_heads(2 * c - 1, 1, c - 1, 1, q.slot, 2 * c)
                norm_heads(2 * c, 0, c, 0, q.slot + 8, 2 * c)

            def pair_of(m):
                return m[:].rearrange("p (b n) -> p b n", b=2)[:, :, 0:384]

            def soft_pair(hp):
                z = pair_of(aux[0])
                dve.wait_ge(sem("ell"), hp + 1)
                own.inc(dve.scalar_tensor_tensor(soft[:], z, 0.0, ell[:], ALU.max, ALU.add))
                own.inc(dve.scalar_tensor_tensor(logb[:], z, 0.0, ell[:], ALU.min, ALU.subtract))
                own.settle()
                d = soft[:].rearrange("p b (c n) -> p b c n", c=3)[:, :, 0:3:2, :]
                dve.tensor_tensor(d, d, earlier[:].unsqueeze(1).unsqueeze(1).broadcast_to([P, 2, 2, P]),
                                  ALU.mult).then_inc(sem("soft"), 1)

            def log_pair(hp):
                dve.wait_ge(sem("suffix"), hp + 1)
                dve.tensor_tensor(logb[:], logb[:], pair_of(aux[1]), ALU.subtract).then_inc(
                    sem("log_weights"), 1)

            v = st["v"]
            for g in range(4):
                for i in range(2):
                    soft_pair(2 * g + i)
                    for j in range(4):
                        cuts(v.slot + 8 * g, js=range(4 * i + j, 4 * i + j + 1))
                        if j == 2:
                            log_pair(2 * g + i)
                        if g == 0 and 1 <= 4 * i + j <= TG:
                            n = 4 * i + j - 1
                            dve.wait_ge(sem("qk_rooted"), 8)
                            ins = norm_head(n, 1, 12 + n, 1)
                            if n == TG - 1:
                                ins.then_inc(group_read, 1)
                read_group(v, v.slot + 8, g)
                for b in range(TB):
                    ins = dve.tensor_scalar(v_tok[:, 4 * g:4 * g + 4, b, :],
                                            gp[(v.group + g) % 2][:, b * GC:(b + 1) * GC].rearrange(
                                                "p (a d) -> p a d", a=4),
                                            rstd_tok[:, b:b + 1], None, ALU.mult)
                ins.then_inc(group_read, 1)

            def o_lo(q):
                dve.wait_ge(sem("o_hi"), q + 1)
                dve.tensor_tensor(xb[:, 4 * q:4 * q + 4, 1, :], aux[q % 2][:].rearrange("p (a b) -> p a b", a=4),
                                  xb[:, 4 * q:4 * q + 4, 0, :].bitcast(F32), ALU.subtract).then_inc(
                                      sem("o_lo"), 1)

            o_lo(0)
            o_lo(1)

            def p_lo(l):
                dve.wait_ge(sem(f"p_hi{l}"), 1)
                dve.tensor_tensor(p_t[:, :, 1, :], aux[0][:, 0:GC].rearrange("p (a b) -> p a b", a=2),
                                  p_t[:, :, 0, :].bitcast(F32), ALU.subtract).then_inc(sem(f"p_lo{l}"), 1)

            s = st["wo"]
            for c in range(4):
                for j in range(HS_PER_GROUP):
                    cuts(s.slot + 8 * c, js=range(j, j + 1))
                    if c == 0 and j in (1, 3):
                        o_lo(2 + j // 2)
                    if c == 3 and j == 4:
                        p_lo(0)
                residual(s, s.slot + 8 * c + 8, 0, c, (s.group + c) % 2, "mlp0", xa)
            cuts(st["ple0"].slot, js=range(4))

            def mlp(l, x_next):
                s = st[f"mlp{l}"]
                ub = xb if l == 0 else xa
                g0 = s.group % 2

                def relu(c, f, par):
                    read_group(s, s.slot + 8, 8 * f + c)
                    dve.scalar_tensor_tensor(rbuf[:], gp[par][:].rearrange("p (a b) -> p a b", a=TG), 0.0,
                                             rstd4, ALU.max, ALU.mult).then_inc(group_read, 1)
                    dve.wait_ge(sem(f"u_hi{l}"), 4 * f + c + 1)
                    dve.tensor_tensor(ub[:, bass.ds(4 * c, 4), 1, :], ubuf[:],
                                      ub[:, bass.ds(4 * c, 4), 0, :].bitcast(F32),
                                      ALU.subtract).then_inc(sem(f"u_lo{l}"), 1)

                def up_down(f, first=False, last=False):
                    if first:
                        cuts(s.slot, js=range(0, 7))
                        norm_recip(f"mlp{l}")
                        cuts(s.slot, js=range(7, 8))
                        dve.wait_ge(group_read, s.group)
                        relu(0, 0, g0)
                        cuts(s.slot + 8, js=range(0, 7))
                        dve.wait_ge(sem(f"e{l}_root"), 1)
                        own.inc(dve.reciprocal(rstd_e[:], rstd_e[:]))
                        own.settle()
                        cuts(s.slot + 8, js=range(7, 8))
                        relu(1, 0, (g0 + 1) % 2)
                        for b in range(2):
                            for j in range(HS_PER_GROUP):
                                cuts(s.slot + 16 + 8 * b, js=range(j, j + 1))
                                if j % 4 == 2:
                                    for k in range(8 * b + 4 * (j // 4), 8 * b + 4 * (j // 4) + 4):
                                        ins = dve.scalar_tensor_tensor(e[:, k, :], e[:, k, :],
                                                                       gain(G_PLE + KT * l + k), rstd_e[:],
                                                                       ALU.mult, ALU.mult)
                                    own.inc(ins)
                            relu(2 + b, 0, (g0 + b) % 2)
                    else:
                        with dve.Fori(0, 2) as c2:
                            for b in range(2):
                                cuts(s.slot + 8 * b, 8 * f + 2 * c2)
                                relu(2 * c2 + b, f, (g0 + b) % 2)
                    with dve.Fori(0, 2) as c2:
                        for b in range(2):
                            cuts(s.slot + 32 + 8 * b, 8 * f + 2 * c2)
                            residual(s, s.slot + 40 + 8 * b, 8 * f + 2 * c2, 2 * c2 + b, (g0 + b) % 2,
                                     *((f"gate{l}", x_next) if last else ()))

                up_down(0, first=True)
                with dve.Fori(1, 3) as f:
                    up_down(f)
                up_down(3, last=True)

            def gate(l, x_next, next_name):
                s = st[f"gate{l}"]
                for c in range(4):
                    cuts(s.slot + 8 * c, js=range(0 if c == 0 else 2, 7))
                    if c == 0:
                        norm_recip(f"gate{l}")
                    cuts(s.slot + 8 * c, js=range(7, 8))
                    read_group(s, s.slot + 8, c)
                    dve.tensor_tensor(rbuf[:], gp[(s.group + c) % 2][:].rearrange("p (a b) -> p a b", a=TG),
                                      rstd4, ALU.mult).then_inc(group_read, 1)
                    cuts(s.slot + 8 * c + 8, js=range(0, 1))
                    dve.wait_ge(sem(f"gate_open{l}"), c + 1)
                    own.settle()
                    own.inc(dve.tensor_tensor(sig[:], sig[:], e[:, 4 * c:4 * c + 4, :], ALU.mult))
                    own.settle()
                    hc = h[:, 4 * c:4 * c + 4, :]
                    dve.tensor_tensor(hc, hc, sig[:], ALU.add).then_inc(sem(f"{next_name}_h"), 1)
                    cuts(s.slot + 8 * c + 8, js=range(1, 2))
                    if x_next is not None:
                        x_lo(next_name, c, x_next)

            def conv_open(q, s, done, r, par):
                read_group(s, done, r)
                if not isinstance(q, int) or q >= 1:
                    dve.wait_ge(sem("conv_silu"), q)
                own.inc(dve.tensor_tensor(xr[:, :, KC - 1:], gp[par][:].rearrange("p (a b) -> p a b", a=TG),
                                          rstd4, ALU.mult))
                own.settle()
                dve.sem_inc(group_read, 1)

            def conv_tap(tap, col):
                for n in range(TG):
                    w = conv_w[:, bass.ds(tap * CONV_TILES + col + n, 1)]
                    o = xc[:, n * T:(n + 1) * T]
                    if tap == 0:
                        ins = dve.tensor_scalar(o, xr[:, n, 0:T], w, None, ALU.mult)
                    else:
                        ins = dve.scalar_tensor_tensor(o, xr[:, n, tap:tap + T], w, o, ALU.mult, ALU.add)
                if tap < KC - 1:
                    own.inc(ins)
                    own.settle()
                else:
                    ins.then_inc(sem("conv"), 1)

            def conv_taps(slot, r, col):
                conv_tap(0, col)
                for tap in range(1, KC):
                    conv_tap(tap, col)
                    cuts(slot, r, range(tap - 1, tap))
                cuts(slot, r, range(KC - 1, KC))

            def dt_open():
                s = st["dt"]
                read_group(s, s.slot + 1)
                dve.wait_ge(sem("heads_in"), 48)
                for b in range(TB):
                    ins = dve.scalar_tensor_tensor(dt[:, b, :], gp[s.group % 2][:, b * GC:b * GC + SH],
                                                   rstd_tok[:, b:b + 1], head_p[:, 0, :], ALU.mult, ALU.add)
                own.inc(ins)
                own.settle()
                dve.sem_inc(group_read, 1)
                dve.sem_inc(sem("dt_raw"), 1)

            def dt_steps():
                dve.wait_ge(sem("dt_ell"), 1)
                own.inc(dve.scalar_tensor_tensor(dt[:], dt[:], 0.0, dt_ell[:], ALU.max, ALU.add))
                own.settle()
                dve.scalar_tensor_tensor(dt_a[:], dt[:], -1.0, head_p[:, 1, :].unsqueeze(1).broadcast_to([P, TB, SH]),
                                         ALU.mult, ALU.mult).then_inc(sem("dt_a"), 1)

            def dt_offsets():
                dve.wait_ge(sem("cumulated"), 1)
                dve.tensor_copy(decay_t[:], aux[1][0:SH, 0:T]).then_inc(sem("decay_t"), 1)
                dve.tensor_scalar(offset[:, 0:2, :], aux[1][:, GC:GC + 2 * SH].rearrange("p (b h) -> p b h", b=2),
                                  -1.0, None, ALU.mult)
                dve.tensor_copy(offset[:, 2, :], aux[1][:, GC + 2 * SH:GC + 3 * SH]).then_inc(sem("offset"), 1)

            def keep_cb(g):
                dve.wait_ge(sem("cb_raw"), g + 1)
                dve.tensor_copy(cb[:, g, :], aux[0][:, (g % 2) * GC:(g % 2) * GC + 384]).then_inc(sem("cb"), 1)

            def mix_heads(g, b):
                dve.wait_ge(sem("decayed"), 2 * g + b + 1)
                dve.tensor_tensor(mix[:, b], mix[:, b], cb[:, bass.ds(g, 1), :].broadcast_to([P, 4, 384]),
                                  ALU.mult).then_inc(sem("mixed"), 1)

            def y_gate(g):
                dve.wait_ge(sem("y"), g + 1)
                own.inc(dve.tensor_tensor(x_skip[:], x_skip[:], aux[1][:], ALU.add))
                dve.wait_ge(sem("z_silu"), g + 1)
                dve.sem_inc(group_read, 1)
                own.settle()
                dve.tensor_tensor(zg[:], zg[:], x_skip[:], ALU.mult).then_inc(sem("gated"), 1)

            def y_scale(g):
                dve.wait_ge(sem("y_root"), g + 1)
                own.inc(dve.reciprocal(y_rms[:], y_rms[:]))
                own.settle()
                for b in range(TB):
                    ins = dve.tensor_scalar(zg[:, b * GC:(b + 1) * GC], zg[:, b * GC:(b + 1) * GC],
                                            y_rms[:, b:b + 1], None, ALU.mult)
                ins.then_inc(sem("y_scaled"), 1)

            def y_lo(g, half):
                dve.wait_ge(sem("y_hi"), g + 1)
                for n in range(TG):
                    k = bass.ds(4 * g - KT * half + n, 1)
                    ins = dve.scalar_tensor_tensor(xa[:, k, 1, :], aux[0][:, n * T:(n + 1) * T],
                                                   misc[:, bass.ds(OUT_COL + 4 * g + n, 1)],
                                                   xa[:, k, 0, :].bitcast(F32), ALU.mult, ALU.subtract)
                ins.then_inc(sem("y_lo"), 1)

            def spread_x(g):
                dve.wait_ge(sem("x_tok"), g + 1)
                for b in range(TB):
                    src = aux[0][:, b * GC:(b + 1) * GC].rearrange("p (h d) -> p h d", h=8)
                    for dst, w in ((x_skip, head_p[:, 2, bass.ds(8 * g, 8)]), (xc, dt[:, b, bass.ds(8 * g, 8)])):
                        ins = dve.tensor_tensor(dst[:, b * GC:(b + 1) * GC].rearrange("p (h d) -> p h d", h=8), src,
                                                w.unsqueeze(2).broadcast_to([P, 8, SHD]), ALU.mult)
                ins.then_inc(sem("x_dt"), 1)

            def ssm_pair(half, g, i, first):
                sx = st[f"xz{half}"]
                s, r = sx.slot, 2 * i
                if first and half == 0:
                    conv_taps(s, r, 44)
                    cuts(s, r, range(4, 5))
                else:
                    cuts(s, r, range(0, 2))
                    if not first:
                        y_gate(g - 1)
                    cuts(s, r, range(2, 3))
                    if not first:
                        y_scale(g - 1)
                    cuts(s, r, range(3, 5))
                if not first:
                    y_lo(g - 1, half)
                if first and half == 0:
                    for j in range(4):
                        keep_cb(2 * j)
                        keep_cb(2 * j + 1)
                        if j < 3:
                            cuts(s, r, range(5 + j, 6 + j))
                else:
                    cuts(s, r, range(5, 8))
                conv_open(4 + g, sx, s + 8, r, sx.group % 2)
                conv_taps(s + 8, r, 4 * g)
                cuts(s + 8, r, range(4, 5))
                mix_heads(g, 0)
                cuts(s + 8, r, range(5, 7))
                mix_heads(g, 1)
                cuts(s + 8, r, range(7, 8))
                spread_x(g)

            def ssm():
                own.inc(dve.memset(xr[:, :, 0:KC - 1], 0.0))
                s = st["bc0"]
                cuts(s.slot, js=range(2, 6))
                norm_recip("ssm", tok=True)
                cuts(s.slot, js=range(6, 8))
                conv_open(0, s, s.slot + 8, 0, s.group % 2)
                for tap in range(KC):
                    conv_tap(tap, 32)
                cuts(st["dt"].slot, js=range(1))
                s = st["bc"]
                dt_open()
                cuts(s.slot, js=range(0, 1))
                dt_steps()
                cuts(s.slot, js=range(1, 4))
                dt_offsets()
                cuts(s.slot, js=range(4, 8))
                for q in range(3):
                    conv_open(q + 1, s, s.slot + 8 * q + 8, 0, (s.group + q) % 2)
                    if q < 2:
                        conv_taps(s.slot + 8 * q + 8, 0, 36 + 4 * q)
                        cuts(s.slot + 8 * q + 8, js=range(4, 8))
                for half in range(2):
                    ssm_pair(half, 4 * half, 0, True)
                    with own.loop(1, 4, 6) as i:
                        ssm_pair(half, 4 * half + i, i, False)
                    s = st[f"out{half}"]
                    for c in range(4):
                        cuts(s.slot + 8 * c, js=range(0, 2))
                        if c == 0:
                            y_gate(4 * half + 3)
                        cuts(s.slot + 8 * c, js=range(2, 3))
                        if c == 0:
                            y_scale(4 * half + 3)
                        cuts(s.slot + 8 * c, js=range(3, 5))
                        if c == 0:
                            y_lo(4 * half + 3, half)
                        if half == 1 and c == 3:
                            p_lo(1)
                        cuts(s.slot + 8 * c, js=range(5, 8))
                        residual(s, s.slot + 8, c, c, (s.group + c) % 2, *(("mlp1", xb) if half else ()))
                cuts(st["ple1"].slot, js=range(4))

            mlp(0, xa)
            gate(0, xb if layers > 1 else None, "ssm" if layers > 1 else "final")
            if layers > 1:
                ssm()
                mlp(1, xb)
                gate(1, None, "final")
            for c in range(4):
                dve.wait_ge(sem("final_turned"), c + 1)
                if c >= 2:
                    dve.wait_ge(sem(f"out_done{c % 2}"), 16)
                dve.tensor_copy((rbuf if c % 2 == 0 else ubuf)[:].rearrange("p a b -> p (a b)"),
                                aux[c % 2][:]).then_inc(sem("out_staged"), 1)

        @block.tensor
        def _(pe):
            def open_group(group, par):
                if not isinstance(group, int) or group >= 2:
                    pe.wait_ge(group_read, group - 1)
                return gp[par]

            def products(pst, slot, r, xs, k0, first, last):
                pe.wait_ge(lo_made, slot + 1 + RAW * r)
                hi, lo = w_hi[slot % CUT], w_lo[slot % CUT]
                for n in range(TG):
                    for k in range(2):
                        cols = slice(n * P, (n + 1) * P)
                        for i, (w, part) in enumerate(((hi, 0), (hi, 1), (lo, 0))):
                            mm = pe.matmul(pst[:, n * T:(n + 1) * T], w[:, k, cols], xs[:, k0 + k, part, :],
                                           start=first and k == 0 and i == 0 and n % 2 == 0,
                                           stop=last and k == 1 and i == 2, skip_group_check=True)
                            if n == TG - 1 and k == 1 and i == 2:
                                mm.then_inc(slot_used, 1)

            def products_tok(pst, slot, r, xs, k0, first, last):
                pe.wait_ge(lo_made, slot + 1 + RAW * r)
                hi, lo = w_hi[slot % CUT], w_lo[slot % CUT]
                for b in range(TB):
                    for k in range(2):
                        for i, (w, part) in enumerate(((hi, 0), (hi, 1), (lo, 0))):
                            mm = pe.matmul(pst[:, b * GC:(b + 1) * GC], xs[:, k0 + k, part, b * P:(b + 1) * P],
                                           w[:, k, :], start=first and k == 0 and i == 0,
                                           stop=last and k == 1 and i == 2)
                            if b == TB - 1 and k == 1 and i == 2:
                                mm.then_inc(slot_used, 1)

            def half_slots(pst, slot, r, xs, js, x_ready=None, x_from=0, fn=products):
                for j in js:
                    if x_ready is not None and j % 2 == 0:
                        if j % 2 == 0:
                            pe.wait_ge(x_ready, x_from + (2 * j) // 4 + 1)
                    fn(pst, slot + j, r, xs, 2 * j, j == 0, j == HS_PER_GROUP - 1)

            def mean(name, tok=False):
                pe.wait_ge(sem(f"{name}_sum"), 1)
                mm = pe.matmul(aux[1][:, 0:T], ones[:], acc4[:, 0, :], start=True, stop=True)
                if tok:
                    for b in range(TB):
                        mm = pe.matmul(aux[1][:, GC + b:GC + b + 1], acc4[:, 0, b * P:(b + 1) * P], ones[:, 0:1],
                                       start=True, stop=True)
                mm.then_inc(sem(f"{name}_mean"), 1)

            pe.wait_ge(sem("masks"), 5)
            pe.wait_ge(sem("gain_in"), 16)
            pe.transpose(aux[1][:, 0:KT], rows4[0:KT, :], ident[0:KT, 0:KT]).then_inc(sem("gain_turned"), 1)

            def turn_rows():
                pe.wait_ge(sem("rows_in"), 16 * 10)
                pe.wait_ge(sem("attn_h"), 4)
                for i, (src, n) in enumerate(((rows0, N_GAIN - KT), (rows1, P), (rows2, N_CONV - P),
                                              (rows3, N_CB + 2 + INNER // P))):
                    tr = pe.transpose(aux[1][:, 128 * i:128 * i + n], src[0:n, :], ident[0:n, 0:n])
                tr.then_inc(sem("rows_turned"), 1)

            def turn_x_in(c):
                pe.wait_ge(sem(f"x_in{c}"), 16)
                if c == 2:
                    pe.wait_ge(sem("gain_kept"), 1)
                if c == 3:
                    pe.wait_ge(sem("attn_h"), 1)
                for n in range(TG):
                    for b in range(TB):
                        tr = pe.transpose((gp[1], aux[0], aux[1])[c % 3][:, n * T + b * P:n * T + (b + 1) * P],
                                          x_tok[:, b, (4 * c + n) * P:(4 * c + n + 1) * P], ident[:])
                tr.then_inc(sem("x_turned"), 1)

            q = st["qk"]

            def head_means(m, pair=0):
                pe.wait_ge(sem("qk_squares"), m + 1)
                for b in range(2):
                    mm = pe.matmul(aux[pair][:, b * GC:(b + 1) * GC], ones[:],
                                   sq[:, 2 * b:2 * b + 2, :], start=True, stop=True)
                mm.then_inc(sem("qk_mean"), 1)

            for c in range(4):
                turn_x_in(c)
            ps = open_group(0, 0)
            for c in range(4):
                if c == 2:
                    turn_rows()
                if c == 3:
                    pe.wait_ge(sem("params"), 1)
                    mean("attn", tok=True)
                half_slots(ps, q.slot, 0, xa, range(2 * c, 2 * c + 2), sem("attn_lo"))
            pe.wait_ge(sem("attn_h"), 4)
            ps = open_group(1, 1)
            half_slots(ps, q.slot + 8, 0, xa, range(0, 2))
            head_means(0)
            half_slots(ps, q.slot + 8, 0, xa, range(2, 8))
            with pe.Fori(1, 4) as c:
                for m in range(2):
                    ps = open_group(q.group + 2 * c + m, m)
                    half_slots(ps, q.slot + 8 * m, 2 * c, xa, range(0, 2))
                    head_means(2 * c + m - 1)
                    half_slots(ps, q.slot + 8 * m, 2 * c, xa, range(2, 8))

            def scores(hd):
                b = hd % 2
                z = aux[0][:, b * GC:b * GC + 384]
                pe.matmul(z[:, 0:T], qk[:, hd, 1, 0:P], qk[:, hd, 0, :], start=True, stop=True)
                return pe.matmul(z[:, T:T + P], qk[:, hd, 1, P:T], qk[:, hd, 0, P:T], start=True, stop=True)

            def score_pair(hp):
                pe.wait_ge(group_read, 8 if hp >= 6 else 7)
                if hp:
                    pe.wait_ge(sem("soft"), hp)
                scores(2 * hp)
                scores(2 * hp + 1).then_inc(sem("z"), 1)

            def suffix_pair(hp):
                pe.wait_ge(sem("soft"), hp + 1)
                if hp:
                    pe.wait_ge(sem("log_weights"), hp)
                for b in range(2):
                    u = aux[1][:, b * GC:b * GC + 384]
                    pe.matmul(u, later[:], soft[:, b, :], start=True, stop=False, skip_group_check=True)
                    mm = pe.matmul(u[:, P:T], ones[:], soft[:, b, T:T + P], start=False, stop=True,
                                   skip_group_check=True)
                mm.then_inc(sem("suffix"), 1)

            v = st["v"]
            for g in range(4):
                ps = open_group(v.group + g, (v.group + g) % 2)
                for i in range(2):
                    score_pair(2 * g + i)
                    half_slots(ps, v.slot + 8 * g, 0, xa, range(4 * i, 4 * i + 2), fn=products_tok)
                    if g == i == 0:
                        head_means(7, pair=1)
                    half_slots(ps, v.slot + 8 * g, 0, xa, range(4 * i + 2, 4 * i + 3), fn=products_tok)
                    if g == i == 0:
                        pe.wait_ge(sem("qk_rooted"), 8)
                    suffix_pair(2 * g + i)
                    half_slots(ps, v.slot + 8 * g, 0, xa, range(4 * i + 3, 4 * i + 4), fn=products_tok)

            def weigh_values(q):
                pe.wait_ge(group_read, v.group + q + 1)
                if q < 2:
                    pe.wait_ge(sem("log_weights" if q else "soft"), HEADS // 2)
                else:
                    pe.wait_ge(sem("o_lo"), q - 1)
                for n in range(4):
                    hd = 4 * q + n
                    pe.wait_ge(sem("weights_masked"), hd // 2 + 1)
                    o = aux[q % 2][:, n * T:(n + 1) * T]
                    a = qk[:, hd].rearrange("p a b -> p (a b)")
                    pe.matmul(o, v_tok[:, hd, 0, :], a[:, 0:T], start=n % 2 == 0, stop=False,
                              skip_group_check=True)
                    mm = pe.matmul(o[:, P:T], v_tok[:, hd, 1, :], a[:, T:T + P], start=False, stop=True,
                                   skip_group_check=True)
                mm.then_inc(sem("o"), 1)

            def turn_p(l):
                pe.wait_ge(sem(f"p_in{l}"), 16)
                for k in range(2):
                    for b in range(TB):
                        tr = pe.transpose(aux[0][:, k * T + b * P:k * T + (b + 1) * P],
                                          p_tok[:, b, k * P:(k + 1) * P], ident[:])
                tr.then_inc(sem(f"p_turned{l}"), 1)

            def embed(l):
                s = st[f"ple{l}"]
                pe.wait_ge(sem(f"p_lo{l}"), 1)
                for j in range(4):
                    ps = open_group(s.group + j, (s.group + j) % 2)
                    products(ps, s.slot + j, 0, p_t, 0, True, True)

            s = st["wo"]
            weigh_values(0)
            weigh_values(1)
            for c in range(4):
                ps = open_group(s.group + c, (s.group + c) % 2)
                if c == 0:
                    for i in range(4):
                        half_slots(ps, s.slot, 0, xb, range(2 * i, 2 * i + 2), sem("o_lo"))
                        if i < 2:
                            weigh_values(i + 2)
                else:
                    half_slots(ps, s.slot + 8 * c, 0, xb, range(0, 4))
                    if c == 3:
                        turn_p(0)
                    half_slots(ps, s.slot + 8 * c, 0, xb, range(4, 8))
            embed(0)

            def pair_loop(s, slot, group, xs, x_ready, x_step, n=2, r0=0, start=0, wait_from=0):
                with pe.Fori(start, n) as c2:
                    for b in range(2):
                        ps = open_group(group + 2 * c2 + b + r0, (s.group + b) % 2)
                        for j in range(HS_PER_GROUP):
                            if x_ready is not None and j % 2 == 0:
                                pe.wait_ge(x_ready, wait_from + x_step * (j // 2 + 1))
                            products(ps, slot + 8 * b + j, 2 * c2 + r0, xs, 2 * j, j == 0, j == 7)

            def mlp(l, xs, us):
                s = st[f"mlp{l}"]
                ps = open_group(s.group, s.group % 2)
                half_slots(ps, s.slot, 0, xs, range(0, 6), sem(f"mlp{l}_lo"))
                mean(f"mlp{l}")
                half_slots(ps, s.slot, 0, xs, range(6, 8), sem(f"mlp{l}_lo"))
                ps = open_group(s.group + 1, (s.group + 1) % 2)
                half_slots(ps, s.slot + 8, 0, xs, range(0, 6))
                pe.wait_ge(sem(f"e{l}_sum"), 1)
                pe.matmul(aux[1][:, GC:GC + T], ones[:], acc_e[:, 0, :], start=True,
                          stop=True).then_inc(sem(f"e{l}_mean"), 1)
                half_slots(ps, s.slot + 8, 0, xs, range(6, 8))
                pair_loop(s, s.slot, s.group, xs, None, 0, start=1)
                pair_loop(s, s.slot + 32, s.group + 4, us, sem(f"u_lo{l}"), 1)
                with pe.Fori(1, 4) as f:
                    pair_loop(s, s.slot, s.group, xs, None, 0, r0=8 * f)
                    pair_loop(s, s.slot + 32, s.group + 4, us, sem(f"u_lo{l}"), 1, r0=8 * f, wait_from=4 * f)

            def gate(l, xs):
                s = st[f"gate{l}"]
                for c in range(4):
                    ps = open_group(s.group + c, (s.group + c) % 2)
                    half_slots(ps, s.slot + 8 * c, 0, xs, range(0, 6), sem(f"gate{l}_lo"))
                    if c == 0:
                        mean(f"gate{l}")
                    half_slots(ps, s.slot + 8 * c, 0, xs, range(6, 8), sem(f"gate{l}_lo"))

            def cumulate():
                pe.wait_ge(sem("dt_a"), 1)
                for b in range(TB):
                    pe.matmul(aux[1][0:SH, b * P:(b + 1) * P], dt_a[:, b, :], upto[:], start=True, stop=True)
                for b in range(TB):
                    pe.matmul(aux[1][:, GC + b * SH:GC + (b + 1) * SH], upto[:], dt_a[:, b, :], start=True,
                              stop=True)
                pe.matmul(aux[1][:, GC + 2 * SH:GC + 3 * SH], later[:], dt_a[:, 0, :], start=True,
                          stop=True).then_inc(sem("cumulated"), 1)

            def cb_products(g):
                pe.wait_ge(sem("conv_silu"), 4)
                if g >= 2:
                    pe.wait_ge(sem("cb"), g - 1)
                o = aux[0][:, (g % 2) * GC:(g % 2) * GC + 384]
                pe.matmul(o[:, 0:T], bt[:, g, 0:P], ct[:, g, :], start=True, stop=True)
                pe.matmul(o[:, T:T + P], bt[:, g, P:T], ct[:, g, P:T], start=True,
                          stop=True).then_inc(sem("cb_raw"), 1)

            def turn_y(g):
                pe.wait_ge(sem("y_scaled"), g + 1)
                for n in range(TG):
                    for b in range(TB):
                        tr = pe.transpose(aux[0][:, n * T + b * P:n * T + (b + 1) * P],
                                          zg[:, b * GC + n * P:b * GC + (n + 1) * P], ident[:])
                tr.then_inc(sem("y_turned"), 1)

            def turn_x(g):
                pe.wait_ge(sem("conv_silu"), g + 5)
                if not isinstance(g, int) or g:
                    pe.wait_ge(sem("y_lo"), g)
                else:
                    pe.wait_ge(sem("cb"), SG)
                for n in range(TG):
                    for b in range(TB):
                        tr = pe.transpose(aux[0][:, b * GC + n * P:b * GC + (n + 1) * P],
                                          xc[:, n * T + b * P:n * T + (b + 1) * P], ident[:])
                tr.then_inc(sem("x_tok"), 1)

            def y_products(g):
                pe.wait_ge(sem("mixed"), 2 * g + 2)
                pe.wait_ge(sem("x_dt"), g + 1)
                for hd in range(8):
                    m = mix[:, hd // 4, hd % 4, :]
                    c = slice(hd * SHD, (hd + 1) * SHD)
                    x0, x1 = xc[:, 0:GC][:, c], xc[:, GC:2 * GC][:, c]
                    y0, y1 = aux[1][:, 0:GC][:, c], aux[1][:, GC:2 * GC][:, c]
                    pe.matmul(y0, m[:, 0:P], x0, start=True, stop=True)
                    pe.matmul(y1, m[:, P:T], x0, start=True, stop=False)
                    mm = pe.matmul(y1, m[:, T:T + P], x1, start=False, stop=True)
                mm.then_inc(sem("y"), 1)
                pe.wait_ge(sem("y"), g + 1)
                pe.sem_inc(sem("mix_free"), 1)

            def ssm_pair(half, g, i, first):
                sx = st[f"xz{half}"]
                s, r = sx.slot, 2 * i
                ps = open_group(sx.group + 2 * i, sx.group % 2)
                half_slots(ps, s, r, xb, range(0, 2))
                if not first:
                    y_products(g - 1)
                half_slots(ps, s, r, xb, range(2, 5))
                if first:
                    if half == 0:
                        for j in range(3):
                            cb_products(2 * j)
                            cb_products(2 * j + 1)
                            half_slots(ps, s, r, xb, range(5 + j, 6 + j))
                        cb_products(6)
                        cb_products(7)
                    else:
                        half_slots(ps, s, r, xb, range(5, 8))
                else:
                    turn_y(g - 1)
                    half_slots(ps, s, r, xb, range(5, 8))
                ps = open_group(sx.group + 2 * i + 1, (sx.group + 1) % 2)
                half_slots(ps, s + 8, r, xb, range(0, 6), fn=products_tok)
                turn_x(g)
                half_slots(ps, s + 8, r, xb, range(6, 8), fn=products_tok)

            def ssm():
                pe.sem_inc(sem("mix_free"), 1)
                s = st["bc0"]
                ps = open_group(s.group, s.group % 2)
                half_slots(ps, s.slot, 0, xb, range(0, 6), sem("ssm_lo"))
                mean("ssm", tok=True)
                half_slots(ps, s.slot, 0, xb, range(6, 8), sem("ssm_lo"))
                s = st["dt"]
                pe.wait_ge(lo_made, s.slot + 1)
                ps = open_group(s.group, s.group % 2)
                hi, lo = (w[s.slot % CUT][:].rearrange("p a b -> p (a b)").rearrange("p (k n) -> p k n", k=KT)
                          for w in (w_hi, w_lo))
                for b in range(TB):
                    for k in range(KT):
                        for i, (w, part) in enumerate(((hi, 0), (hi, 1), (lo, 0))):
                            mm = pe.matmul(ps[:, b * GC:b * GC + SH], xb[:, k, part, b * P:(b + 1) * P], w[:, k, :],
                                           start=k == 0 and i == 0, stop=k == KT - 1 and i == 2)
                mm.then_inc(slot_used, 1)
                s = st["bc"]
                for q in range(3):
                    ps = open_group(s.group + q, (s.group + q) % 2)
                    half_slots(ps, s.slot + 8 * q, 0, xb, range(0, 4))
                    if q == 0:
                        cumulate()
                    half_slots(ps, s.slot + 8 * q, 0, xb, range(4, 8))
                for half in range(2):
                    ssm_pair(half, 4 * half, 0, True)
                    with pe.Fori(1, 4) as i:
                        ssm_pair(half, 4 * half + i, i, False)
                    s = st[f"out{half}"]
                    for c in range(4):
                        ps = open_group(s.group + c, (s.group + c) % 2)
                        half_slots(ps, s.slot + 8 * c, 0, xa, range(0, 2), sem("y_lo"), 4 * half)
                        if c == 0:
                            y_products(4 * half + 3)
                        half_slots(ps, s.slot + 8 * c, 0, xa, range(2, 5), sem("y_lo"), 4 * half)
                        if half == 1 and c == 3:
                            turn_p(1)
                        if c == 0:
                            turn_y(4 * half + 3)
                        half_slots(ps, s.slot + 8 * c, 0, xa, range(5, 8), sem("y_lo"), 4 * half)
                embed(1)

            mlp(0, xa, xb)
            gate(0, xa)
            if layers > 1:
                ssm()
                mlp(1, xb, xa)
                gate(1, xb)
            for c in range(4):
                pe.wait_ge(sem("final_h"), c + 1)
                if c >= 2:
                    pe.wait_ge(sem("out_staged"), c - 1)
                for b in range(TB):
                    for n in range(TG):
                        tr = pe.transpose(aux[c % 2][:, b * GC + n * P:b * GC + (n + 1) * P],
                                          h[:, 4 * c + n, b * P:(b + 1) * P], ident[:])
                tr.then_inc(sem("final_turned"), 1)


_INS = ['x', 'p', 'attn_norm', 'attn_w_qkv', 'attn_q_norm', 'attn_k_norm', 'attn_w_o', 'ssm_norm',
        'ssm_w_in', 'ssm_conv_w', 'ssm_conv_b', 'ssm_dt_bias', 'ssm_a_log', 'ssm_d', 'ssm_out_norm',
        'ssm_w_out', 'mlp_norm', 'mlp_w_up', 'mlp_w_down', 'ple_w_proj', 'ple_norm', 'ple_gate_norm',
        'ple_w_gate']


def kernel(**inputs):
    import numpy as _np
    import concourse.bacc as _bacc
    from concourse import mybir as _mybir
    from concourse.bass_utils import run_bass_kernel_spmd as _run

    nc = _bacc.Bacc("TRN2", target_bir_lowering=False, num_devices=1)
    arrays, args = {}, {}
    for name in _INS:
        a = _np.ascontiguousarray(inputs[name])
        arrays[f"in_{name}"] = a
        args[name] = nc.dram_tensor(f"in_{name}", a.shape, _mybir.dt.from_np(a.dtype), kind="ExternalInput").ap()
    args["out"] = nc.dram_tensor("out_h", (1, T, D), F32, kind="ExternalOutput").ap()
    args["decay_rows"] = nc.dram_tensor("decay_rows", (SH, T), F32).ap()
    build_trunk(nc, 2, **args)
    r = _run(nc, [arrays], core_ids=[0])
    return r.results[0]["out_h"]
```

```python
from contextlib import ExitStack, contextmanager

import concourse.bass as bass
from concourse import mybir

F32 = mybir.dt.float32
F32R = mybir.dt.float32r
ALU = mybir.AluOpType
ACT = mybir.ActivationFunctionType

P = 128
D = 2048
T = 256
KT = D // P
TB = T // P
EPS = 1e-6
HEADS, HD = 16, 128
FF = 4 * D
PLE = 256
GC = 512
TG = GC // P
HS_PER_GROUP = KT // 2
RAW, CUT = 8, 4
AHEAD = CUT
INNER = 4096
SH, SHD, SG, SN = 64, 64, 8, 128
CONV_TILES = (INNER + 2 * SG * SN) // P
KC = 4


class Steps:

    def __init__(self, eng, sem):
        self.eng, self.sem, self.base, self.k = eng, sem, 0, 0

    def inc(self, ins):
        ins.then_inc(self.sem, 1)
        self.k += 1

    def settle(self):
        self.eng.wait_ge(self.sem, self.base + self.k)

    @contextmanager
    def loop(self, start, end, per):
        base, k = self.base, self.k
        with self.eng.Fori(start, end) as i:
            self.base, self.k = base + k + (i - start) * per, 0
            yield i
            assert self.k == per, (self.k, per)
        self.base, self.k = base, k + (end - start) * per


class Stage:

    def __init__(self, slot, group, groups, per_group):
        self.slot, self.group, self.groups, self.per_group = slot, group, groups, per_group


def plan(layers):
    st, at = {}, [0, 0]

    def add(name, groups, per_group=HS_PER_GROUP):
        st[name] = Stage(at[0], at[1], groups, per_group)
        at[0] += groups * per_group
        at[1] += groups

    for l in range(layers):
        if l == 0:
            add("qk", 8)
            add("v", 4)
            add("wo", 4)
        else:
            add("bc0", 1)
            add("dt", 1, 1)
            add("bc", 3)
            for half in range(2):
                add(f"xz{half}", SG)
                add(f"out{half}", 4)
        add(f"ple{l}", 4, 1)
        add(f"mlp{l}", 32)
        add(f"gate{l}", 4)
    return st, at[0]


def build_trunk(nc, layers, x, p, attn_norm, attn_w_qkv, attn_q_norm, attn_k_norm, attn_w_o,
                ssm_norm, ssm_w_in, ssm_conv_w, ssm_conv_b, ssm_dt_bias, ssm_a_log, ssm_d,
                ssm_out_norm, ssm_w_out, mlp_norm, mlp_w_up, mlp_w_down,
                ple_w_proj, ple_norm, ple_gate_norm, ple_w_gate, out, decay_rows):
    st, n_slots = plan(layers)
    with ExitStack() as ctx:
        def sb(name, shape, dt=F32):
            return ctx.enter_context(nc.sbuf_tensor(name, shape, dt))

        sems = {}

        def sem(name):
            if name not in sems:
                sems[name] = ctx.enter_context(nc.semaphore(name))
            return sems[name]

        raw = [sb(f"raw{i}", [P, 2, GC]) for i in range(RAW)]
        w_hi = [sb(f"w_hi{i}", [P, 2, GC], F32R) for i in range(CUT)]
        w_lo = [sb(f"w_lo{i}", [P, 2, GC], F32R) for i in range(CUT)]
        h = sb("h", [P, KT, T])
        xa = sb("xa", [P, KT, 2, T], F32R)
        ident = sb("ident", [P, P])
        ones = sb("ones", [P, P])
        later = sb("later", [P, P])
        earlier = sb("earlier", [P, P])
        upto = sb("upto", [P, P])
        eps = sb("eps", [P, 1])
        never = sb("never", [P, P])
        N_GAIN, N_CONV, N_CB = 8 * KT, KC * CONV_TILES, CONV_TILES
        gains = sb("gains", [P, N_GAIN])
        conv_w = sb("conv_w", [P, N_CONV])
        misc = sb("misc", [P, N_CB + 2 + INNER // P])
        G_SSM, G_MLP, G_PLE, G_GATE, G_ATTN = 0, KT, 3 * KT, 5 * KT, 7 * KT
        Q_COL, K_COL, OUT_COL = N_CB, N_CB + 1, N_CB + 2
        qscale = sb("qscale", [P, 1])
        rstd = sb("rstd", [P, T])
        rstd_tok = sb("rstd_tok", [P, TB])
        rstd_e = sb("rstd_e", [P, T])
        head_eps = rstd_e
        sq4 = sb("sq4", [P, TG, T])
        acc4 = sb("acc4", [P, TG, T])

        with ExitStack() as c:
            c.enter_context(nc.sbuf_tensor("xb_first_half", [P, KT * T], F32))
            v_tok = c.enter_context(nc.sbuf_tensor("v_tok", [P, HEADS, TB, HD], F32))
        xb = sb("xb", [P, KT, 2, T], F32R)

        def phase(tensors):
            with ExitStack() as c:
                return [c.enter_context(nc.sbuf_tensor(n, s, dt)) for n, s, dt in tensors]

        x_tok, rows0, rows1, rows2, rows3, rows4 = phase(
            [("x_tok", [P, TB, D], F32)] + [(f"rows{i}", [P, P], F32) for i in range(5)])
        qk, sq, nrm = phase([("qk", [P, HEADS, 2, T], F32), ("sq", [P, TG, T], F32),
                             ("nrm", [P, TG, T], F32)])
        soft, logb, ell = phase([("qk_again", [P, HEADS, 2, T], F32), ("sq_again", [P, TG, T], F32),
                                    ("nrm_again", [P, TG, T], F32), ("soft", [P, 2, 384], F32),
                                    ("logb", [P, 2, 384], F32), ("ell", [P, 2, 384], F32)])[3:]
        e, rbuf, ubuf, p_tok, p_t, sig, acc_e = phase(
            [("e", [P, KT, T], F32), ("rbuf", [P, TG, T], F32), ("ubuf", [P, TG, T], F32),
             ("p_tok", [P, TB, PLE], F32), ("p_t", [P, 2, 2, T], F32R), ("sig", [P, TG, T], F32),
             ("acc_e", [P, TG, T], F32)])

        ssm_shapes = [("cb", [P, SG, 384], F32), ("xr", [P, TG, KC - 1 + T], F32), ("xc", [P, TG * T], F32),
                      ("x_skip", [P, TB * GC], F32), ("zg", [P, TB * GC], F32), ("dt", [P, TB, SH], F32),
                      ("dt_a", [P, TB, SH], F32), ("dt_ell", [P, TB, SH], F32), ("decay_t", [SH, T], F32),
                      ("offset", [P, 3, SH], F32), ("head_p", [P, 3, SH], F32), ("y_rms", [P, TB], F32)]
        cb, xr, xc, x_skip, zg, dt, dt_a, dt_ell, decay_t, offset, head_p, y_rms, rb, mix = phase(
            ssm_shapes + [("rb", [P, 4, T], F32), ("mix", [P, 2, 4, 384], F32)])
        bt, ct = phase([(n + "_again", *z) for n, *z in ssm_shapes] +
                       [("bt", [P, SG, T], F32), ("ct", [P, SG, T], F32)])[-2:]

        wide = [ctx.enter_context(nc.psum_tensor(f"banks{i}", [P, 4 * GC], F32)) for i in range(2)]
        gp, aux = ([w[:, 2 * GC * i:2 * GC * (i + 1)] for i in range(2)] for w in wide)

        def wide_part(i, part):
            return wide[i][:].rearrange("p (n x t) -> p n x t", n=TG, x=2)[:, :, part, :]

        def mean_at(name):
            return aux[1] if name == "attn" else gp[1]

        landed = [sem(f"landed{i}") for i in range(RAW)]
        hi_made = sem("hi_made")
        lo_made = sem("lo_made")
        slot_used = sem("slot_used")
        group_read = sem("group_read")

        def gain(col, n=1):
            return gains[:, bass.ds(col, n)]

        norm_col = {"attn": G_ATTN, "ssm": G_SSM}
        for l in range(layers):
            norm_col[f"mlp{l}"] = G_MLP + KT * l
            norm_col[f"gate{l}"] = G_GATE + KT * l

        def staged(c):
            return raw[c][:].rearrange("p a b -> p (a b)")

        block = ctx.enter_context(nc.Block())

        @block.sync
        def _(sp):
            def load_x(c):
                sp.dma_start(x_tok[:, :, c * GC:(c + 1) * GC],
                             x[0, :, c * GC:(c + 1) * GC].rearrange("(b q) n -> q b n", q=P)).then_inc(
                                 sem(f"x_in{c}"), 16)
            sp.dma_start(rows4[0:KT, :], attn_norm.rearrange("l (k p) -> (l k) p", p=P)).then_inc(
                sem("gain_in"), 16)
            load_x(0)
            rows = [
                (rows0, G_SSM, ssm_norm.rearrange("l (k p) -> (l k) p", p=P)),
                (rows0, G_MLP, mlp_norm.rearrange("l (k p) -> (l k) p", p=P)),
                (rows0, G_PLE, ple_norm.rearrange("l (k p) -> (l k) p", p=P)),
                (rows0, G_GATE, ple_gate_norm.rearrange("l (k p) -> (l k) p", p=P)),
                (rows1, 0, ssm_conv_w[0].rearrange("c (k p) -> (c k) p", p=P)[0:P]),
                (rows2, 0, ssm_conv_w[0].rearrange("c (k p) -> (c k) p", p=P)[P:N_CONV]),
                (rows3, 0, ssm_conv_b.rearrange("l (k p) -> (l k) p", p=P)),
                (rows3, Q_COL, attn_q_norm),
                (rows3, K_COL, attn_k_norm),
                (rows3, OUT_COL, ssm_out_norm.rearrange("l (k p) -> (l k) p", p=P)),
            ]

            def load(slot, r, src, shape=None):
                dst = raw[slot % RAW][:] if shape is None else \
                    raw[slot % RAW][:].rearrange("p a b -> p (a b)").rearrange("p (k n) -> p k n", k=shape)
                if slot >= RAW or not isinstance(r, int):
                    sp.wait_ge(lo_made, slot - RAW + 1 + RAW * r)
                sp.dma_start(dst, src).then_inc(landed[slot % RAW], 16)

            def load_group(slot, r, w, k0, col):
                for j in range(HS_PER_GROUP):
                    load(slot + j, r, w[:, bass.ds(k0 + 2 * j, 2), bass.ds(col, GC)])

            def tiles(w):
                return w.rearrange("(k p) n -> p k n", p=P)

            def load_out(name, w, k0, l=None):
                for c in range(4):
                    if c != 2 or l is None:
                        load_group(st[name].slot, c, w, k0, c * GC)
                    else:
                        for j in range(HS_PER_GROUP):
                            load(st[name].slot + 8 * c + j, 0, w[:, k0 + 2 * j:k0 + 2 * j + 2, c * GC:(c + 1) * GC])
                            if j != 2:
                                continue
                            sp.dma_start(p_tok[:], p[l, 0].rearrange("(b q) n -> q b n", q=P)).then_inc(
                                sem(f"p_in{l}"), 16)

            def load_mlp(l):
                s = st[f"mlp{l}"].slot
                up, down = tiles(mlp_w_up[l]), tiles(mlp_w_down[l])
                with sp.Fori(0, 4) as f:
                    with sp.Fori(0, 4) as c:
                        load_group(s, f * 8 + c, up, 0, f * D + c * GC)
                    with sp.Fori(0, 4) as c:
                        load_group(s + 32, f * 8 + c, down, f * KT, c * GC)

            def load_ple(l):
                s = st[f"ple{l}"].slot
                for j in range(4):
                    load(s + j, 0, tiles(ple_w_proj[l])[:, :, j * GC:(j + 1) * GC])

            def load_simple(name, w, groups, col=0):
                with sp.Fori(0, groups) as c:
                    load_group(st[name].slot, c, w, 0, c * GC + col)

            wqkv = tiles(attn_w_qkv[0])
            s = st["qk"].slot
            for j in range(HS_PER_GROUP):
                load(s + j, 0, wqkv[:, 2 * j:2 * j + 2, 0:GC])
                if j < 2:
                    load_x(j + 1)
                if j == 1:
                    load_x(3)
                if j == 3:
                    for dst, at, src in rows:
                        sp.dma_start(dst[at:at + src.shape[0], :], src).then_inc(sem("rows_in"), 16)
            load_group(s + 8, 0, wqkv, 0, D)
            with sp.Fori(1, 4) as c:
                load_group(s, c * 2, wqkv, 0, c * GC)
                load_group(s + 8, c * 2, wqkv, 0, c * GC + D)
            load_simple("v", wqkv, 4, 2 * D)
            load_out("wo", tiles(attn_w_o[0]), 0, 0)
            for l in range(layers):
                if l == 1:
                    w_in, w_out = tiles(ssm_w_in[0]), tiles(ssm_w_out[0])
                    load_group(st["bc0"].slot, 0, w_in, 0, 2 * INNER)
                    load(st["dt"].slot, 0, w_in[:, :, 2 * INNER + 2 * SG * SN:], shape=KT)
                    load_simple("bc", w_in, 3, 2 * INNER + GC)
                    for half in range(2):
                        with sp.Fori(1, 5) as i:
                            first, col = st[f"xz{half}"].slot - 2 * HS_PER_GROUP, half * D - GC
                            load_group(first, 2 * i, w_in, 0, INNER + col + i * GC)
                            load_group(first + HS_PER_GROUP, 2 * i, w_in, 0, col + i * GC)
                        load_out(f"out{half}", w_out, half * KT, 1 if half else None)
                load_ple(l)
                load_mlp(l)
                load_simple(f"gate{l}", tiles(ple_w_gate[l]), 4)
            for c in range(4):
                sp.wait_ge(sem("out_staged"), c + 1 if c < 3 else 5)
                sp.dma_start(out[0].rearrange("(b q) n -> q b n", q=P)[:, :, c * GC:(c + 1) * GC],
                             staged(c).rearrange("p (b n) -> p b n", b=TB)).then_inc(sem("out_done"), 16)
            sp.wait_ge(sem("out_done"), 64)

        @block.gpsimd
        def _(pool):
            own = Steps(pool, sem("pool_step"))
            for m in (ident, later, earlier, never):
                own.inc(pool.memset(m[:], 0.0))
            for m in (ones, upto):
                own.inc(pool.memset(m[:], 1.0))
            own.inc(pool.memset(eps[:], EPS))
            own.settle()
            def mask(m, op, sign, fill):
                pool.affine_select(out=m[:], in_=m[:], compare_op=op, fill=fill, base=0,
                                   pattern=[[-sign, P]], channel_multiplier=sign).then_inc(sem("masks"), 1)
            mask(ident, ALU.not_equal, 1, 1.0)
            mask(later, ALU.is_ge, -1, 1.0)
            mask(earlier, ALU.is_ge, 1, 1.0)
            mask(never, ALU.is_ge, -1, -1e38)
            mask(upto, ALU.is_ge, -1, 0.0)

            def square_group(src, ready, value, acc, first):
                pool.wait_ge(ready, value)
                own.settle()
                if first:
                    own.inc(pool.tensor_tensor(acc[:], src, src, ALU.mult))
                    return
                own.inc(pool.tensor_tensor(sq4[:], src, src, ALU.mult))
                own.settle()
                own.inc(pool.tensor_tensor(acc[:], acc[:], sq4[:], ALU.add))

            def fold(name, acc):
                own.settle()
                own.inc(pool.tensor_tensor(acc[:, 0:2, :], acc[:, 0:2, :], acc[:, 2:4, :], ALU.add))
                own.settle()
                pool.tensor_tensor(acc[:, 0, :], acc[:, 0, :], acc[:, 1, :], ALU.add).then_inc(
                    sem(f"{name}_sum"), 1)

            def square_h(name, before=None, ready=None, at=0):
                if before:
                    pool.wait_ge(sem(f"{before}_mean"), 1)
                for c in range(4):
                    square_group(h[:, 4 * c:4 * c + 4, :], ready or sem(f"{name}_h"), at + c + 1, acc4, c == 0)
                fold(name, acc4)

            def decays():
                for i, a in enumerate((ssm_dt_bias, ssm_a_log, ssm_d)):
                    if i == 0:
                        pool.wait_ge(sem("ssm_h"), 4)
                    pool.dma_start(head_p[:, i, :], a.broadcast_to([P, SH])).then_inc(sem("heads_in"), 16)
                pool.wait_ge(sem("decay_t"), 1)
                pool.dma_start(decay_rows, decay_t[:]).then_inc(sem("rows_out"), 16)
                pool.wait_ge(sem("rows_out"), 16)
                pool.wait_ge(sem("cb"), SG)
                for half in range(2):
                    with own.loop(4 * half, 4 * half + 4, 6) as g:
                        for b in range(2):
                            own.settle()
                            pool.dma_start(rb[:], decay_rows[bass.ds(8 * g + 4 * b, 4), :].unsqueeze(0)
                                           .broadcast_to([P, 4, T])).then_inc(sem("rb_in"), 16)
                            pool.wait_ge(sem("rb_in"), 32 * g + 16 * b + 16)
                            if b == 0:
                                pool.wait_ge(sem("mix_free"), g + 1)
                            for dst, src, o in ((0, 0, 0), (1, 1, 2), (2, 1, 1)):
                                own.inc(pool.tensor_tensor(
                                    mix[:, b, :, dst * P:(dst + 1) * P], rb[:, :, src * P:(src + 1) * P],
                                    offset[:, o, bass.ds(8 * g + 4 * b, 4)].unsqueeze(2).broadcast_to([P, 4, P]),
                                    ALU.add))
                            own.settle()
                            diagonal = mix[:, b].rearrange("p h (c n) -> p h c n", c=3)[:, :, 0:3:2, :]
                            pool.tensor_tensor(diagonal, diagonal,
                                               never[:].unsqueeze(1).unsqueeze(1).broadcast_to([P, 4, 2, P]),
                                               ALU.add).then_inc(sem("exponents"), 1)

            square_h("attn")
            pool.wait_ge(sem("head_eps"), 1)
            with pool.Fori(0, 8) as m:
                pool.wait_ge(sem("qk_squared"), m + 1)
                pool.tensor_tensor(sq[:], sq[:], head_eps[:].unsqueeze(1).broadcast_to([P, TG, T]),
                                   ALU.add).then_inc(sem("qk_squares"), 1)
            for hp in range(HEADS // 2):
                pool.wait_ge(sem("weights_raw"), hp + 1)
                a = qk[:, 2 * hp:2 * hp + 2].rearrange("p h a b -> p h (a b)")[:, :, 0:384].rearrange(
                    "p h (c n) -> p h c n", c=3)[:, :, 0:3:2, :]
                pool.tensor_tensor(a, a, earlier[:].unsqueeze(1).unsqueeze(1).broadcast_to([P, 2, 2, P]),
                                   ALU.mult).then_inc(sem("weights_masked"), 1)
            for l in range(layers):
                if l == 1:
                    square_h("ssm", before="gate0")
                    decays()
                m = st[f"mlp{l}"].group
                square_h(f"mlp{l}", "attn" if l == 0 else "ssm", group_read, m - 8)
                for c in range(4):
                    square_group(e[:, 4 * c:4 * c + 4, :], group_read, m - 4 + c + 1, acc_e, c == 0)
                fold(f"e{l}", acc_e)
                square_h(f"gate{l}", f"mlp{l}", group_read, m + 28)

        @block.scalar
        def _(act):
            own = Steps(act, sem("act_step"))

            def cut(slot, r=0):
                if slot >= n_slots:
                    return
                act.wait_ge(landed[slot % RAW], 16 * (slot // RAW + 1) + 16 * r)
                if slot >= CUT:
                    act.wait_ge(slot_used, slot - CUT + 1 + RAW * r)
                act.activation(w_hi[slot % CUT][:], raw[slot % RAW][:], ACT.Copy).then_inc(hi_made, 1)

            def cuts(slot, r=0, js=range(HS_PER_GROUP)):
                for j in js:
                    cut(slot + AHEAD + j, r)

            def x_hi(name, c, dst, ready, value):
                col = norm_col[name]
                act.wait_ge(ready, value)
                for n in range(TG):
                    k = 4 * c + n
                    ins = act.activation(dst[:, bass.ds(k, 1), 0, :], h[:, bass.ds(k, 1), :], ACT.Copy,
                                         scale=gain(col + k))
                ins.then_inc(sem(f"{name}_hi"), 1)

            def norm_root(name, tok=False):
                act.wait_ge(sem(f"{name}_mean"), 1)
                ins = act.activation(rstd[:], mean_at(name)[:, 0:T], ACT.Sqrt, bias=eps[:, 0:1],
                                     scale=1.0 / D)
                if tok:
                    ins = act.activation(rstd_tok[:], mean_at(name)[:, GC:GC + TB], ACT.Sqrt, bias=eps[:, 0:1],
                                         scale=1.0 / D)
                ins.then_inc(sem(f"{name}_root"), 1)

            act.wait_ge(sem("masks"), 5)
            act.wait_ge(sem("gain_kept"), 1)
            for c in range(4):
                if c != 2:
                    first = (0, 2, None, 4)[c]
                    cut(first)
                    cut(first + 1)
                x_hi("attn", c, xa, sem("attn_h"), c + 1)

            def square_heads(m, par, done, r):
                act.wait_ge(slot_used, done + RAW * r)
                act.activation(sq[:], gp[par][:].rearrange("p (a b) -> p a b", a=TG),
                               ACT.Square).then_inc(sem("qk_squared"), 1)

            def root_heads(m, pair=0):
                act.wait_ge(sem("qk_mean"), m + 1)
                if not isinstance(m, int) or m:
                    act.wait_ge(group_read, m)
                act.activation(nrm[:], aux[pair][:], ACT.Sqrt, scale=1.0 / HD).then_inc(sem("qk_rooted"), 1)

            q = st["qk"]
            cuts(q.slot, js=range(2, 7))
            norm_root("attn", tok=True)
            act.wait_ge(sem("attn_root"), 1)
            act.activation(head_eps[:], rstd[:], ACT.Square, scale=EPS ** 0.5).then_inc(sem("head_eps"), 1)
            cuts(q.slot, js=range(7, 8))
            square_heads(0, 0, q.slot + 8, 0)
            cuts(q.slot + 8, js=range(0, 2))
            root_heads(0)
            cuts(q.slot + 8, js=range(2, 8))
            square_heads(1, 1, q.slot + 16, 0)
            with act.Fori(1, 4) as c:
                for m in range(2):
                    cuts(q.slot + 8 * m, 2 * c, range(0, 2))
                    root_heads(2 * c + m - 1)
                    cuts(q.slot + 8 * m, 2 * c, range(2, 8))
                    square_heads(2 * c + m, m, q.slot + 8 * m + 8, 2 * c)
            def pair_of(m):
                return m[:].rearrange("p (b n) -> p b n", b=2)[:, :, 0:384]

            def soft_pair(hp):
                act.wait_ge(sem("z"), hp + 1)
                own.inc(act.activation(ell[:], pair_of(aux[0]), ACT.Abs))
                own.settle()
                own.inc(act.activation(ell[:], ell[:], ACT.Exp, scale=-1.0))
                own.settle()
                act.activation(ell[:], ell[:], ACT.Ln, bias=1.0).then_inc(sem("ell"), 1)

            def weigh_pair(hp):
                act.wait_ge(sem("log_weights"), hp + 1)
                act.activation(qk[:, 2 * hp:2 * hp + 2].rearrange("p h a b -> p h (a b)")[:, :, 0:384], logb[:],
                               ACT.Exp).then_inc(sem("weights_raw"), 1)

            for g in range(4):
                for i in range(2):
                    if 2 * g + i:
                        weigh_pair(2 * g + i - 1)
                    soft_pair(2 * g + i)
                    cuts(st["v"].slot + 8 * g, js=range(4 * i, 4 * i + 2))
                    if g == i == 0:
                        root_heads(7, pair=1)
                    cuts(st["v"].slot + 8 * g, js=range(4 * i + 2, 4 * i + 4))
            weigh_pair(HEADS // 2 - 1)

            def o_hi(q):
                act.wait_ge(sem("o"), q + 1)
                act.activation(xb[:, 4 * q:4 * q + 4, 0, :], aux[q % 2][:].rearrange("p (a b) -> p a b", a=4),
                               ACT.Copy).then_inc(sem("o_hi"), 1)

            o_hi(0)
            o_hi(1)

            def p_hi(l):
                act.wait_ge(sem(f"p_turned{l}"), 1)
                act.activation(p_t[:, :, 0, :], aux[0][:, 0:GC].rearrange("p (a b) -> p a b", a=2),
                               ACT.Copy).then_inc(sem(f"p_hi{l}"), 1)

            def keep_e(l, j):
                act.wait_ge(slot_used, st[f"ple{l}"].slot + j + 1)
                if j == 0:
                    act.wait_ge(group_read, st[f"ple{l}"].group)
                act.activation(e[:, 4 * j:4 * j + 4, :],
                               gp[(st[f"ple{l}"].group + j) % 2][:].rearrange("p (a b) -> p a b", a=TG),
                               ACT.Copy).then_inc(group_read, 1)

            def embed(l, x_next):
                s = st[f"ple{l}"]
                cuts(s.slot, js=range(1))
                keep_e(l, 0)
                x_hi(f"mlp{l}", 3, x_next, group_read, s.group)
                for j in range(1, 4):
                    cuts(s.slot + j, js=range(1))
                    keep_e(l, j)

            for c in range(4):
                for j in range(HS_PER_GROUP):
                    cuts(st["wo"].slot + 8 * c, js=range(j, j + 1))
                    if c == 0 and j in (1, 3):
                        o_hi(2 + j // 2)
                    if c == 2 and j == 4:
                        p_hi(0)
                if c < 3:
                    x_hi("mlp0", c, xa, group_read, st["wo"].group + c + 1)
            embed(0, xa)

            def keep_b(done, r, par, name):
                act.wait_ge(slot_used, done + RAW * r)
                act.activation(rbuf[:], wide_part(par, 1), ACT.Copy).then_inc(sem(name), 1)

            def mlp(l, x_next):
                s = st[f"mlp{l}"].slot
                ub = xb if l == 0 else xa

                def squares(c, f, par):
                    keep_b(s + 8, 8 * f + c, par, f"up_b{l}")
                    act.wait_ge(sem(f"relu{l}"), 4 * f + c + 1)
                    own.inc(act.activation(ubuf[:], rbuf[:], ACT.Square))
                    own.settle()
                    act.activation(ub[:, bass.ds(4 * c, 4), 0, :], ubuf[:], ACT.Copy).then_inc(
                        sem(f"u_hi{l}"), 1)

                def up_down(f, first=False, last=False):
                    if first:
                        cuts(s, js=range(0, 7))
                        norm_root(f"mlp{l}")
                        cuts(s, js=range(7, 8))
                        squares(0, 0, 1)
                        cuts(s + 8)
                        act.wait_ge(sem(f"e{l}_mean"), 1)
                        act.activation(rstd_e[:], wide[1][:, 3 * GC:3 * GC + T], ACT.Sqrt, bias=eps[:, 0:1],
                                       scale=1.0 / D).then_inc(sem(f"e{l}_root"), 1)
                        squares(1, 0, 0)
                    with own.loop(int(first), 2, 2) as c2:
                        for b in range(2):
                            cuts(s + 8 * b, 8 * f + 2 * c2)
                            squares(2 * c2 + b, f, 1 - b)
                    with act.Fori(0, 4) as c:
                        cuts(s + 32, 8 * f + c)
                        if last:
                            x_hi(f"gate{l}", c, x_next, group_read, st[f"mlp{l}"].group + 28 + c + 1)

                up_down(0, first=True)
                with own.loop(1, 3, 4) as f:
                    up_down(f)
                up_down(3, last=True)

            def stage_out(c):
                act.wait_ge(sem("final_turned"), c + 1)
                act.activation(staged(c), aux[c % 2], ACT.Copy).then_inc(sem("out_staged"), 1)

            def last_gate(l, s):
                act.wait_ge(lo_made, n_slots)
                for c in range(3):
                    stage_out(c)
                act.wait_ge(slot_used, s + 32)
                for m in range(2):
                    act.activation(rbuf[:, 2 * m:2 * m + 2, :], wide_part(0, 1)[:, 2 * m:2 * m + 2, :],
                                   ACT.Copy).then_inc(sem(f"gate_b{l}"), 1)
                for m in range(2):
                    act.wait_ge(sem(f"gate_in{l}"), 4 + m)
                    act.activation(sig[:, 2 * m:2 * m + 2, :], rbuf[:, 2 * m:2 * m + 2, :],
                                   ACT.Sigmoid).then_inc(sem(f"gate_open{l}"), 1)
                act.wait_ge(sem("final_turned"), 4)
                act.activation(staged(3)[:, 0:GC], aux[1][:, 0:GC], ACT.Copy).then_inc(sem("out_staged"), 1)

            def gate(l, x_next, next_name):
                s = st[f"gate{l}"].slot
                for c in range(4):
                    cuts(s + 8 * c, js=range(0 if c == 0 else 2, 6))
                    if c == 0:
                        norm_root(f"gate{l}")
                    cuts(s + 8 * c, js=range(6, 8))
                    if c:
                        act.wait_ge(sem(f"gate_open{l}"), c)
                    if c == 3 and next_name == "final":
                        last_gate(l, s)
                        break
                    keep_b(s + 8 * c + 8, 0, 1 - c % 2, f"gate_b{l}")
                    cuts(s + 8 * c + 8, js=range(0, 1))
                    act.wait_ge(sem(f"gate_in{l}"), c + 1)
                    act.activation(sig[:], rbuf[:], ACT.Sigmoid).then_inc(sem(f"gate_open{l}"), 1)
                    cuts(s + 8 * c + 8, js=range(1, 2))
                    if x_next is not None:
                        x_hi(next_name, c, x_next, sem(f"{next_name}_h"), c + 1)

            def silu_conv(q, dst, bias_col):
                act.wait_ge(sem("conv"), q + 1)
                for n in range(TG):
                    ins = act.activation(dst(n), xc[:, n * T:(n + 1) * T], ACT.Silu,
                                         bias=misc[:, bass.ds(bias_col + n, 1)])
                ins.then_inc(sem("conv_silu"), 1)

            def y_square(g):
                act.wait_ge(sem("gated"), g + 1)
                for b in range(TB):
                    own.inc(act.activation(sq4[:].rearrange("p a b -> p (a b)")[:, b * GC:(b + 1) * GC],
                                              zg[:, b * GC:(b + 1) * GC], ACT.Square,
                                              accum_out=y_rms[:, b:b + 1]))
                own.settle()
                act.activation(y_rms[:], y_rms[:], ACT.Sqrt, bias=eps[:, 0:1],
                               scale=1.0 / GC).then_inc(sem("y_root"), 1)

            def y_hi(g, half):
                act.wait_ge(sem("y_turned"), g + 1)
                for n in range(TG):
                    ins = act.activation(xa[:, bass.ds(4 * g - KT * half + n, 1), 0, :],
                                         aux[0][:, n * T:(n + 1) * T], ACT.Copy,
                                         scale=misc[:, bass.ds(OUT_COL + 4 * g + n, 1)])
                ins.then_inc(sem("y_hi"), 1)

            def decay(g, b):
                act.wait_ge(sem("exponents"), 2 * g + b + 1)
                act.activation(mix[:, b], mix[:, b], ACT.Exp).then_inc(sem("decayed"), 1)

            def ssm_pair(half, g, i, first):
                s, r = st[f"xz{half}"].slot, 2 * i
                cuts(s, r, range(0, 2))
                if not first:
                    y_square(g - 1)
                cuts(s, r, range(2, 4))
                if first and half == 0:
                    silu_conv(3, lambda n: ct[:, 4 + n, :], 44)
                cuts(s, r, range(4, 5))
                if not first:
                    y_hi(g - 1, half)
                cuts(s, r, range(5, 8))
                if not first:
                    decay(g, 0)
                cuts(s + 8, r, range(0, 1))
                if not first:
                    decay(g, 1)
                cuts(s + 8, r, range(1, 4))
                silu_conv(4 + g, lambda n: xc[:, n * T:(n + 1) * T], 4 * g)
                cuts(s + 8, r, range(4, 5))
                if first:
                    decay(g, 0)
                cuts(s + 8, r, range(5, 7))
                if first:
                    decay(g, 1)
                cuts(s + 8, r, range(7, 8))
                act.wait_ge(slot_used, s + 16 + RAW * r)
                for b in range(TB):
                    ins = act.activation(zg[:, b * GC:(b + 1) * GC],
                                         gp[(st[f"xz{half}"].group + 1) % 2][:, b * GC:(b + 1) * GC],
                                         ACT.Silu, scale=rstd_tok[:, b:b + 1])
                ins.then_inc(sem("z_silu"), 1)

            def ssm():
                s = st["bc0"].slot
                cuts(s, js=range(2, 6))
                norm_root("ssm", tok=True)
                cuts(s, js=range(6, 8))
                cuts(st["dt"].slot, js=range(1))
                s = st["bc"].slot
                act.wait_ge(sem("dt_raw"), 1)
                own.inc(act.activation(dt_ell[:], dt[:], ACT.Abs))
                own.settle()
                own.inc(act.activation(dt_ell[:], dt_ell[:], ACT.Exp, scale=-1.0))
                own.inc(act.activation(head_p[:, 1, :], head_p[:, 1, :], ACT.Exp))
                own.settle()
                cuts(s, js=range(0, 1))
                act.activation(dt_ell[:], dt_ell[:], ACT.Ln, bias=1.0).then_inc(sem("dt_ell"), 1)
                silu_conv(0, lambda n: bt[:, n, :], 32)
                cuts(s, js=range(1, 8))
                for q in range(1, 3):
                    cuts(s + 8 * q, js=range(0, 4))
                    silu_conv(q, lambda n: (bt if q < 2 else ct)[:, 4 * (q % 2) + n, :], 32 + 4 * q)
                    cuts(s + 8 * q, js=range(4, 8))
                for half in range(2):
                    ssm_pair(half, 4 * half, 0, True)
                    with own.loop(1, 4, 2) as i:
                        ssm_pair(half, 4 * half + i, i, False)
                    s = st[f"out{half}"]
                    for c in range(4):
                        cuts(s.slot + 8 * c, js=range(0, 2))
                        if c == 0:
                            y_square(4 * half + 3)
                        cuts(s.slot + 8 * c, js=range(2, 5))
                        if c == 0:
                            y_hi(4 * half + 3, half)
                        if half == 1 and c == 2:
                            p_hi(1)
                        cuts(s.slot + 8 * c, js=range(5, 8))
                        if half == 1 and c < 3:
                            x_hi("mlp1", c, xb, group_read, s.group + c + 1)
                embed(1, xb)

            mlp(0, xa)
            gate(0, xb if layers > 1 else None, "ssm")
            if layers > 1:
                ssm()
                mlp(1, xb)
                gate(1, None, "final")

        @block.vector
        def _(dve):
            own = Steps(dve, sem("dve_step"))

            def cut(slot, r=0):
                if slot >= n_slots:
                    return
                dve.wait_ge(hi_made, slot + 1 + RAW * r)
                dve.tensor_tensor(w_lo[slot % CUT][:], raw[slot % RAW][:], w_hi[slot % CUT][:].bitcast(F32),
                                  ALU.subtract).then_inc(lo_made, 1)

            def cuts(slot, r=0, js=range(HS_PER_GROUP)):
                for j in js:
                    cut(slot + AHEAD + j, r)

            def x_lo(name, c, dst):
                col = norm_col[name]
                dve.wait_ge(sem(f"{name}_hi"), c + 1)
                for n in range(TG):
                    k = 4 * c + n
                    ins = dve.scalar_tensor_tensor(
                        dst[:, bass.ds(k, 1), 1, :], h[:, bass.ds(k, 1), :], gain(col + k),
                        dst[:, bass.ds(k, 1), 0, :].bitcast(F32), ALU.mult, ALU.subtract)
                ins.then_inc(sem(f"{name}_lo"), 1)

            def read_group(s, done, r=0):
                dve.wait_ge(slot_used, done + RAW * r)

            def project(s, c, name=None, dst=None):
                read_group(s, s.slot + 8 * c + 8)
                hc = h[:, 4 * c:4 * c + 4, :]
                if c == 0:
                    src = gp[s.group % 2].rearrange("p (a b) -> p a b", a=TG)
                else:
                    own.inc(dve.tensor_tensor(hc, hc, wide_part(c % 2, 1), ALU.add))
                    own.settle()
                    src = wide_part(c % 2, 0)
                dve.tensor_tensor(hc, hc, src, ALU.add).then_inc(group_read, 1)
                if name:
                    x_lo(name, c, dst)

            def norm_recip(name, tok=False):
                dve.wait_ge(sem(f"{name}_root"), 1)
                own.inc(dve.reciprocal(rstd[:], rstd[:]))
                if tok:
                    own.inc(dve.reciprocal(rstd_tok[:], rstd_tok[:]))
                own.settle()

            rstd4 = rstd[:].unsqueeze(1).broadcast_to([P, TG, T])

            dve.wait_ge(sem("gain_turned"), 1)
            dve.tensor_copy(gains[:, G_ATTN:G_ATTN + KT], aux[1][:, 0:KT]).then_inc(sem("gain_kept"), 1)

            def keep_rows():
                dve.wait_ge(sem("rows_turned"), 1)
                for i, (dst, n, at) in enumerate(((gains, N_GAIN - KT, 0), (conv_w, P, 0),
                                                  (conv_w, N_CONV - P, P),
                                                  (misc, N_CB + 2 + INNER // P, 0))):
                    ins = dve.tensor_copy(dst[:, at:at + n], aux[1][:, 128 * i:128 * i + n])
                own.inc(ins)
                own.settle()
                dve.tensor_scalar(qscale[:], misc[:, Q_COL:Q_COL + 1], float(HD) ** -0.5, None,
                                  ALU.mult).then_inc(sem("params"), 1)

            def keep_x(c):
                dve.wait_ge(sem("x_turned"), c + 1)
                dve.tensor_copy(h[:, 4 * c:4 * c + 4, :],
                                (gp[1], aux[0], aux[1])[c % 3][:].rearrange("p (a b) -> p a b", a=TG)).then_inc(
                                    sem("attn_h"), 1)

            keep_x(0)
            for c in range(4):
                if c < 3:
                    keep_x(c + 1)
                if c != 2:
                    first = (0, 2, None, 4)[c]
                    cut(first)
                    cut(first + 1)
                x_lo("attn", c, xa)
            keep_rows()

            q = st["qk"]

            def norm_head(n, par, k, which):
                g = qscale[:, 0:1] if which == 0 else misc[:, K_COL:K_COL + 1]
                own.inc(dve.reciprocal(nrm[:, n, :], nrm[:, n, :]))
                own.settle()
                return dve.scalar_tensor_tensor(qk[:, bass.ds(k, 1), which, :], gp[par][:, n * T:(n + 1) * T],
                                                g, nrm[:, n, :], ALU.mult, ALU.mult)

            def norm_heads(m, par, c, which, slot, r):
                cuts(slot, r, range(0, 2))
                dve.wait_ge(sem("qk_rooted"), m + 1)
                for n in range(TG):
                    ins = norm_head(n, par, 4 * c + n, which)
                    if n == TG - 1:
                        ins.then_inc(group_read, 1)
                    cuts(slot, r, range(2 + n, 3 + n))
                cuts(slot, r, range(6, 8))

            cuts(q.slot, js=range(2, 8))
            dve.wait_ge(sem("attn_root"), 1)
            own.inc(dve.reciprocal(rstd_tok[:], rstd_tok[:]))
            own.settle()
            norm_heads(0, 0, 0, 0, q.slot + 8, 0)
            with own.loop(1, 4, 8) as c:
                norm_heads(2 * c - 1, 1, c - 1, 1, q.slot, 2 * c)
                norm_heads(2 * c, 0, c, 0, q.slot + 8, 2 * c)

            def pair_of(m):
                return m[:].rearrange("p (b n) -> p b n", b=2)[:, :, 0:384]

            def soft_pair(hp):
                z = pair_of(aux[0])
                dve.wait_ge(sem("ell"), hp + 1)
                own.inc(dve.scalar_tensor_tensor(soft[:], z, 0.0, ell[:], ALU.max, ALU.add))
                own.inc(dve.scalar_tensor_tensor(logb[:], z, 0.0, ell[:], ALU.min, ALU.subtract))
                own.settle()
                d = soft[:].rearrange("p b (c n) -> p b c n", c=3)[:, :, 0:3:2, :]
                dve.tensor_tensor(d, d, earlier[:].unsqueeze(1).unsqueeze(1).broadcast_to([P, 2, 2, P]),
                                  ALU.mult).then_inc(sem("soft"), 1)

            def log_pair(hp):
                dve.wait_ge(sem("suffix"), hp + 1)
                dve.tensor_tensor(logb[:], logb[:], pair_of(aux[1]), ALU.subtract).then_inc(
                    sem("log_weights"), 1)

            v = st["v"]
            for g in range(4):
                for i in range(2):
                    soft_pair(2 * g + i)
                    for j in range(4):
                        cuts(v.slot + 8 * g, js=range(4 * i + j, 4 * i + j + 1))
                        if j == 2:
                            log_pair(2 * g + i)
                        if g == 0 and 1 <= 4 * i + j <= TG:
                            n = 4 * i + j - 1
                            dve.wait_ge(sem("qk_rooted"), 8)
                            ins = norm_head(n, 1, 12 + n, 1)
                            if n == TG - 1:
                                ins.then_inc(group_read, 1)
                read_group(v, v.slot + 8, g)
                for b in range(TB):
                    ins = dve.tensor_scalar(v_tok[:, 4 * g:4 * g + 4, b, :],
                                            gp[(v.group + g) % 2][:, b * GC:(b + 1) * GC].rearrange(
                                                "p (a d) -> p a d", a=4),
                                            rstd_tok[:, b:b + 1], None, ALU.mult)
                ins.then_inc(group_read, 1)

            def o_lo(q):
                dve.wait_ge(sem("o_hi"), q + 1)
                dve.tensor_tensor(xb[:, 4 * q:4 * q + 4, 1, :], aux[q % 2][:].rearrange("p (a b) -> p a b", a=4),
                                  xb[:, 4 * q:4 * q + 4, 0, :].bitcast(F32), ALU.subtract).then_inc(
                                      sem("o_lo"), 1)

            o_lo(0)
            o_lo(1)

            def p_lo(l):
                dve.wait_ge(sem(f"p_hi{l}"), 1)
                dve.tensor_tensor(p_t[:, :, 1, :], aux[0][:, 0:GC].rearrange("p (a b) -> p a b", a=2),
                                  p_t[:, :, 0, :].bitcast(F32), ALU.subtract).then_inc(sem(f"p_lo{l}"), 1)

            s = st["wo"]
            for c in range(4):
                for j in range(HS_PER_GROUP):
                    cuts(s.slot + 8 * c, js=range(j, j + 1))
                    if c == 0 and j in (1, 3):
                        o_lo(2 + j // 2)
                    if c == 2 and j == 4:
                        p_lo(0)
                project(s, c, "mlp0", xa)
            cuts(st["ple0"].slot, js=range(4))

            def mlp(l, x_next):
                s = st[f"mlp{l}"]
                ub = xb if l == 0 else xa

                def relu(c, f, par):
                    dve.wait_ge(sem(f"up_b{l}"), 4 * f + c + 1)
                    dve.tensor_tensor(rbuf[:], rbuf[:], wide_part(par, 0), ALU.add).then_inc(group_read, 1)
                    dve.wait_ge(group_read, s.group + 8 * f + c + 1)
                    dve.scalar_tensor_tensor(rbuf[:], rbuf[:], 0.0, rstd4, ALU.max, ALU.mult).then_inc(
                        sem(f"relu{l}"), 1)
                    dve.wait_ge(sem(f"u_hi{l}"), 4 * f + c + 1)
                    dve.tensor_tensor(ub[:, bass.ds(4 * c, 4), 1, :], ubuf[:],
                                      ub[:, bass.ds(4 * c, 4), 0, :].bitcast(F32),
                                      ALU.subtract).then_inc(sem(f"u_lo{l}"), 1)

                def wide_residual(c, f, par, last):
                    read_group(s, s.slot + 40, 8 * f + c)
                    hc = h[:, bass.ds(4 * c, 4), :]
                    dve.tensor_tensor(hc, hc, wide_part(par, 1), ALU.add).then_inc(sem(f"down_b{l}"), 1)
                    dve.wait_ge(sem(f"down_b{l}"), 4 * f + c + 1)
                    dve.tensor_tensor(hc, hc, wide_part(par, 0), ALU.add).then_inc(group_read, 1)
                    if last:
                        x_lo(f"gate{l}", c, x_next)

                def up_down(f, first=False, last=False):
                    if first:
                        cuts(s.slot, js=range(0, 7))
                        norm_recip(f"mlp{l}")
                        cuts(s.slot, js=range(7, 8))
                        dve.wait_ge(group_read, s.group)
                        relu(0, 0, 1)
                        cuts(s.slot + 8)
                        relu(1, 0, 0)
                        for b in range(2):
                            for j in range(HS_PER_GROUP):
                                cuts(s.slot + 16 + 8 * b, js=range(j, j + 1))
                                if b == 0 and j == 1:
                                    dve.wait_ge(sem(f"e{l}_root"), 1)
                                    own.inc(dve.reciprocal(rstd_e[:], rstd_e[:]))
                                    own.settle()
                                if j % 4 == 2:
                                    for k in range(8 * b + 4 * (j // 4), 8 * b + 4 * (j // 4) + 4):
                                        ins = dve.scalar_tensor_tensor(e[:, k, :], e[:, k, :],
                                                                       gain(G_PLE + KT * l + k), rstd_e[:],
                                                                       ALU.mult, ALU.mult)
                                    own.inc(ins)
                            relu(2 + b, 0, 1 - b)
                    else:
                        with dve.Fori(0, 2) as c2:
                            for b in range(2):
                                cuts(s.slot + 8 * b, 8 * f + 2 * c2)
                                relu(2 * c2 + b, f, 1 - b)
                    with dve.Fori(0, 2) as c2:
                        for b in range(2):
                            cuts(s.slot + 32 + 8 * b, 8 * f + 2 * c2)
                            wide_residual(2 * c2 + b, f, 1 - b, last)

                up_down(0, first=True)
                with dve.Fori(1, 3) as f:
                    up_down(f)
                up_down(3, last=True)

            def last_gate(l):
                for m in range(2):
                    part = rbuf[:, 2 * m:2 * m + 2, :]
                    dve.wait_ge(sem(f"gate_b{l}"), 4 + m)
                    own.inc(dve.tensor_tensor(part, part, wide_part(0, 0)[:, 2 * m:2 * m + 2, :], ALU.add))
                    own.settle()
                    dve.tensor_tensor(part, part, rstd[:].unsqueeze(1).broadcast_to([P, 2, T]),
                                      ALU.mult).then_inc(sem(f"gate_in{l}"), 1)
                for m in range(2):
                    part, hc = sig[:, 2 * m:2 * m + 2, :], h[:, 12 + 2 * m:14 + 2 * m, :]
                    dve.wait_ge(sem(f"gate_open{l}"), 4 + m)
                    own.inc(dve.tensor_tensor(part, part, e[:, 12 + 2 * m:14 + 2 * m, :], ALU.mult))
                    own.settle()
                    dve.tensor_tensor(hc, hc, part, ALU.add).then_inc(sem("final_h"), 1)
                dve.wait_ge(sem("final_turned"), 4)
                dve.tensor_copy(staged(3)[:, GC:], aux[1][:, GC:]).then_inc(sem("out_staged"), 1)

            def gate(l, x_next, next_name):
                s = st[f"gate{l}"]
                for c in range(4):
                    cuts(s.slot + 8 * c, js=range(0 if c == 0 else 2, 7))
                    if c == 0:
                        norm_recip(f"gate{l}")
                    cuts(s.slot + 8 * c, js=range(7, 8))
                    if c == 3 and next_name == "final":
                        last_gate(l)
                        break
                    dve.wait_ge(sem(f"gate_b{l}"), c + 1)
                    dve.tensor_tensor(rbuf[:], rbuf[:], wide_part(1 - c % 2, 0), ALU.add).then_inc(group_read, 1)
                    dve.wait_ge(group_read, s.group + c + 1)
                    dve.tensor_tensor(rbuf[:], rbuf[:], rstd4, ALU.mult).then_inc(sem(f"gate_in{l}"), 1)
                    cuts(s.slot + 8 * c + 8, js=range(0, 1))
                    dve.wait_ge(sem(f"gate_open{l}"), c + 1)
                    own.settle()
                    own.inc(dve.tensor_tensor(sig[:], sig[:], e[:, 4 * c:4 * c + 4, :], ALU.mult))
                    own.settle()
                    hc = h[:, 4 * c:4 * c + 4, :]
                    dve.tensor_tensor(hc, hc, sig[:], ALU.add).then_inc(sem(f"{next_name}_h"), 1)
                    cuts(s.slot + 8 * c + 8, js=range(1, 2))
                    if x_next is not None:
                        x_lo(next_name, c, x_next)

            def conv_open(q, s, done, r, par):
                read_group(s, done, r)
                if not isinstance(q, int) or q >= 1:
                    dve.wait_ge(sem("conv_silu"), q)
                own.inc(dve.tensor_tensor(xr[:, :, KC - 1:], gp[par][:].rearrange("p (a b) -> p a b", a=TG),
                                          rstd4, ALU.mult))
                own.settle()
                dve.sem_inc(group_read, 1)

            def conv_open_wide(s):
                read_group(s, s.slot + 8)
                own.inc(dve.tensor_tensor(xr[:, :, KC - 1:], wide_part(1, 0), rstd4, ALU.mult))
                xc4 = xc[:].rearrange("p (a b) -> p a b", a=TG)
                own.inc(dve.tensor_tensor(xc4, wide_part(1, 1), rstd4, ALU.mult))
                own.settle()
                dve.sem_inc(group_read, 1)
                own.inc(dve.tensor_tensor(xr[:, :, KC - 1:], xr[:, :, KC - 1:], xc4, ALU.add))
                own.settle()

            def conv_tap(tap, col):
                for n in range(TG):
                    w = conv_w[:, bass.ds(tap * CONV_TILES + col + n, 1)]
                    o = xc[:, n * T:(n + 1) * T]
                    if tap == 0:
                        ins = dve.tensor_scalar(o, xr[:, n, 0:T], w, None, ALU.mult)
                    else:
                        ins = dve.scalar_tensor_tensor(o, xr[:, n, tap:tap + T], w, o, ALU.mult, ALU.add)
                if tap < KC - 1:
                    own.inc(ins)
                    own.settle()
                else:
                    ins.then_inc(sem("conv"), 1)

            def conv_taps(slot, r, col):
                conv_tap(0, col)
                for tap in range(1, KC):
                    conv_tap(tap, col)
                    cuts(slot, r, range(tap - 1, tap))
                cuts(slot, r, range(KC - 1, KC))

            def dt_keep():
                s = st["dt"]
                read_group(s, s.slot + 1)
                own.inc(dve.tensor_copy(decay_t[:], gp[s.group % 2][0:SH, 0:T]))
                own.settle()
                dve.sem_inc(group_read, 1)
                dve.sem_inc(sem("dt_kept"), 1)

            def dt_open():
                dve.wait_ge(sem("dt_turned"), 1)
                dve.wait_ge(sem("heads_in"), 48)
                for b in range(TB):
                    ins = dve.scalar_tensor_tensor(dt[:, b, :], aux[0][:, b * GC:b * GC + SH],
                                                   rstd_tok[:, b:b + 1], head_p[:, 0, :], ALU.mult, ALU.add)
                own.inc(ins)
                own.settle()
                dve.sem_inc(sem("dt_raw"), 1)

            def dt_steps():
                dve.wait_ge(sem("dt_ell"), 1)
                own.inc(dve.scalar_tensor_tensor(dt[:], dt[:], 0.0, dt_ell[:], ALU.max, ALU.add))
                own.settle()
                dve.scalar_tensor_tensor(dt_a[:], dt[:], -1.0, head_p[:, 1, :].unsqueeze(1).broadcast_to([P, TB, SH]),
                                         ALU.mult, ALU.mult).then_inc(sem("dt_a"), 1)

            def dt_offsets():
                dve.wait_ge(sem("cumulated"), 1)
                dve.tensor_copy(decay_t[:], aux[1][0:SH, 0:T]).then_inc(sem("decay_t"), 1)
                dve.tensor_scalar(offset[:, 0:2, :], aux[1][:, GC:GC + 2 * SH].rearrange("p (b h) -> p b h", b=2),
                                  -1.0, None, ALU.mult)
                dve.tensor_copy(offset[:, 2, :], aux[1][:, GC + 2 * SH:GC + 3 * SH]).then_inc(sem("offset"), 1)

            def keep_cb(g):
                dve.wait_ge(sem("cb_raw"), g + 1)
                dve.tensor_copy(cb[:, g, :], aux[0][:, (g % 2) * GC:(g % 2) * GC + 384]).then_inc(sem("cb"), 1)

            def mix_heads(g, b):
                dve.wait_ge(sem("decayed"), 2 * g + b + 1)
                dve.tensor_tensor(mix[:, b], mix[:, b], cb[:, bass.ds(g, 1), :].broadcast_to([P, 4, 384]),
                                  ALU.mult).then_inc(sem("mixed"), 1)

            def y_gate(g):
                dve.wait_ge(sem("y"), g + 1)
                own.inc(dve.tensor_tensor(x_skip[:], x_skip[:], aux[1][:], ALU.add))
                dve.wait_ge(sem("z_silu"), g + 1)
                dve.sem_inc(group_read, 1)
                own.settle()
                dve.tensor_tensor(zg[:], zg[:], x_skip[:], ALU.mult).then_inc(sem("gated"), 1)

            def y_scale(g):
                dve.wait_ge(sem("y_root"), g + 1)
                own.inc(dve.reciprocal(y_rms[:], y_rms[:]))
                own.settle()
                for b in range(TB):
                    ins = dve.tensor_scalar(zg[:, b * GC:(b + 1) * GC], zg[:, b * GC:(b + 1) * GC],
                                            y_rms[:, b:b + 1], None, ALU.mult)
                ins.then_inc(sem("y_scaled"), 1)

            def y_lo(g, half):
                dve.wait_ge(sem("y_hi"), g + 1)
                for n in range(TG):
                    k = bass.ds(4 * g - KT * half + n, 1)
                    ins = dve.scalar_tensor_tensor(xa[:, k, 1, :], aux[0][:, n * T:(n + 1) * T],
                                                   misc[:, bass.ds(OUT_COL + 4 * g + n, 1)],
                                                   xa[:, k, 0, :].bitcast(F32), ALU.mult, ALU.subtract)
                ins.then_inc(sem("y_lo"), 1)

            def spread_x(g):
                dve.wait_ge(sem("x_tok"), g + 1)
                for b in range(TB):
                    src = aux[0][:, b * GC:(b + 1) * GC].rearrange("p (h d) -> p h d", h=8)
                    for dst, w in ((x_skip, head_p[:, 2, bass.ds(8 * g, 8)]), (xc, dt[:, b, bass.ds(8 * g, 8)])):
                        ins = dve.tensor_tensor(dst[:, b * GC:(b + 1) * GC].rearrange("p (h d) -> p h d", h=8), src,
                                                w.unsqueeze(2).broadcast_to([P, 8, SHD]), ALU.mult)
                ins.then_inc(sem("x_dt"), 1)

            def ssm_pair(half, g, i, first):
                sx = st[f"xz{half}"]
                s, r = sx.slot, 2 * i
                if first and half == 0:
                    conv_taps(s, r, 44)
                    cuts(s, r, range(4, 5))
                else:
                    cuts(s, r, range(0, 2))
                    if not first:
                        y_gate(g - 1)
                    cuts(s, r, range(2, 3))
                    if not first:
                        y_scale(g - 1)
                    cuts(s, r, range(3, 5))
                if not first:
                    y_lo(g - 1, half)
                if first and half == 0:
                    for j in range(4):
                        keep_cb(2 * j)
                        keep_cb(2 * j + 1)
                        if j < 3:
                            cuts(s, r, range(5 + j, 6 + j))
                else:
                    cuts(s, r, range(5, 8))
                conv_open(4 + g, sx, s + 8, r, sx.group % 2)
                conv_taps(s + 8, r, 4 * g)
                cuts(s + 8, r, range(4, 5))
                mix_heads(g, 0)
                cuts(s + 8, r, range(5, 7))
                mix_heads(g, 1)
                cuts(s + 8, r, range(7, 8))
                spread_x(g)

            def ssm():
                own.inc(dve.memset(xr[:, :, 0:KC - 1], 0.0))
                s = st["bc0"]
                cuts(s.slot, js=range(2, 6))
                norm_recip("ssm", tok=True)
                cuts(s.slot, js=range(6, 8))
                conv_open_wide(s)
                conv_tap(0, 32)
                dt_keep()
                cuts(st["dt"].slot, js=range(1))
                s = st["bc"]
                conv_tap(1, 32)
                dt_open()
                conv_tap(2, 32)
                cuts(s.slot, js=range(0, 1))
                conv_tap(3, 32)
                dt_steps()
                cuts(s.slot, js=range(1, 5))
                dt_offsets()
                cuts(s.slot, js=range(5, 8))
                for q in range(3):
                    conv_open(q + 1, s, s.slot + 8 * q + 8, 0, (s.group + q) % 2)
                    if q < 2:
                        conv_taps(s.slot + 8 * q + 8, 0, 36 + 4 * q)
                        cuts(s.slot + 8 * q + 8, js=range(4, 8))
                for half in range(2):
                    ssm_pair(half, 4 * half, 0, True)
                    with own.loop(1, 4, 6) as i:
                        ssm_pair(half, 4 * half + i, i, False)
                    s = st[f"out{half}"]
                    for c in range(4):
                        cuts(s.slot + 8 * c, js=range(0, 2))
                        if c == 0:
                            y_gate(4 * half + 3)
                        cuts(s.slot + 8 * c, js=range(2, 3))
                        if c == 0:
                            y_scale(4 * half + 3)
                        cuts(s.slot + 8 * c, js=range(3, 5))
                        if c == 0:
                            y_lo(4 * half + 3, half)
                        if half == 1 and c == 2:
                            p_lo(1)
                        cuts(s.slot + 8 * c, js=range(5, 8))
                        project(s, c, *(("mlp1", xb) if half else ()))
                cuts(st["ple1"].slot, js=range(4))

            mlp(0, xa)
            gate(0, xb if layers > 1 else None, "ssm" if layers > 1 else "final")
            if layers > 1:
                ssm()
                mlp(1, xb)
                gate(1, None, "final")

        @block.tensor
        def _(pe):
            def open_group(group, par=None):
                if not isinstance(group, int) or group >= 2:
                    pe.wait_ge(group_read, group - 1)
                return None if par is None else gp[par]

            def products(pst, slot, r, xs, k0, first, last):
                pe.wait_ge(lo_made, slot + 1 + RAW * r)
                hi, lo = w_hi[slot % CUT], w_lo[slot % CUT]
                for n in range(TG):
                    for k in range(2):
                        cols = slice(n * P, (n + 1) * P)
                        for i, (w, part) in enumerate(((hi, 0), (hi, 1), (lo, 0))):
                            mm = pe.matmul(pst[:, n * T:(n + 1) * T], w[:, k, cols], xs[:, k0 + k, part, :],
                                           start=first and k == 0 and i == 0 and n % 2 == 0,
                                           stop=last and k == 1 and i == 2, skip_group_check=True)
                            if n == TG - 1 and k == 1 and i == 2:
                                mm.then_inc(slot_used, 1)

            def products_tok(pst, slot, r, xs, k0, first, last):
                pe.wait_ge(lo_made, slot + 1 + RAW * r)
                hi, lo = w_hi[slot % CUT], w_lo[slot % CUT]
                for b in range(TB):
                    for k in range(2):
                        for i, (w, part) in enumerate(((hi, 0), (hi, 1), (lo, 0))):
                            mm = pe.matmul(pst[:, b * GC:(b + 1) * GC], xs[:, k0 + k, part, b * P:(b + 1) * P],
                                           w[:, k, :], start=first and k == 0 and i == 0,
                                           stop=last and k == 1 and i == 2)
                            if b == TB - 1 and k == 1 and i == 2:
                                mm.then_inc(slot_used, 1)

            def products_wide(pst, slot, r, xs, k0, first, last, before=None):
                pe.wait_ge(lo_made, slot + 1 + RAW * r)
                hi, lo = w_hi[slot % CUT], w_lo[slot % CUT]
                for n in range(TG):
                    if before and n == TG - 1:
                        pe.wait_ge(before, 1)
                    for k in range(2):
                        cols = slice(n * P, (n + 1) * P)
                        pe.matmul(pst[:, n * GC:(n + 1) * GC], hi[:, k, cols],
                                  xs[:, k0 + k, :, :], start=first and k == 0, stop=False, skip_group_check=True)
                        mm = pe.matmul(pst[:, n * GC:n * GC + T], lo[:, k, cols], xs[:, k0 + k, 0, :],
                                       start=False, stop=last and k == 1, skip_group_check=True)
                mm.then_inc(slot_used, 1)

            def half_slots(pst, slot, r, xs, js, x_ready=None, x_from=0, fn=products):
                for j in js:
                    if x_ready is not None and j % 2 == 0:
                        pe.wait_ge(x_ready, x_from + j // 2 + 1)
                    fn(pst, slot + j, r, xs, 2 * j, j == 0, j == HS_PER_GROUP - 1)

            def mean(name, tok=False):
                pe.wait_ge(sem(f"{name}_sum"), 1)
                mm = pe.matmul(mean_at(name)[:, 0:T], ones[:], acc4[:, 0, :], start=True, stop=True)
                if tok:
                    for b in range(TB):
                        mm = pe.matmul(mean_at(name)[:, GC + b:GC + b + 1], acc4[:, 0, b * P:(b + 1) * P], ones[:, 0:1],
                                       start=True, stop=True)
                mm.then_inc(sem(f"{name}_mean"), 1)

            pe.wait_ge(sem("masks"), 5)
            pe.wait_ge(sem("gain_in"), 16)
            pe.transpose(aux[1][:, 0:KT], rows4[0:KT, :], ident[0:KT, 0:KT]).then_inc(sem("gain_turned"), 1)

            def turn_rows():
                pe.wait_ge(sem("rows_in"), 16 * 10)
                pe.wait_ge(sem("attn_h"), 4)
                for i, (src, n) in enumerate(((rows0, N_GAIN - KT), (rows1, P), (rows2, N_CONV - P),
                                              (rows3, N_CB + 2 + INNER // P))):
                    tr = pe.transpose(aux[1][:, 128 * i:128 * i + n], src[0:n, :], ident[0:n, 0:n])
                tr.then_inc(sem("rows_turned"), 1)

            def turn_x_in(c):
                pe.wait_ge(sem(f"x_in{c}"), 16)
                if c == 2:
                    pe.wait_ge(sem("gain_kept"), 1)
                if c == 3:
                    pe.wait_ge(sem("attn_h"), 1)
                for n in range(TG):
                    for b in range(TB):
                        tr = pe.transpose((gp[1], aux[0], aux[1])[c % 3][:, n * T + b * P:n * T + (b + 1) * P],
                                          x_tok[:, b, (4 * c + n) * P:(4 * c + n + 1) * P], ident[:])
                tr.then_inc(sem("x_turned"), 1)

            q = st["qk"]

            def head_means(m, pair=0):
                pe.wait_ge(sem("qk_squares"), m + 1)
                for b in range(2):
                    mm = pe.matmul(aux[pair][:, b * GC:(b + 1) * GC], ones[:],
                                   sq[:, 2 * b:2 * b + 2, :], start=True, stop=True)
                mm.then_inc(sem("qk_mean"), 1)

            for c in range(4):
                turn_x_in(c)
            ps = open_group(0, 0)
            for c in range(4):
                if c == 2:
                    turn_rows()
                if c == 3:
                    pe.wait_ge(sem("params"), 1)
                    mean("attn", tok=True)
                half_slots(ps, q.slot, 0, xa, range(2 * c, 2 * c + 2), sem("attn_lo"))
            pe.wait_ge(sem("attn_h"), 4)
            ps = open_group(1, 1)
            half_slots(ps, q.slot + 8, 0, xa, range(0, 2))
            head_means(0)
            half_slots(ps, q.slot + 8, 0, xa, range(2, 8))
            with pe.Fori(1, 4) as c:
                for m in range(2):
                    ps = open_group(q.group + 2 * c + m, m)
                    half_slots(ps, q.slot + 8 * m, 2 * c, xa, range(0, 2))
                    head_means(2 * c + m - 1)
                    half_slots(ps, q.slot + 8 * m, 2 * c, xa, range(2, 8))

            def scores(hd):
                b = hd % 2
                z = aux[0][:, b * GC:b * GC + 384]
                pe.matmul(z[:, 0:T], qk[:, hd, 1, 0:P], qk[:, hd, 0, :], start=True, stop=True)
                return pe.matmul(z[:, T:T + P], qk[:, hd, 1, P:T], qk[:, hd, 0, P:T], start=True, stop=True)

            def score_pair(hp):
                pe.wait_ge(group_read, 8 if hp >= 6 else 7)
                if hp:
                    pe.wait_ge(sem("soft"), hp)
                scores(2 * hp)
                scores(2 * hp + 1).then_inc(sem("z"), 1)

            def suffix_pair(hp):
                pe.wait_ge(sem("soft"), hp + 1)
                if hp:
                    pe.wait_ge(sem("log_weights"), hp)
                for b in range(2):
                    u = aux[1][:, b * GC:b * GC + 384]
                    pe.matmul(u, later[:], soft[:, b, :], start=True, stop=False, skip_group_check=True)
                    mm = pe.matmul(u[:, P:T], ones[:], soft[:, b, T:T + P], start=False, stop=True,
                                   skip_group_check=True)
                mm.then_inc(sem("suffix"), 1)

            v = st["v"]
            for g in range(4):
                ps = open_group(v.group + g, (v.group + g) % 2)
                for i in range(2):
                    score_pair(2 * g + i)
                    half_slots(ps, v.slot + 8 * g, 0, xa, range(4 * i, 4 * i + 2), fn=products_tok)
                    if g == i == 0:
                        head_means(7, pair=1)
                    half_slots(ps, v.slot + 8 * g, 0, xa, range(4 * i + 2, 4 * i + 3), fn=products_tok)
                    if g == i == 0:
                        pe.wait_ge(sem("qk_rooted"), 8)
                    suffix_pair(2 * g + i)
                    half_slots(ps, v.slot + 8 * g, 0, xa, range(4 * i + 3, 4 * i + 4), fn=products_tok)

            def weigh_values(q):
                pe.wait_ge(group_read, v.group + q + 1)
                if q < 2:
                    pe.wait_ge(sem("log_weights" if q else "soft"), HEADS // 2)
                else:
                    pe.wait_ge(sem("o_lo"), q - 1)
                for n in range(4):
                    hd = 4 * q + n
                    pe.wait_ge(sem("weights_masked"), hd // 2 + 1)
                    o = aux[q % 2][:, n * T:(n + 1) * T]
                    a = qk[:, hd].rearrange("p a b -> p (a b)")
                    pe.matmul(o, v_tok[:, hd, 0, :], a[:, 0:T], start=n % 2 == 0, stop=False,
                              skip_group_check=True)
                    mm = pe.matmul(o[:, P:T], v_tok[:, hd, 1, :], a[:, T:T + P], start=False, stop=True,
                                   skip_group_check=True)
                mm.then_inc(sem("o"), 1)

            def turn_p(l):
                pe.wait_ge(sem(f"p_in{l}"), 16)
                pe.wait_ge(group_read, st[f"ple{l}"].group - 2)
                for k in range(2):
                    for b in range(TB):
                        tr = pe.transpose(aux[0][:, k * T + b * P:k * T + (b + 1) * P],
                                          p_tok[:, b, k * P:(k + 1) * P], ident[:])
                tr.then_inc(sem(f"p_turned{l}"), 1)

            def embed(l):
                s = st[f"ple{l}"]
                pe.wait_ge(sem(f"p_lo{l}"), 1)
                for j in range(4):
                    pe.wait_ge(group_read, s.group + (j - 1 if j >= 2 else -1))
                    products(gp[(s.group + j) % 2], s.slot + j, 0, p_t, 0, True, True)

            s = st["wo"]
            weigh_values(0)
            weigh_values(1)
            for c in range(4):
                ps = open_group(s.group + c, s.group % 2)
                if c == 0:
                    for i in range(4):
                        half_slots(ps, s.slot, 0, xb, range(2 * i, 2 * i + 2), sem("o_lo"))
                        if i < 2:
                            weigh_values(i + 2)
                else:
                    if c == 3:
                        pe.wait_ge(sem("p_lo0"), 1)
                    half_slots(wide[c % 2], s.slot + 8 * c, 0, xb, range(0, 4), fn=products_wide)
                    if c == 2:
                        turn_p(0)
                    half_slots(wide[c % 2], s.slot + 8 * c, 0, xb, range(4, 8), fn=products_wide)
            embed(0)

            def pair_loop(s, slot, group, xs, x_ready, x_step, n=2, r0=0, start=0, wait_from=0):
                with pe.Fori(start, n) as c2:
                    for b in range(2):
                        open_group(group + 2 * c2 + b + r0)
                        for j in range(HS_PER_GROUP):
                            if x_ready is not None and j % 2 == 0:
                                pe.wait_ge(x_ready, wait_from + x_step * (j // 2 + 1))
                            products_wide(wide[1 - b], slot + 8 * b + j, 2 * c2 + r0, xs, 2 * j, j == 0, j == 7)

            def mlp(l, xs, us):
                s = st[f"mlp{l}"]
                ready = sem(f"mlp{l}_lo")
                half_slots(wide[1], s.slot, 0, xs, range(0, 6), ready, fn=products_wide)
                pe.wait_ge(group_read, s.group)
                mean(f"mlp{l}")
                half_slots(wide[1], s.slot, 0, xs, range(6, 8), ready, fn=products_wide)
                pe.wait_ge(sem(f"mlp{l}_root"), 1)
                half_slots(wide[0], s.slot + 8, 0, xs, range(8), fn=products_wide)
                open_group(s.group + 2)
                pe.wait_ge(sem(f"e{l}_sum"), 1)
                pe.matmul(wide[1][:, 3 * GC:3 * GC + T], ones[:], acc_e[:, 0, :], start=True,
                          stop=True).then_inc(sem(f"e{l}_mean"), 1)
                products_wide(wide[1], s.slot + 16, 0, xs, 0, True, False, before=sem(f"e{l}_root"))
                half_slots(wide[1], s.slot + 16, 0, xs, range(1, 8), fn=products_wide)
                open_group(s.group + 3)
                half_slots(wide[0], s.slot + 24, 0, xs, range(8), fn=products_wide)
                pair_loop(s, s.slot + 32, s.group + 4, us, sem(f"u_lo{l}"), 1)
                with pe.Fori(1, 4) as f:
                    pair_loop(s, s.slot, s.group, xs, None, 0, r0=8 * f)
                    pair_loop(s, s.slot + 32, s.group + 4, us, sem(f"u_lo{l}"), 1, r0=8 * f, wait_from=4 * f)

            def turn_out(c, ns=range(TG)):
                pe.wait_ge(sem("final_h"), c + 1 + (ns[0] > 0))
                if c >= 2:
                    pe.wait_ge(sem("out_staged"), c - 1)
                for b in range(TB):
                    for n in ns:
                        tr = pe.transpose(aux[c % 2][:, b * GC + n * P:b * GC + (n + 1) * P],
                                          h[:, 4 * c + n, b * P:(b + 1) * P], ident[:])
                if ns[-1] == TG - 1:
                    tr.then_inc(sem("final_turned"), 1)

            def gate(l, xs):
                s = st[f"gate{l}"]
                final = l == layers - 1
                for c in range(4):
                    open_group(s.group + c)
                    if c == 1:
                        pe.wait_ge(sem(f"gate{l}_root"), 1)
                    ps = wide[1 - c % 2]
                    half_slots(ps, s.slot + 8 * c, 0, xs, range(0, 6), sem(f"gate{l}_lo"), fn=products_wide)
                    if c == 0:
                        pe.wait_ge(group_read, s.group)
                        mean(f"gate{l}")
                    if c == 3 and final:
                        turn_out(0)
                        turn_out(1)
                    half_slots(ps, s.slot + 8 * c, 0, xs, range(6, 7), sem(f"gate{l}_lo"), fn=products_wide)
                    if c == 3 and final:
                        turn_out(2)
                    half_slots(ps, s.slot + 8 * c, 0, xs, range(7, 8), sem(f"gate{l}_lo"), fn=products_wide)
                if final:
                    turn_out(3, range(0, 2))
                    turn_out(3, range(2, 4))

            def cumulate():
                pe.wait_ge(sem("dt_a"), 1)
                for b in range(TB):
                    pe.matmul(aux[1][0:SH, b * P:(b + 1) * P], dt_a[:, b, :], upto[:], start=True, stop=True)
                for b in range(TB):
                    pe.matmul(aux[1][:, GC + b * SH:GC + (b + 1) * SH], upto[:], dt_a[:, b, :], start=True,
                              stop=True)
                pe.matmul(aux[1][:, GC + 2 * SH:GC + 3 * SH], later[:], dt_a[:, 0, :], start=True,
                          stop=True).then_inc(sem("cumulated"), 1)

            def cb_products(g):
                pe.wait_ge(sem("conv_silu"), 4)
                if g >= 2:
                    pe.wait_ge(sem("cb"), g - 1)
                o = aux[0][:, (g % 2) * GC:(g % 2) * GC + 384]
                pe.matmul(o[:, 0:T], bt[:, g, 0:P], ct[:, g, :], start=True, stop=True)
                pe.matmul(o[:, T:T + P], bt[:, g, P:T], ct[:, g, P:T], start=True,
                          stop=True).then_inc(sem("cb_raw"), 1)

            def turn_y(g):
                pe.wait_ge(sem("y_scaled"), g + 1)
                for n in range(TG):
                    for b in range(TB):
                        tr = pe.transpose(aux[0][:, n * T + b * P:n * T + (b + 1) * P],
                                          zg[:, b * GC + n * P:b * GC + (n + 1) * P], ident[:])
                tr.then_inc(sem("y_turned"), 1)

            def turn_x(g):
                pe.wait_ge(sem("conv_silu"), g + 5)
                if not isinstance(g, int) or g:
                    pe.wait_ge(sem("y_lo"), g)
                else:
                    pe.wait_ge(sem("cb"), SG)
                for n in range(TG):
                    for b in range(TB):
                        tr = pe.transpose(aux[0][:, b * GC + n * P:b * GC + (n + 1) * P],
                                          xc[:, n * T + b * P:n * T + (b + 1) * P], ident[:])
                tr.then_inc(sem("x_tok"), 1)

            def y_products(g):
                pe.wait_ge(sem("mixed"), 2 * g + 2)
                pe.wait_ge(sem("x_dt"), g + 1)
                for hd in range(8):
                    m = mix[:, hd // 4, hd % 4, :]
                    c = slice(hd * SHD, (hd + 1) * SHD)
                    x0, x1 = xc[:, 0:GC][:, c], xc[:, GC:2 * GC][:, c]
                    y0, y1 = aux[1][:, 0:GC][:, c], aux[1][:, GC:2 * GC][:, c]
                    pe.matmul(y0, m[:, 0:P], x0, start=True, stop=True)
                    pe.matmul(y1, m[:, P:T], x0, start=True, stop=False)
                    mm = pe.matmul(y1, m[:, T:T + P], x1, start=False, stop=True)
                mm.then_inc(sem("y"), 1)
                pe.wait_ge(sem("y"), g + 1)
                pe.sem_inc(sem("mix_free"), 1)

            def ssm_pair(half, g, i, first):
                sx = st[f"xz{half}"]
                s, r = sx.slot, 2 * i
                ps = open_group(sx.group + 2 * i, sx.group % 2)
                half_slots(ps, s, r, xb, range(0, 2))
                if not first:
                    y_products(g - 1)
                half_slots(ps, s, r, xb, range(2, 5))
                if first:
                    if half == 0:
                        for j in range(3):
                            cb_products(2 * j)
                            cb_products(2 * j + 1)
                            half_slots(ps, s, r, xb, range(5 + j, 6 + j))
                        cb_products(6)
                        cb_products(7)
                    else:
                        half_slots(ps, s, r, xb, range(5, 8))
                else:
                    turn_y(g - 1)
                    half_slots(ps, s, r, xb, range(5, 8))
                ps = open_group(sx.group + 2 * i + 1, (sx.group + 1) % 2)
                half_slots(ps, s + 8, r, xb, range(0, 6), fn=products_tok)
                turn_x(g)
                half_slots(ps, s + 8, r, xb, range(6, 8), fn=products_tok)

            def ssm():
                pe.sem_inc(sem("mix_free"), 1)
                s = st["bc0"]
                open_group(s.group)
                half_slots(wide[1], s.slot, 0, xb, range(0, 6), sem("ssm_lo"), fn=products_wide)
                pe.wait_ge(group_read, s.group)
                mean("ssm", tok=True)
                half_slots(wide[1], s.slot, 0, xb, range(6, 8), sem("ssm_lo"), fn=products_wide)
                pe.wait_ge(sem("ssm_root"), 1)
                s = st["dt"]
                pe.wait_ge(lo_made, s.slot + 1)
                ps = open_group(s.group, s.group % 2)
                hi, lo = (w[s.slot % CUT][:].rearrange("p a b -> p (a b)").rearrange("p (k n) -> p k n", k=KT)
                          for w in (w_hi, w_lo))
                for k in range(KT):
                    for i, (w, part) in enumerate(((hi, 0), (hi, 1), (lo, 0))):
                        mm = pe.matmul(ps[0:SH, 0:T], w[:, k, :], xb[:, k, part, :],
                                       start=k == 0 and i == 0, stop=k == KT - 1 and i == 2)
                mm.then_inc(slot_used, 1)
                s = st["bc"]
                for q in range(3):
                    ps = open_group(s.group + q, (s.group + q) % 2)
                    half_slots(ps, s.slot + 8 * q, 0, xb, range(0, 1))
                    if q == 0:
                        pe.wait_ge(sem("dt_kept"), 1)
                        for b in range(TB):
                            tr = pe.transpose(aux[0][:, b * GC:b * GC + SH], decay_t[:, b * P:(b + 1) * P],
                                              ident[0:SH, 0:SH])
                        tr.then_inc(sem("dt_turned"), 1)
                    half_slots(ps, s.slot + 8 * q, 0, xb, range(1, 5))
                    if q == 0:
                        cumulate()
                    half_slots(ps, s.slot + 8 * q, 0, xb, range(5, 8))
                for half in range(2):
                    ssm_pair(half, 4 * half, 0, True)
                    with pe.Fori(1, 4) as i:
                        ssm_pair(half, 4 * half + i, i, False)
                    s = st[f"out{half}"]
                    for c in range(4):
                        ps = open_group(s.group + c, s.group % 2)
                        fn = products
                        if c:
                            ps, fn = wide[c % 2], products_wide
                        if half == 1 and c == 3:
                            pe.wait_ge(sem("p_lo1"), 1)
                        half_slots(ps, s.slot + 8 * c, 0, xa, range(0, 2), sem("y_lo"), 4 * half, fn=fn)
                        if c == 0:
                            y_products(4 * half + 3)
                        half_slots(ps, s.slot + 8 * c, 0, xa, range(2, 5), sem("y_lo"), 4 * half, fn=fn)
                        if half == 1 and c == 2:
                            turn_p(1)
                        if c == 0:
                            turn_y(4 * half + 3)
                        half_slots(ps, s.slot + 8 * c, 0, xa, range(5, 8), sem("y_lo"), 4 * half, fn=fn)
                embed(1)

            mlp(0, xa, xb)
            gate(0, xa)
            if layers > 1:
                ssm()
                mlp(1, xb, xa)
                gate(1, xb)


_INS = ['x', 'p', 'attn_norm', 'attn_w_qkv', 'attn_q_norm', 'attn_k_norm', 'attn_w_o', 'ssm_norm',
        'ssm_w_in', 'ssm_conv_w', 'ssm_conv_b', 'ssm_dt_bias', 'ssm_a_log', 'ssm_d', 'ssm_out_norm',
        'ssm_w_out', 'mlp_norm', 'mlp_w_up', 'mlp_w_down', 'ple_w_proj', 'ple_norm', 'ple_gate_norm',
        'ple_w_gate']


def kernel(**inputs):
    import numpy as _np
    import concourse.bacc as _bacc
    from concourse import mybir as _mybir
    from concourse.bass_utils import run_bass_kernel_spmd as _run

    nc = _bacc.Bacc("TRN2", target_bir_lowering=False, num_devices=1)
    arrays, args = {}, {}
    for name in _INS:
        a = _np.ascontiguousarray(inputs[name])
        arrays[f"in_{name}"] = a
        args[name] = nc.dram_tensor(f"in_{name}", a.shape, _mybir.dt.from_np(a.dtype), kind="ExternalInput").ap()
    args["out"] = nc.dram_tensor("out_h", (1, T, D), F32, kind="ExternalOutput").ap()
    args["decay_rows"] = nc.dram_tensor("decay_rows", (SH, T), F32).ap()
    build_trunk(nc, 2, **args)
    r = _run(nc, [arrays], core_ids=[0])
    return r.results[0]["out_h"]
```
